# Optimizing a Trainium2 kernel written in Bass

```python
import jax, jax.numpy as jnp
from jax import lax
import numpy as np

D_MODEL = 1024
BATCH = 1
SEQ = 1024
DEPTH = 2

CTX_LEN = 256
GRID_W = 64

WIN_HEADS = 8
WIN_KV_HEADS = 2
WIN_GROUP = WIN_HEADS // WIN_KV_HEADS
WIN_HEAD_DIM = 64
WINDOW = 128
BAND_BLOCK = 128
MLA_HEADS = 8
MLA_Q_RANK = 384
MLA_KV_RANK = 256
MLA_NOPE_DIM = 64
MLA_ROPE_DIM = 32
MLA_V_DIM = 64
QUERY_BLOCK = 128
N_EXPERTS = 16
CAPACITY_FACTOR = 2
EXPERT_FF = 1024

ROPE_THETA = 10000.0
LN_EPS = 1e-5
RMS_EPS = 1e-6
NEG_INF = -1e30
ALPHA = (2 * DEPTH) ** 0.25
BETA = (8 * DEPTH) ** -0.25
N_BRANCH = 2
WIN_Q_W = WIN_HEADS * WIN_HEAD_DIM
WIN_KV_W = WIN_KV_HEADS * WIN_HEAD_DIM
MLA_OUT_W = MLA_HEADS * MLA_V_DIM
WIN_SCALE = WIN_HEAD_DIM ** -0.5
MLA_SCALE = (MLA_NOPE_DIM + MLA_ROPE_DIM) ** -0.5
KEY_SIZES = [WIN_KV_W, WIN_KV_W, MLA_KV_RANK, MLA_ROPE_DIM]
QUERY_SIZES = [WIN_Q_W, MLA_Q_RANK, N_BRANCH * D_MODEL]
KEY_COLS = sum(KEY_SIZES)
IN_COLS = KEY_COLS + sum(QUERY_SIZES)

kernel_name = "hybrid_dit_gqa_mla_ecmoe"

def split_cols(t, sizes):
    return jnp.split(t, np.cumsum(sizes)[:-1].tolist(), axis=-1)

def layer_norm(x, g, b):
    xf = x.astype(jnp.float32)
    mu = jnp.mean(xf, axis=-1, keepdims=True)
    var = jnp.mean(jnp.square(xf - mu), axis=-1, keepdims=True)
    return ((xf - mu) * lax.rsqrt(var + LN_EPS) * g.astype(jnp.float32) + b.astype(jnp.float32)).astype(x.dtype)

def rms_norm(x, g):
    xf = x.astype(jnp.float32)
    return (xf * lax.rsqrt(jnp.mean(jnp.square(xf), axis=-1, keepdims=True) + RMS_EPS) * g.astype(jnp.float32)).astype(x.dtype)

def adaln(cond, w, b):
    mod = jax.nn.silu(cond) @ w + b
    return jnp.split(mod[:, None, :], 6, axis=-1)

def modulate(x, shift, scale):
    return x * (1 + scale) + shift

def axial_angles(n, rot_dim):
    rows = n // GRID_W
    row = jnp.repeat(jnp.arange(rows, dtype=jnp.float32), GRID_W)
    col = jnp.tile(jnp.arange(GRID_W, dtype=jnp.float32), rows)
    n_freq = rot_dim // 4
    inv_freq = ROPE_THETA ** (-jnp.arange(n_freq, dtype=jnp.float32) / n_freq)
    ang = jnp.stack([row[:, None] * inv_freq, col[:, None] * inv_freq], axis=1)
    return jnp.cos(ang), jnp.sin(ang)

def apply_axial_rope(x, cos, sin):
    shp = x.shape
    xr = x.reshape(shp[:-1] + (2, 2, shp[-1] // 4))
    x1, x2 = xr[..., 0, :], xr[..., 1, :]
    bshape = (1, shp[1]) + (1,) * (x.ndim - 3) + cos.shape[1:]
    c = cos.reshape(bshape).astype(x.dtype)
    s = sin.reshape(bshape).astype(x.dtype)
    return jnp.stack([x1 * c - x2 * s, x1 * s + x2 * c], axis=-2).reshape(shp)

def sink_softmax(scores, sink):
    s = scores.astype(jnp.float32)
    sk = jnp.broadcast_to(sink.astype(jnp.float32), s.shape[:-1] + (1,))
    return jax.nn.softmax(jnp.concatenate([s, sk], axis=-1), axis=-1)[..., :-1]

def band_view(t, nb):
    B = t.shape[0]
    tp = jnp.pad(t, ((0, 0), (BAND_BLOCK, BAND_BLOCK), (0, 0), (0, 0)))
    tb = tp.reshape((B, nb + 2, BAND_BLOCK) + t.shape[2:])
    return jnp.concatenate([tb[:, :-2], tb[:, 1:-1], tb[:, 2:]], axis=2)

def window_attention_latent(q, k, v, k_c, v_c, sink):
    B, n = q.shape[:2]
    nb = n // BAND_BLOCK
    qb = q.reshape(B, nb, BAND_BLOCK, WIN_KV_HEADS, WIN_GROUP, WIN_HEAD_DIM)
    kw, vw = band_view(k, nb), band_view(v, nb)
    blk = jnp.arange(nb)
    key_pos = blk[:, None] * BAND_BLOCK - BAND_BLOCK + jnp.arange(3 * BAND_BLOCK)[None, :]
    q_pos = blk[:, None] * BAND_BLOCK + jnp.arange(BAND_BLOCK)[None, :]
    kp = key_pos[:, None, :]
    allowed = (jnp.abs(kp - q_pos[:, :, None]) <= WINDOW) & (kp >= 0) & (kp < n)
    s_loc = jnp.einsum('bnqkgd,bnskd->bnkgqs', qb, kw).astype(jnp.float32) * WIN_SCALE
    s_loc = jnp.where(allowed[None, :, None, None], s_loc, NEG_INF)
    s_ctx = jnp.einsum('bnqkgd,bckd->bnkgqc', qb, k_c).astype(jnp.float32) * WIN_SCALE
    p = sink_softmax(jnp.concatenate([s_loc, s_ctx], axis=-1), sink).astype(v.dtype)
    o = (jnp.einsum('bnkgqs,bnskd->bnqkgd', p[..., :3 * BAND_BLOCK], vw)
         + jnp.einsum('bnkgqc,bckd->bnqkgd', p[..., 3 * BAND_BLOCK:], v_c))
    return o.reshape(B, n, WIN_Q_W)

def window_attention_ctx(q_c, k_c, v_c, sink):
    B, Lc = q_c.shape[:2]
    s = jnp.einsum('bqkgd,bskd->bkgqs', q_c, k_c) * WIN_SCALE
    p = sink_softmax(s, sink).astype(v_c.dtype)
    return jnp.einsum('bkgqs,bskd->bqkgd', p, v_c).reshape(B, Lc, WIN_Q_W)

def mla_expand_q(cq, g_qn, w_uq):
    B, n = cq.shape[:2]
    q = (rms_norm(cq, g_qn) @ w_uq).reshape(B, n, MLA_HEADS, MLA_NOPE_DIM + MLA_ROPE_DIM)
    return q[..., :MLA_NOPE_DIM], q[..., MLA_NOPE_DIM:]

def mla_expand_kv(ckv, g_kvn, w_ukv):
    B, n = ckv.shape[:2]
    kv = (rms_norm(ckv, g_kvn) @ w_ukv).reshape(B, n, MLA_HEADS, MLA_NOPE_DIM + MLA_V_DIM)
    return kv[..., :MLA_NOPE_DIM], kv[..., MLA_NOPE_DIM:]

def mla_dense(qn, qr, kn, kr, v):
    s = jnp.einsum('bqhd,bkhd->bhqk', qn, kn) + jnp.einsum('bqhd,bkd->bhqk', qr, kr)
    p = jax.nn.softmax(s.astype(jnp.float32) * MLA_SCALE, axis=-1).astype(v.dtype)
    return jnp.einsum('bhqk,bkhd->bqhd', p, v)

def token_mixer(h_c, h_l, w_in, sink, g_qn, g_kvn, w_uq, w_ukv, w_oa, w_ob, w_out, rope_win, rope_mla, need_ctx):
    B, n, _ = h_l.shape
    Lc = h_c.shape[1]
    sink_g = sink.reshape(WIN_KV_HEADS, WIN_GROUP, 1, 1)
    p_l = h_l @ w_in
    ka_l, va_l, ckv_l, kr_l = split_cols(p_l[..., :KEY_COLS], KEY_SIZES)
    qa_l, cq_l, gt_l = split_cols(p_l[..., KEY_COLS:], QUERY_SIZES)
    p_c = h_c @ (w_in if need_ctx else w_in[:, :KEY_COLS])
    ka_c, va_c, ckv_c, kr_c = split_cols(p_c[..., :KEY_COLS], KEY_SIZES)

    ka_l = apply_axial_rope(ka_l.reshape(B, n, WIN_KV_HEADS, WIN_HEAD_DIM), *rope_win)
    va_l = va_l.reshape(B, n, WIN_KV_HEADS, WIN_HEAD_DIM)
    ka_c = ka_c.reshape(B, Lc, WIN_KV_HEADS, WIN_HEAD_DIM)
    va_c = va_c.reshape(B, Lc, WIN_KV_HEADS, WIN_HEAD_DIM)
    qa_l = apply_axial_rope(qa_l.reshape(B, n, WIN_HEADS, WIN_HEAD_DIM), *rope_win)
    qa_l = qa_l.reshape(B, n, WIN_KV_HEADS, WIN_GROUP, WIN_HEAD_DIM)
    oa_l = window_attention_latent(qa_l, ka_l, va_l, ka_c, va_c, sink_g)

    kn_l, v_l = mla_expand_kv(ckv_l, g_kvn, w_ukv)
    kn_c, v_c = mla_expand_kv(ckv_c, g_kvn, w_ukv)
    kr_l = apply_axial_rope(kr_l[:, :, None], *rope_mla)[:, :, 0]
    qn_l, qr_l = mla_expand_q(cq_l, g_qn, w_uq)
    qr_l = apply_axial_rope(qr_l, *rope_mla)
    kn_all = jnp.concatenate([kn_c, kn_l], axis=1)
    kr_all = jnp.concatenate([kr_c, kr_l], axis=1)
    v_all = jnp.concatenate([v_c, v_l], axis=1)
    nq = n // QUERY_BLOCK
    qn_b = jnp.moveaxis(qn_l.reshape(B, nq, QUERY_BLOCK, MLA_HEADS, MLA_NOPE_DIM), 1, 0)
    qr_b = jnp.moveaxis(qr_l.reshape(B, nq, QUERY_BLOCK, MLA_HEADS, MLA_ROPE_DIM), 1, 0)
    ob = lax.map(lambda blk: mla_dense(blk[0], blk[1], kn_all, kr_all, v_all), (qn_b, qr_b))
    ob_l = jnp.moveaxis(ob, 0, 1).reshape(B, n, MLA_OUT_W)

    def merge(o_a, o_b, gates):
        g_a, g_b = jnp.split(gates, N_BRANCH, axis=-1)
        return (jax.nn.sigmoid(g_a) * (o_a @ w_oa) + jax.nn.sigmoid(g_b) * (o_b @ w_ob)) @ w_out

    y_l = merge(oa_l, ob_l, gt_l)
    if not need_ctx:
        return None, y_l
    qa_c, cq_c, gt_c = split_cols(p_c[..., KEY_COLS:], QUERY_SIZES)
    qa_c = qa_c.reshape(B, Lc, WIN_KV_HEADS, WIN_GROUP, WIN_HEAD_DIM)
    oa_c = window_attention_ctx(qa_c, ka_c, va_c, sink_g)
    qn_c, qr_c = mla_expand_q(cq_c, g_qn, w_uq)
    ob_c = mla_dense(qn_c, qr_c, kn_c, kr_c, v_c).reshape(B, Lc, MLA_OUT_W)
    return merge(oa_c, ob_c, gt_c), y_l

def ec_moe(h, w_router, w_gate, w_up, w_down):
    B, N, D = h.shape
    cap = CAPACITY_FACTOR * N // N_EXPERTS
    aff = jax.nn.softmax((h @ w_router).astype(jnp.float32), axis=-1)
    top_aff, top_idx = lax.top_k(jnp.swapaxes(aff, 1, 2), cap)
    xg = jax.vmap(lambda hb, ib: hb[ib])(h, top_idx)
    a = jnp.einsum('becd,edf->becf', xg, w_gate)
    u = jnp.einsum('becd,edf->becf', xg, w_up)
    y = jnp.einsum('becf,efd->becd', jax.nn.silu(a) * u, w_down) * top_aff[..., None].astype(h.dtype)
    return jax.vmap(lambda yb, ib: jnp.zeros((N, D), h.dtype).at[ib.reshape(-1)].add(yb.reshape(-1, D)))(y, top_idx)

def setup_inputs(seed: int = 0) -> dict:
    key = jax.random.key(seed)
    ks = jax.random.split(key, 24)
    f32 = jnp.float32
    L, D = DEPTH, D_MODEL

    def nrm(k, shape, scale):
        return jax.random.normal(k, shape, f32) * scale

    def gain(k, shape):
        return 1.0 + 0.02 * jax.random.normal(k, shape, f32)

    return {
        "x": nrm(ks[0], (BATCH, SEQ, D), 1.0),
        "c": nrm(ks[1], (BATCH, D), 1.0),
        "ctx": nrm(ks[2], (BATCH, CTX_LEN, D), 1.0),
        "c_ctx": nrm(ks[3], (D,), 1.0),
        "w_ada": nrm(ks[4], (L, D, 6 * D), 0.5 * D ** -0.5),
        "b_ada": nrm(ks[5], (L, 6 * D), 0.02),
        "w_in": nrm(ks[6], (L, D, IN_COLS), D ** -0.5),
        "attn_sink": nrm(ks[7], (L, WIN_HEADS), 0.5),
        "mla_q_norm": gain(ks[8], (L, MLA_Q_RANK)),
        "mla_kv_norm": gain(ks[9], (L, MLA_KV_RANK)),
        "w_uq": nrm(ks[10], (L, MLA_Q_RANK, MLA_HEADS * (MLA_NOPE_DIM + MLA_ROPE_DIM)), MLA_Q_RANK ** -0.5),
        "w_ukv": nrm(ks[11], (L, MLA_KV_RANK, MLA_HEADS * (MLA_NOPE_DIM + MLA_V_DIM)), MLA_KV_RANK ** -0.5),
        "w_oa": nrm(ks[12], (L, WIN_Q_W, D), WIN_Q_W ** -0.5),
        "w_ob": nrm(ks[13], (L, MLA_OUT_W, D), MLA_OUT_W ** -0.5),
        "w_out": nrm(ks[14], (L, D, D), BETA * D ** -0.5),
        "ln1_g": gain(ks[15], (L, D)),
        "ln1_b": nrm(ks[16], (L, D), 0.02),
        "w_router": nrm(ks[17], (L, D, N_EXPERTS), D ** -0.5),
        "w_exp_gate": nrm(ks[18], (L, N_EXPERTS, D, EXPERT_FF), D ** -0.5),
        "w_exp_up": nrm(ks[19], (L, N_EXPERTS, D, EXPERT_FF), D ** -0.5),
        "w_exp_down": nrm(ks[20], (L, N_EXPERTS, EXPERT_FF, D), BETA * EXPERT_FF ** -0.5),
        "ln2_g": gain(ks[21], (L, D)),
        "ln2_b": nrm(ks[22], (L, D), 0.02),
    }

def reference(x, c, ctx, c_ctx, w_ada, b_ada, w_in, attn_sink, mla_q_norm, mla_kv_norm, w_uq, w_ukv,
              w_oa, w_ob, w_out, ln1_g, ln1_b, w_router, w_exp_gate, w_exp_up, w_exp_down, ln2_g, ln2_b):
    n = x.shape[1]
    rope_win = axial_angles(n, WIN_HEAD_DIM)
    rope_mla = axial_angles(n, MLA_ROPE_DIM)
    x_l, x_c = x, ctx
    for l in range(DEPTH):
        need_ctx = l < DEPTH - 1
        m_l = adaln(c, w_ada[l], b_ada[l])
        m_c = adaln(c_ctx[None], w_ada[l], b_ada[l])
        h_l = modulate(x_l, m_l[0], m_l[1])
        h_c = modulate(x_c, m_c[0], m_c[1])
        y_c, y_l = token_mixer(h_c, h_l, w_in[l], attn_sink[l], mla_q_norm[l], mla_kv_norm[l], w_uq[l], w_ukv[l],
                               w_oa[l], w_ob[l], w_out[l], rope_win, rope_mla, need_ctx)
        x_l = layer_norm(ALPHA * x_l + m_l[2] * y_l, ln1_g[l], ln1_b[l])
        h_l = modulate(x_l, m_l[3], m_l[4])
        x_l = layer_norm(ALPHA * x_l + m_l[5] * ec_moe(h_l, w_router[l], w_exp_gate[l], w_exp_up[l], w_exp_down[l]),
                         ln2_g[l], ln2_b[l])
        if need_ctx:
            x_c = layer_norm(ALPHA * x_c + m_c[2] * y_c, ln1_g[l], ln1_b[l])
            h_c = modulate(x_c, m_c[3], m_c[4])
            x_c = layer_norm(ALPHA * x_c + m_c[5] * ec_moe(h_c, w_router[l], w_exp_gate[l], w_exp_up[l], w_exp_down[l]),
                             ln2_g[l], ln2_b[l])
    return x_l


_drawn_inputs = setup_inputs


def setup_inputs(seed=0):
    import zlib

    import numpy as np

    out = dict(_drawn_inputs(seed))
    spreads = {}
    factors = {'ctx': 8.0,
     'c_ctx': 4.205,
     'b_ada': 8.0,
     'attn_sink': 64.0,
     'mla_q_norm': 8.0,
     'mla_kv_norm': 8.0,
     'w_uq': 8.0,
     'w_oa': 2.807,
     'w_ob': 2.815}
    for name, (base, spread) in spreads.items():
        noise = np.random.default_rng([zlib.crc32(name.encode()), seed]).standard_normal(out[name].shape)
        drawn = base * np.exp(spread * noise) if base else spread * noise
        out[name] = __import__('jax').numpy.asarray(drawn.astype(out[name].dtype))
    for name, factor in factors.items():
        out[name] = (out[name] * factor).astype(out[name].dtype)
    return out
```

```python
from contextlib import ExitStack

import concourse.bass as bass
import numpy as np
from concourse import mybir

F32 = mybir.dt.float32
U32 = mybir.dt.uint32
ALU = mybir.AluOpType
ACT = mybir.ActivationFunctionType
AX = mybir.AxisListType

P = 128
D = 1024
KD = D // P
CTX, SEQ = 256, 1024
TOK = CTX + SEQ
TC, TT = CTX // P, TOK // P
DEPTH = 2
GRID_W = 64
WH, WKV, WD = 8, 2, 64
MH, NOPE, ROPE, MV = 8, 64, 32, 64
QR, KVR = 384, 256
MQ = NOPE + ROPE
E, FF = 16, 1024
CAP_L, CAP_C = 2 * SEQ // E, 2 * CTX // E
THETA = 10000.0
LN_EPS, RMS_EPS, NEG = 1e-5, 1e-6, -1e30
ALPHA = float((2 * DEPTH) ** 0.25)
WSCALE = float(WD ** -0.5)
MSCALE = float(MQ ** -0.5)
C_KA, C_CKV, C_KR, C_QA, C_CQ, C_G = 0, 256, 512, 544, 1056, 1440
NPJ = C_G


def ds(i, n):
    return slice(i, i + n) if isinstance(i, int) else bass.ds(i, n)


class Sems:

    def __init__(self, sems, before=None):
        self.sems, self.before = sems, before or {}

    def __getitem__(self, name):
        return self.sems[name]

    def __call__(self, name, n):
        return self.sems[name], n + self.before.get(name, 0)


def layer_counts(tiles, chunks, tr, ctx):
    pairs, g = tiles // 2, 1 + ctx
    n = dict(wp_in=14 * 16, q_in0=pairs * 48, q_in1=pairs * 48, m_in=32, tr=tr, pt=tr, pv=pairs * 32, hT_in0=16, hT_in1=16, hT_in2=16, mw_in0=KD * 32, mw_in1=KD * 32,
             wo_in=16, lnc_in=5 * 16, m5_in=32, z_in0=16 * pairs, z_in1=16 * pairs, gb2_in=32, out_st=16 * tiles)
    n |= {f"ring{i}": 16 * E * (2 if i < 4 else 1) for i in range(8)}
    n |= {k: 16 * TT for k in "x_in h_st qW_st qM_st".split()}
    n |= {k: TT for k in "h_a h_d p1 p2 p0 rms rstd norm latT latc_a latc_d used_d ropeW kr kn qro tW qW_cp ka_cp".split()}
    n |= {k: 2 * TT for k in "xT ukv uq tK tQ kT_cp qM_cp".split()}
    n |= {k: 16 * pairs for k in "sM sW mxM mxW pM pW".split()}
    n |= {k: KD * chunks for k in "g sg mrg".split()}
    n |= {k: 16 * tiles for k in "xr_in x1_st z_st".split()}
    n |= {k: tiles for k in "es tot mst y y_used lnv lnr lnb lnn x1 h2a h2d zs z_set rt rt_cp st2 sq2 rs2 n2 g2".split()}
    n |= {k: 2 * tiles for k in "osb fT fcp x1T".split()}
    n |= {k: 1 for k in "sm_m sm_e aff affT topk sel sel_cp".split()}
    n |= {k: E for k in "stage_g stage_s xa xd".split()}
    n |= {k: 16 * E * g for k in "gat sc".split()}
    n |= {k: 8 * E for k in "au sil act yt".split()}
    n |= {k: 4 * E for k in "yc_a yc_d".split()}
    n |= {k: 2 * E for k in "xgT bk ylat".split()}
    n["yctx"] = 2 * E * ctx
    return n


def build(nc, a, out):
    with ExitStack() as ctx:
        def dram(name, shape):
            return nc.dram_tensor(name, shape, F32, kind="Internal").ap()

        mod_d = dram("mod_rows", (DEPTH, 96, P))
        hT_d = dram("h_transposed", (P, KD, TOK))
        qM_d = dram("q_latent_attn", (TT, MQ, MH * P))
        qW_d = dram("q_window", (TT, P, 4 * P))
        x1_d = dram("x_mid", (TOK, D))
        z_d = dram("moe_sum", (TOK, D))
        xs_d = dram("x_next", (TOK, D))

        WORDS = 53200
        arena = ctx.enter_context(nc.sbuf_tensor("arena", [P, WORDS], F32))
        PS = ctx.enter_context(nc.psum_tensor("PS", [P, 8, 512], F32))

        def at(off, *dims):
            n = int(np.prod(dims))
            assert off + n <= WORDS, (off, dims)
            v = arena[:, off:off + n]
            if len(dims) == 1:
                return v
            names = "abcd"[:len(dims)]
            return v.rearrange(f"p ({' '.join(names)}) -> p {' '.join(names)}", **{c: d for c, d in zip(names, dims)})

        ident = at(0, P)
        modT = at(128, DEPTH, 2, 6, KD)
        silc = at(320, 2, KD)
        gcol = at(336, DEPTH, 5)
        epsc = at(346, 2)
        sinks = at(352, DEPTH, 2, WH)
        stat = at(384, 96)
        ones1 = at(480, 2)
        R = 512
        RING, SLOT = 12, KD * 256
        O = R + RING * SLOT
        adaw = at(O, 2, KD, 512)
        adab = at(O + 8192, 2, 512)
        adar = at(O + 9216, 2, 512)
        crow = at(O + 10240, P)
        mrow = at(O + 10368, DEPTH, P)
        w_pj = at(R, KD, NPJ)
        w_uq = at(R + 11520, 3, MH * MQ)
        w_ukv = at(R + 13824, 2, MH * (NOPE + MV))
        hts = at(R + 15872, KD, P)
        xb = at(R + 16896, D)
        rW = at(R + 17920, 10, WD)
        rC = at(R + 18560, 10, WD)
        latn = at(R + 19200, KVR + QR)
        latTt = at(R + 19840, 5, P)
        ksb = at(R + 20480, MH, MQ)
        qsb = at(R + 21248, MH, MQ)
        qWs = at(R + 22016, 4, P)
        qMs = at(R + 22528, MH, P)
        tmpm = at(R + 23552, 4, ROPE)
        junk = at(R + 23680, QR)
        krr = at(R + 24064, ROPE)
        krt = at(R + 24096, ROPE)
        kT = at(O, MH, TOK)
        V = at(O + 10240, TT, MH * MV)
        kaZ = at(O + 15360, WKV, TOK + P)
        va = at(O + 18176, TT + 1, WKV * WD)
        tabs = at(O + 25728, TT, 192)
        oaT = at(R, 4, TOK)
        obT = at(R + 5120, 4, TOK)
        PM = at(R + 10240, 1280)
        PW = at(R + 11520, 640)
        PTM = at(R + 12160, 10, P)
        PTW = at(R + 13440, 5, P)
        qMt = at(R + 15360, 2, MH, P)
        qWt = at(R + 17408, 2, 4, P)
        mask = at(R + 18432, 2, 640)
        osb = at(R + 19712, 2, 512)
        hTr = at(O, KD, TOK)
        mrgT = at(O + 10240, KD, TOK)
        mwt = at(O + 20480, 2, 24, P)
        sg = at(R + 10240, 2, 2, 512)
        w_o = at(R + 14336, KD, D)
        xr = at(O, D)
        zt = at(O + 1024, D)
        xn = at(O + 2048, D)
        x1t = at(O + 3072, D)
        mst = at(O + 4096, KD, P)
        h2t = at(O + 5120, KD, P)
        zs = at(O + 6144, D)
        gb1 = at(O + 7168, 2, D)
        m2b = at(O + 20480, 2, D)
        wrt = at(O + 22528, KD, E)
        logit = at(O + 22656, TT, E)
        afft = at(O + 22816, TT, E)
        affT = at(O + 23040, TOK)
        wk = at(O + 24320, SEQ)
        vals = at(O + 25344, CAP_L)
        idx8 = at(O + 25472, CAP_L).bitcast(U32)
        idxf = at(O + 25600, CAP_L)
        valc = at(O + 25728, CAP_C)
        idc8 = at(O + 25760, CAP_C).bitcast(U32)
        idcf = at(O + 25792, CAP_C)
        idxT = at(O + 25824, 2, E).bitcast(U32)
        affS = at(O + 25856, 2, E)
        icur = at(O + 25888, 4).bitcast(U32)
        xg = at(O + 10240, D)
        xgc = at(O + 11264, D)
        xgT = at(O + 12288, KD, 160)
        actT = at(O + 13568, KD, 160)
        yT = at(O + 14848, KD, 160)
        Y = at(O + 16128, D)
        Yc = at(O + 17152, D)
        silb = at(O + 18176, 2, 160)
        m5b = at(O + 26000, 2, D)
        ring = at(R, RING, KD, 256)
        z2 = at(O + 19584, 2, D)
        o2 = at(O + 21632, 2, D)
        gb2 = at(O + 23680, 2, D)

        TL = [list(range(TT)), list(range(TC, TT))]
        NT = [len(t) for t in TL]
        NPAIR = [n // 2 for n in NT]
        CH = [[(0, 256), (256, 512), (768, 512)], [(256, 512), (768, 512)]]
        NCH = [len(c) for c in CH]
        NN = [CAP_L + CAP_C, CAP_L]

        def sems(names):
            return {n: ctx.enter_context(nc.semaphore(n)) for n in names}
        G = Sems(sems("const_in cond_in cT silc ada_in0 ada_in1 ada rowc mod_st modr_in modT modT_cp mod1 bars".split()))
        counts = layer_counts(TT, NCH[0], 32 + 4 * 80, 1)
        own = sems(counts)
        L = [Sems(own), Sems(own, counts)]
        block = ctx.enter_context(nc.Block())

        def x_rows(l, t):
            if l:
                return xs_d[ds(t * P, P), :]
            if isinstance(t, int) and t < TC:
                return a["ctx"][0, t * P:(t + 1) * P, :]
            return a["x"][0, ds((t - TC) * P, P), :]

        def tiles(eng, body, first=0):
            for t in range(first, TC):
                body(t, t, False)
            with eng.Fori(TC, TT - 1) as t:
                body(t, t, False)
            body(TT - 1, TT - 1, True)

        def kind(t):
            return 1 if isinstance(t, int) and t < TC else 0

        def mod_bc(l, v, part):
            r = (v * 6 + part) * KD
            return mod_d[l, r:r + KD, :].rearrange("(o k) p -> o (k p)", o=1).to_broadcast([P, D])

        def pairs(eng, l, body):
            if l == 0:
                body(0, 0, None)
                with eng.Fori(0, 4) as i:
                    body(i + 1, TC + i * 2, i)
            else:
                with eng.Fori(0, 4) as i:
                    body(i, TC + i * 2, i)

        UN = [(n // 16, (n % 16) // 2, n % 2) for n in range(32)]

        def nchunks(k, full):
            return (3, 2)[k] if full else 1

        def chunk_count(n, full):
            return sum(nchunks(UN[m][2], full) for m in range(n))

        def chunks_before(l, p, lp):
            if lp is None:
                return 0
            return p * chunk_count(32, True) if l else (p - 1) * chunk_count(32, True) + chunk_count(32, False)

        def peeled(eng, n, body):
            body(0)
            with eng.Fori(1, n) as i:
                body(i)

        def with_first(eng, body):
            body(0, False)
            with eng.Fori(1, E - 1) as e:
                body(e, False)
            body(E - 1, True)

        @block.sync
        def _(sp):
            def ld(dst, src, sem):
                sp.dma_start(dst, src).then_inc(sem, 16)

            ld(ident, a["ident"], G["const_in"])
            ld(crow[0:8, :], a["c"].rearrange("b (k p) -> (b k) p", p=P), G["cond_in"])
            ld(crow[8:16, :], a["c_ctx"].rearrange("(k p) -> k p", p=P), G["cond_in"])
            for l in range(DEPTH):
                with nc.allow_non_contiguous_dma(reason="five short columns"):
                    ld(gcol[:, l, 0:2], a["mla_kv_norm"][l].rearrange("(k p) -> p k", p=P), G["const_in"])
                    ld(gcol[:, l, 2:5], a["mla_q_norm"][l].rearrange("(k p) -> p k", p=P), G["const_in"])
                ld(sinks[:, l, 0, :], a["attn_sink"][l:l + 1, :].to_broadcast([P, WH]), G["const_in"])
            for l in range(DEPTH):
                def chunk(i, l=l):
                    for u in range(2):
                        j = l * 12 + i * 2 + u
                        if not isinstance(j, int) or j >= 2:
                            sp.wait_ge(G["ada"], j - 1)
                        cols = ds((i * 2 + u) * 512, 512)
                        ld(adaw[:, u], a["w_ada"][l].rearrange("(k p) n -> p k n", p=P)[:, :, cols], G[f"ada_in{u}"])
                        ld(adab[0:1, u, :], a["b_ada"][l:l + 1, cols], G[f"ada_in{u}"])
                peeled(sp, 6, chunk)
            sp.wait_ge(G["mod_st"], 16 * 12 * DEPTH)
            for l in range(DEPTH):
                ld(mrow[0:96, l, :], mod_d[l], G["modr_in"])

            for l in range(DEPTH):
                s = L[l]
                if l:
                    sp.wait_ge(*L[l - 1]("yt", 8 * E))
                    sp.wait_ge(*L[l - 1]("g2", NT[l - 1]))
                w = a["w_in"][l].rearrange("(k p) n -> p k n", p=P)
                if l == 0:
                    sp.wait_ge(G["modT_cp"], 1)
                for j in range(4):
                    for g in range(2):
                        c0 = C_QA + (g * 4 + j) * WD
                        ld(w_pj[:, :, (2 * j + g) * WD:(2 * j + g + 1) * WD], w[:, :, c0:c0 + WD], s["wp_in"])
                ld(w_pj[:, :, 512:1024], w[:, :, C_KA:C_KR], s["wp_in"])
                ld(w_pj[:, :, 1024:1408], w[:, :, C_CQ:C_G], s["wp_in"])
                ld(w_pj[:, :, 1408:1440], w[:, :, C_KR:C_QA], s["wp_in"])
                ld(w_uq, a["w_uq"][l].rearrange("(k p) n -> p k n", p=P), s["wp_in"])
                ld(w_ukv, a["w_ukv"][l].rearrange("(k p) n -> p k n", p=P), s["wp_in"])
                ld(tabs, a["rope"].rearrange("(t p) n -> p t n", p=P), s["wp_in"])
                if l:
                    sp.wait_ge(*L[l - 1]("out_st", 16 * NT[l - 1]))
                ld(xb, x_rows(l, 0), s["x_in"])

                def step(t, n, last):
                    sp.wait_ge(*s("h_a", t + 1))
                    sp.wait_ge(*s("h_d", t + 1))
                    ld(hT_d[:, :, ds(t * P, P)], hts, s["h_st"])
                    if not last:
                        sp.wait_ge(*s("xT", 2 * t + 2))
                        ld(xb, x_rows(l, t + 1), s["x_in"])
                    sp.wait_ge(*s("qW_cp", t + 1))
                    ld(qW_d[ds(t, 1)].rearrange("o p n -> (o p) n"), qWs.rearrange("p a b -> p (a b)"), s["qW_st"])
                    sp.wait_ge(*s("qM_cp", 2 * t + 2))
                    ld(qM_d[ds(t, 1)].rearrange("o p n -> (o p) n"), qMs[0:MQ].rearrange("p a b -> p (a b)"), s["qM_st"])
                tiles(sp, step)

                sp.wait_ge(*s("qM_st", 16 * TT))
                sp.wait_ge(*s("qW_st", 16 * TT))
                for u in range(2):
                    ld(mask[:, u, :], a["wmask"], s["m_in"])
                sp.wait_ge(*s("m_in", 32))

                def pair(p, t0, lp):
                    for u in range(2):
                        if not (isinstance(p, int) and p == 0):
                            sp.wait_ge(*s("sM", p * 16 - 8 + 8 * u))
                            sp.wait_ge(*s("sW", p * 16 - 8 + 8 * u))
                            sp.wait_ge(*s("mxW", p * 16 - 8 + 8 * u))
                        ld(qMt[0:MQ, u].rearrange("p a b -> p (a b)"), qM_d[ds(t0 + u, 1)].rearrange("o p n -> (o p) n"), s[f"q_in{u}"])
                        ld(qWt[:, u].rearrange("p a b -> p (a b)"), qW_d[ds(t0 + u, 1)].rearrange("o p n -> (o p) n"), s[f"q_in{u}"])
                        if lp is None:
                            ld(mask[:, u, 256:384], a["edge"][0, 0], s[f"q_in{u}"])
                        elif u == 0:
                            ld(mask[:, 0, 256:384], a["edge"][0, ds(lp, 1)].rearrange("o p n -> (o p) n"), s[f"q_in{u}"])
                        else:
                            ld(mask[:, 1, 512:640], a["edge"][1, ds(lp, 1)].rearrange("o p n -> (o p) n"), s[f"q_in{u}"])
                pairs(sp, l, pair)

                sp.wait_ge(*s("pv", 32 * NPAIR[l]))
                for ci, (c0, cn) in enumerate(CH[l]):
                    ld(hTr[:, :, c0:c0 + cn], hT_d[:, :, c0:c0 + cn], s[f"hT_in{ci}"])
                def weights(i):
                    for u in range(2):
                        f = i * 2 + u
                        if not isinstance(i, int):
                            sp.wait_ge(*s("g", (f - 1) * NCH[l]))
                        wg = w[:, :, C_G:C_G + 2 * D].rearrange("p k (g n) -> p k g n", g=2)
                        ld(mwt[:, u, 0:8, :], wg[:, :, 0, ds(f * P, P)], s[f"mw_in{u}"])
                        ld(mwt[:, u, 8:16, :], wg[:, :, 1, ds(f * P, P)], s[f"mw_in{u}"])
                        ld(mwt[:, u, 16:20, :], a["w_oa"][l].rearrange("(k p) n -> p k n", p=P)[:, :, ds(f * P, P)], s[f"mw_in{u}"])
                        ld(mwt[:, u, 20:24, :], a["w_ob"][l].rearrange("(k p) n -> p k n", p=P)[:, :, ds(f * P, P)], s[f"mw_in{u}"])
                peeled(sp, 4, weights)
                ld(w_o, a["w_out"][l].rearrange("(k p) n -> p k n", p=P), s["wo_in"])

                sp.wait_ge(*s("mrg", 8 * NCH[l]))
                ld(gb1[:, 0, :], a["ln1_g"][l:l + 1, :].to_broadcast([P, D]), s["lnc_in"])
                ld(gb1[:, 1, :], a["ln1_b"][l:l + 1, :].to_broadcast([P, D]), s["lnc_in"])
                for v in range(2):
                    ld(m2b[:, v, :], mod_bc(l, v, 2), s["lnc_in"])
                ld(wrt, a["w_router"][l].rearrange("(k p) e -> p k e", p=P), s["lnc_in"])
                for v in range(2):
                    ld(m5b[:, v, :], mod_bc(l, v, 5), s["m5_in"])
                ld(xr, x_rows(l, TL[l][0]), s["xr_in"])

                def step1(t, n, last):
                    n = t - TL[l][0]
                    if not last:
                        sp.wait_ge(*s("zs", n + 1))
                        ld(xr, x_rows(l, t + 1), s["xr_in"])
                    sp.wait_ge(*s("x1", n + 1))
                    ld(x1_d[ds(t * P, P), :], x1t, s["x1_st"])
                    sp.wait_ge(*s("z_set", n + 1))
                    ld(z_d[ds(t * P, P), :], zs, s["z_st"])
                tiles(sp, step1, TL[l][0])

                gw = a["w_exp_gate"][l]
                uw = a["w_exp_up"][l]
                dw = a["w_exp_down"][l]

                def experts(e):
                    first = isinstance(e, int)
                    for c in range(RING):
                        if first:
                            if c == 0:
                                sp.wait_ge(*s("mrg", 8 * NCH[l]))
                            if c == 7:
                                sp.wait_ge(*s("y", NT[l]))
                        elif c < 8:
                            sp.wait_ge(*s("au", (e - 1) * 8 + (c // 2) * 2 + 2))
                        else:
                            sp.wait_ge(*s("yt", (e - 1) * 8 + (c - 8) * 2 + 2))
                        if c < 8:
                            src, blk = (uw if c % 2 else gw), c // 2
                        else:
                            src, blk = dw, c - 8
                        v = src[ds(e, 1)].rearrange("o (k p) n -> p (o k) n", p=P)
                        ld(ring[:, c], v[:, :, blk * 256:(blk + 1) * 256], s[f"ring{c // 2 if c < 8 else c - 4}"])
                experts(0)
                with sp.Fori(1, E) as e:
                    experts(e)

                sp.wait_ge(*s("sc", 16 * E * (2 - l)))
                ld(gb2[:, 0, :], a["ln2_g"][l:l + 1, :].to_broadcast([P, D]), s["gb2_in"])
                ld(gb2[:, 1, :], a["ln2_b"][l:l + 1, :].to_broadcast([P, D]), s["gb2_in"])
                t0 = TL[l][0]
                for u in range(2):
                    ld(z2[:, u, :], z_d[(t0 + u) * P:(t0 + u + 1) * P, :], s[f"z_in{u}"])
                with sp.Fori(0, NPAIR[l] - 1) as i:
                    for u in range(2):
                        sp.wait_ge(*s("n2", i * 2 + u + 1))
                        ld(z2[:, u, :], z_d[ds((i * 2 + u + 2 + t0) * P, P), :], s[f"z_in{u}"])

        @block.tensor
        def _(pe):
            def mms(o, pairs_, start=True, stop=True):
                n = len(pairs_)
                for i, (lt, rh) in enumerate(pairs_):
                    m = pe.matmul(o, lt, rh, start=start and i == 0, stop=stop and i == n - 1)
                return m

            def tr(o, i):
                return pe.transpose(o, i, ident)

            pe.wait_ge(G["const_in"], 16 * 7)
            pe.wait_ge(G["cond_in"], 32)
            pe.matmul(PS[:, 7, 0:16], crow[0:16, :], ident[0:16, 0:16], start=True, stop=True).then_inc(G["cT"], 1)
            pe.wait_ge(G["silc"], 2)
            for l in range(DEPTH):
                def chunk(i, l=l):
                    for u in range(2):
                        j = l * 12 + i * 2 + u
                        pe.wait_ge(G[f"ada_in{u}"], (l * 6 + i + 1) * 32)
                        if not isinstance(j, int) or j >= 2:
                            pe.wait_ge(G["rowc"], j - 1)
                        mms(PS[0:2, u, :], [(silc[:, :, k], adaw[:, u, k, :]) for k in range(KD)], stop=False)
                        pe.matmul(PS[0:2, u, :], ones1[0:1, :], adab[0:1, u, :], start=False, stop=True).then_inc(G["ada"], 1)
                peeled(pe, 6, chunk)
            pe.wait_ge(G["modr_in"], 32)
            for l in range(DEPTH):
                m = pe.matmul(PS[:, 2, l * 96:(l + 1) * 96], mrow[0:96, l, :], ident[0:96, 0:96], start=True, stop=True)
            m.then_inc(G["modT"], 1)

            for l in range(DEPTH):
                s = L[l]

                def x_transposes(t):
                    pe.wait_ge(*s("x_in", (t + 1) * 16))
                    for c in range(2):
                        for k in range(4):
                            m = tr(PS[:, 4 + c, k * P:(k + 1) * P], xb[:, (c * 4 + k) * P:(c * 4 + k + 1) * P])
                        m.then_inc(s["xT"], 1)

                if l == 0:
                    pe.wait_ge(G["mod1"], 1)
                else:
                    pe.wait_ge(*L[l - 1]("bk", 2 * E))
                x_transposes(0)
                pe.wait_ge(*s("wp_in", 16 * 14))

                def step(t, n, last):
                    pe.wait_ge(*s("h_a", t + 1))
                    pe.wait_ge(*s("h_d", t + 1))
                    if not (isinstance(t, int) and t == 0):
                        pe.wait_ge(*s("norm", t))
                        pe.wait_ge(*s("used_d", t))
                        pe.wait_ge(*s("ka_cp", t))
                    mms(PS[:, 1, :], [(hts[:, k, :], w_pj[:, k, 512:1024]) for k in range(KD)]).then_inc(s["p1"], 1)
                    mms(PS[:, 2, 0:416], [(hts[:, k, :], w_pj[:, k, 1024:1440]) for k in range(KD)]).then_inc(s["p2"], 1)
                    mms(PS[:, 0, :], [(hts[:, k, :], w_pj[:, k, 0:512]) for k in range(KD)]).then_inc(s["p0"], 1)
                    pe.wait_ge(*s("norm", t + 1))
                    if not (isinstance(t, int) and t == 0):
                        pe.wait_ge(*s("qW_cp", t))
                        pe.wait_ge(*s("qM_cp", 2 * t))
                        pe.wait_ge(*s("kT_cp", 2 * t))
                    for k in range(2):
                        tr(PS[:, 7, k * P:(k + 1) * P], latn[:, k * P:(k + 1) * P])
                    for k in range(3):
                        m = tr(PS[:, 3, k * P:(k + 1) * P], latn[:, KVR + k * P:KVR + (k + 1) * P])
                    m.then_inc(s["latT"], 1)
                    if not last:
                        x_transposes(t + 1)
                    pe.wait_ge(*s("latc_a", t + 1))
                    mms(PS[:, 6, :], [(latTt[:, k, :], w_ukv[:, k, 512:1024]) for k in range(2)]).then_inc(s["ukv"], 1)
                    if not last:
                        pe.wait_ge(*s("h_d", t + 2))
                        pe.wait_ge(*s("h_a", t + 2))
                    mms(PS[:, 5, :], [(latTt[:, k, :], w_ukv[:, k, 0:512]) for k in range(2)]).then_inc(s["ukv"], 1)
                    pe.wait_ge(*s("latc_d", t + 1))
                    for h in range(2):
                        mms(PS[:, 3 + h, 0:384], [(latTt[:, 2 + k, :], w_uq[:, k, h * 384:(h + 1) * 384]) for k in range(3)]).then_inc(s["uq"], 1)
                    pe.wait_ge(*s("ropeW", t + 1))
                    for k in range(4):
                        tr(PS[:, 7, k * P:(k + 1) * P], rW[:, 2 * k:2 * k + 2, :])
                    tr(PS[:, 1, 0:P], rW[:, 8:10, :]).then_inc(s["tW"], 1)
                    pe.wait_ge(*s("kr", t + 1))
                    pe.wait_ge(*s("kn", t + 1))
                    for g in (1, 0):
                        for h in range(4):
                            m = tr(PS[0:MQ, 5 + g, h * P:(h + 1) * P], ksb[:, g * 4 + h, :])
                        m.then_inc(s["tK"], 1)
                    pe.wait_ge(*s("qro", t + 1))
                    for g in range(2):
                        for h in range(4):
                            m = tr(PS[0:MQ, 3 + g, h * P:(h + 1) * P], qsb[:, g * 4 + h, :])
                        m.then_inc(s["tQ"], 1)
                tiles(pe, step)

                pe.wait_ge(*s("kT_cp", 2 * TT))
                pe.wait_ge(*s("qM_cp", 2 * TT))
                pe.wait_ge(*s("qW_cp", TT))
                pe.wait_ge(*s("ka_cp", TT))
                pe.wait_ge(*s("used_d", TT))

                def pair(p, t0, lp):
                    full = lp is not None
                    ch0 = chunks_before(l, p, lp)

                    def s_parts(n):
                        u, h, k = UN[n]
                        cnt = p * 16 + n // 2

                        def head():
                            if h == 0:
                                pe.wait_ge(*s(f"q_in{u}", p * 48 + 48))
                            if k == 0:
                                if n // 2 or not (isinstance(p, int) and p == 0):
                                    pe.wait_ge(*s("pM", cnt))
                            elif n // 2 or not (isinstance(p, int) and p == 0):
                                pe.wait_ge(*s("mxW", cnt))

                        parts = []
                        if k == 0:
                            nk = 1280 if full else 256
                            q = qMt[0:MQ, u, h, :]
                            for b, c0 in enumerate(range(0, nk, 512)):
                                cn = min(512, nk - c0)
                                parts.append(lambda b=b, c0=c0, cn=cn: pe.matmul(
                                    PS[:, b, 0:cn], q, kT[0:MQ, h, c0:c0 + cn], start=True, stop=True))
                        else:
                            q = qWt[:, u, h % 4, :]
                            kz = kaZ[:, h // 4, :]

                            def bank0():
                                m = pe.matmul(PS[:, 3, 0:256], q, kz[:, 0:256], start=True, stop=True)
                                if full:
                                    m = pe.matmul(PS[:, 3, 256:512], q, kz[:, ds((lp * 2 + u + 1) * P, 256)], start=True, stop=True)
                                return m
                            parts.append(bank0)
                            if full:
                                parts.append(lambda: pe.matmul(PS[:, 4, 0:P], q, kz[:, ds((lp * 2 + u + 3) * P, P)], start=True, stop=True))
                        fns = []
                        for i, f in enumerate(parts):
                            def g(i=i, f=f):
                                if i == 0:
                                    head()
                                m = f()
                                if i == len(parts) - 1:
                                    m.then_inc(s["sW" if k else "sM"], 1)
                            fns.append(g)
                        return fns

                    for n in range(2):
                        for f in s_parts(n):
                            f()
                    for n in range(32):
                        u, h, k = UN[n]
                        nxt = s_parts(n + 2) if n < 30 else []
                        src, dst = (PW, PTW) if k else (PM, PTM)
                        nkt = ((10, 5)[k]) if full else 2
                        pe.wait_ge(*s("pW" if k else "pM", p * 16 + n // 2 + 1))
                        nc_ = nchunks(k, full)
                        for c in range(nc_):
                            cc = ch0 + chunk_count(n, full) + c
                            if not (isinstance(cc, int) and cc == 0):
                                pe.wait_ge(*s("pt", cc))
                            for kt in range(c * 4, min(c * 4 + 4, nkt)):
                                m = tr(PS[:, 5, (kt - c * 4) * P:(kt - c * 4 + 1) * P], src[:, kt * P:(kt + 1) * P])
                            m.then_inc(s["tr"], 1)
                            if c < len(nxt):
                                nxt[c]()
                        for c in range(nc_, len(nxt)):
                            nxt[c]()
                        pe.wait_ge(*s("pt", ch0 + chunk_count(n + 1, full)))
                        if h == 0 and not (isinstance(p, int) and p == 0 and u == 0):
                            pe.wait_ge(*s("osb", (p * 2 + u) * 2))
                        oo = PS[:, 6 + k, h * 64:(h + 1) * 64]
                        if k == 0:
                            vs = [V[:, kt, h * MV:(h + 1) * MV] for kt in range(nkt)]
                        else:
                            g = h // 4
                            vs = [va[:, kt, g * WD:(g + 1) * WD] for kt in range(2)]
                            if full:
                                vs += [va[:, ds(lp * 2 + u + 1 + j, 1), g * WD:(g + 1) * WD].rearrange("p o d -> p (o d)") for j in range(3)]
                        mms(oo, [(dst[:, kt, :], vs[kt]) for kt in range(nkt)]).then_inc(s["pv"], 1)
                        if n in (18, 31):
                            fu = 0 if n == 18 else 1
                            for kk in range(2):
                                pe.wait_ge(*s("osb", (p * 2 + fu) * 2 + kk + 1))
                                pe.wait_ge(*s("pt", ch0 + chunk_count(n + 1, full)))
                                if kk or fu or not (isinstance(p, int) and p == 0):
                                    pe.wait_ge(*s("fcp", (p * 2 + fu) * 2 + kk))
                                for j in range(4):
                                    m = tr(PS[:, 5, j * P:(j + 1) * P], osb[:, kk, j * P:(j + 1) * P])
                                m.then_inc(s["fT"], 1)
                            pe.wait_ge(*s("fcp", (p * 2 + fu) * 2 + 2))
                pairs(pe, l, pair)

                def merge_block(i, u):
                    f = i * 2 + u
                    for ci, (c0, cn) in enumerate(CH[l]):
                        q = f * NCH[l] + ci
                        set_ = (u * NCH[l] + ci) % 2 * 4
                        if not isinstance(q, int) or q >= 2:
                            pe.wait_ge(*s("mrg", q - 1))
                        if ci == 0:
                            pe.wait_ge(*s(f"mw_in{u}", (i + 1) * 64))
                        mms(PS[:, set_, 0:cn], [(mwt[:, u, 16 + k, :], oaT[:, k, c0:c0 + cn]) for k in range(4)])
                        mms(PS[:, set_ + 1, 0:cn], [(mwt[:, u, 20 + k, :], obT[:, k, c0:c0 + cn]) for k in range(4)])
                        pe.wait_ge(*s(f"hT_in{ci}", 16))
                        mms(PS[:, set_ + 2, 0:cn], [(mwt[:, u, k, :], hTr[:, k, c0:c0 + cn]) for k in range(KD)])
                        mms(PS[:, set_ + 3, 0:cn], [(mwt[:, u, 8 + k, :], hTr[:, k, c0:c0 + cn]) for k in range(KD)]).then_inc(s["g"], 1)
                for u in range(2):
                    merge_block(0, u)
                with pe.Fori(1, 4) as i:
                    for u in range(2):
                        merge_block(i, u)

                pe.wait_ge(*s("mrg", 8 * NCH[l]))
                pe.wait_ge(*s("wo_in", 16))
                pe.wait_ge(*s("lnc_in", 16 * 5))

                def y_tile(t):
                    n = t - TL[l][0]
                    pe.wait_ge(*s("mst", n + 1))
                    if not (isinstance(n, int) and n == 0):
                        pe.wait_ge(*s("y_used", n))
                    for h in range(2):
                        m = mms(PS[:, h, :], [(mst[:, k, :], w_o[:, k, h * 512:(h + 1) * 512]) for k in range(KD)])
                    m.then_inc(s["y"], 1)

                def x1_transposes(t):
                    n = t - TL[l][0]
                    pe.wait_ge(*s("x1", n + 1))
                    if not (isinstance(n, int) and n == 0):
                        pe.wait_ge(*s("h2a", n))
                        pe.wait_ge(*s("h2d", n))
                    for c in range(2):
                        for k in range(4):
                            m = tr(PS[:, 2 + c, k * P:(k + 1) * P], x1t[:, (c * 4 + k) * P:(c * 4 + k + 1) * P])
                        m.then_inc(s["x1T"], 1)
                    pe.wait_ge(*s("h2a", n + 1))
                    pe.wait_ge(*s("h2d", n + 1))
                    if not (isinstance(n, int) and n == 0):
                        pe.wait_ge(*s("rt_cp", n))
                    mms(PS[:, 4, 0:E], [(h2t[:, k, :], wrt[:, k, :]) for k in range(KD)]).then_inc(s["rt"], 1)

                t0 = TL[l][0]
                y_tile(t0)
                if l == 0:
                    y_tile(1)
                    x1_transposes(0)
                    y_tile(2)
                    x1_transposes(1)
                with pe.Fori(TC + 1, TT) as t:
                    y_tile(t)
                    x1_transposes(t - 1)
                x1_transposes(TT - 1)

                pe.wait_ge(*s("aff", 1))
                for i, t in enumerate(TL[l]):
                    m = pe.matmul(PS[0:E, 5 + t // 4, (t % 4) * P:(t % 4 + 1) * P], afft[:, t, :], ident, start=True, stop=True)
                m.then_inc(s["affT"], 1)
                pe.wait_ge(*s("topk", 1))
                pe.matmul(PS[:, 0, 0:E], idxf[0:E, :], ident[0:E, 0:E], start=True, stop=True)
                m = pe.matmul(PS[:, 0, E:2 * E], vals[0:E, :], ident[0:E, 0:E], start=True, stop=True)
                if l == 0:
                    pe.matmul(PS[0:CAP_C, 0, 2 * E:3 * E], idcf[0:E, :], ident[0:E, 0:E], start=True, stop=True)
                    m = pe.matmul(PS[0:CAP_C, 0, 3 * E:4 * E], valc[0:E, :], ident[0:E, 0:E], start=True, stop=True)
                m.then_inc(s["sel"], 1)

                N = NN[l]

                def xg_transposes(e):
                    pe.wait_ge(*s("gat", (e + 1) * 16 * (2 - l)))
                    if not (isinstance(e, int) and e == 0):
                        pe.wait_ge(*s("ylat", 2 * e))
                        if l == 0:
                            pe.wait_ge(*s("yctx", 2 * e))
                    for c in range(2):
                        for k in range(4):
                            m = tr(PS[:, c, k * P:(k + 1) * P], xg[:, (c * 4 + k) * P:(c * 4 + k + 1) * P])
                        if l or c == 0:
                            m.then_inc(s["xgT"], 1)
                    if l == 0:
                        for k in range(KD):
                            m = pe.matmul(PS[:, 2, k * 32:(k + 1) * 32], xgc[0:CAP_C, k * P:(k + 1) * P], ident[0:CAP_C, 0:CAP_C], start=True, stop=True)
                        m.then_inc(s["xgT"], 1)

                def expert(e, last):
                    pe.wait_ge(*s("xa", e + 1))
                    pe.wait_ge(*s("xd", e + 1))
                    for f in range(KD):
                        if f % 2 == 0:
                            pe.wait_ge(*s(f"ring{f // 2}", (e + 1) * 32))
                        if not (isinstance(e, int) and e == 0 and f < 2):
                            pe.wait_ge(*s("act", e * 8 + f - 1))
                        for h in range(2):
                            m = mms(PS[:, 3 + f % 2, h * N:(h + 1) * N],
                                    [(ring[:, (f // 2) * 2 + h, k, (f % 2) * P:(f % 2 + 1) * P], xgT[:, k, 0:N]) for k in range(KD)])
                        m.then_inc(s["au"], 1)
                    for d in range(KD):
                        if d % 2 == 0:
                            pe.wait_ge(*s(f"ring{4 + d // 2}", (e + 1) * 16))
                        if d == 0:
                            pe.wait_ge(*s("act", (e + 1) * 8))
                        if not (isinstance(e, int) and e == 0 and d < 2):
                            pe.wait_ge(*s("yc_d" if d % 2 else "yc_a", e * 4 + d // 2))
                        mms(PS[:, 5 + d % 2, 0:N], [(ring[:, 8 + d // 2, k, (d % 2) * P:(d % 2 + 1) * P], actT[:, k, 0:N]) for k in range(KD)]).then_inc(s["yt"], 1)
                    pe.wait_ge(*s("yc_a", e * 4 + 4))
                    pe.wait_ge(*s("yc_d", e * 4 + 4))
                    if not (isinstance(e, int) and e == 0):
                        pe.wait_ge(*s("ylat", 2 * e))
                        if l == 0:
                            pe.wait_ge(*s("yctx", 2 * e))
                    for r in range(2):
                        for j in range(4):
                            m = tr(PS[:, (7, 0)[r], j * P:(j + 1) * P], yT[:, r * 4 + j, 0:P])
                        if l == 0:
                            for j in range(4):
                                m = pe.matmul(PS[0:CAP_C, 1 + r, j * P:(j + 1) * P], yT[:, r * 4 + j, P:P + CAP_C], ident, start=True, stop=True)
                        m.then_inc(s["bk"], 1)
                    if not last:
                        xg_transposes(e + 1)

                pe.wait_ge(*s("sel_cp", 1))
                xg_transposes(0)
                with_first(pe, expert)

        @block.scalar
        def _(act):
            A = act.activation
            act.wait_ge(G["cT"], 1)
            A(silc.rearrange("p v k -> p (v k)"), PS[:, 7, 0:16], ACT.Silu).then_inc(G["silc"], 1)
            act.wait_ge(G["modT"], 1)
            A(arena[:, 128:320], PS[:, 2, 0:192], ACT.Copy).then_inc(G["modT_cp"], 1)

            for l in range(DEPTH):
                s = L[l]

                def h_half(t, sem_val=None):
                    v = kind(t)
                    act.wait_ge(*s("xT", 2 * t + 1))
                    if not (isinstance(t, int) and t == 0):
                        act.wait_ge(*s("h_st", 16 * t))
                        act.wait_ge(*s("p0", t))
                    for k in range(4):
                        m = A(hts[:, k, :], PS[:, 4, k * P:(k + 1) * P], ACT.Identity,
                              scale=modT[:, l, v, 1, k:k + 1], bias=modT[:, l, v, 0, k:k + 1])
                    m.then_inc(s["h_a"], 1)
                act.wait_ge(G["mod1"], 1)
                act.wait_ge(G["bars"], 3)
                h_half(0)

                def step(t, n, last):
                    act.wait_ge(*s("p1", t + 1))
                    A(junk[:, 0:KVR], PS[:, 1, 256:512], ACT.Square, accum_out=stat[:, 0:1])
                    act.drain()
                    act.wait_ge(*s("p2", t + 1))
                    A(junk[:, 0:QR], PS[:, 2, 0:QR], ACT.Square, accum_out=stat[:, 1:2])
                    act.drain()
                    A(stat[:, 2:3], stat[:, 0:1], ACT.Sqrt, scale=1.0 / KVR, bias=epsc[:, 1:2])
                    A(stat[:, 3:4], stat[:, 1:2], ACT.Sqrt, scale=1.0 / QR, bias=epsc[:, 1:2]).then_inc(s["rms"], 1)
                    act.wait_ge(*s("rstd", t + 1))
                    if not (isinstance(t, int) and t == 0):
                        act.wait_ge(*s("latT", t))
                    A(latn[:, 0:KVR], PS[:, 1, 256:512], ACT.Copy, scale=stat[:, 4:5])
                    A(latn[:, KVR:], PS[:, 2, 0:QR], ACT.Copy, scale=stat[:, 5:6]).then_inc(s["norm"], 1)
                    act.wait_ge(*s("latT", t + 1))
                    for k in range(2):
                        m = A(latTt[:, k, :], PS[:, 7, k * P:(k + 1) * P], ACT.Copy, scale=gcol[:, l, k:k + 1])
                    m.then_inc(s["latc_a"], 1)
                    if not last:
                        h_half(t + 1)
                    for i, g in enumerate((1, 0)):
                        act.wait_ge(*s("ukv", 2 * t + i + 1))
                        if i == 0 and not (isinstance(t, int) and t == 0):
                            act.wait_ge(*s("tK", 2 * t))
                        src = PS[:, 5 + g, :].rearrange("p (h c) -> p h c", h=4)
                        A(V[:, ds(t, 1), g * 256:(g + 1) * 256].rearrange("p o (h c) -> p (o h) c", h=4), src[:, :, NOPE:], ACT.Copy)
                        m = A(ksb[:, g * 4:(g + 1) * 4, 0:NOPE], src[:, :, 0:NOPE], ACT.Copy)
                    m.then_inc(s["kn"], 1)
                    act.wait_ge(*s("tW", t + 1))
                    if not (isinstance(t, int) and t == 0):
                        act.wait_ge(*s("qW_st", 16 * t))
                    A(qWs.rearrange("p a b -> p (a b)"), PS[:, 7, :], ACT.Copy).then_inc(s["qW_cp"], 1)
                    for i, g in enumerate((1, 0)):
                        act.wait_ge(*s("tK", 2 * t + i + 1))
                        A(kT[0:MQ, g * 4:(g + 1) * 4, ds(t * P, P)], PS[0:MQ, 5 + g, :].rearrange("p (h c) -> p h c", h=4), ACT.Copy).then_inc(s["kT_cp"], 1)
                tiles(act, step)

                def pair(p, t0, lp):
                    full = lp is not None
                    ch0 = chunks_before(l, p, lp)

                    def expo(n):
                        u, h, k = UN[n]
                        cnt = p * 16 + n // 2
                        act.wait_ge(*s("mxW" if k else "mxM", cnt + 1))
                        if k == 0:
                            nk = 1280 if full else 256
                            if n >= 2 or not (isinstance(p, int) and p == 0):
                                act.wait_ge(*s("tr", ch0 + chunk_count(n - 1, full) if n >= 2 else ch0))
                            src = PS[:, 0:3, :].rearrange("p b n -> p (b n)")[:, 0:nk]
                            A(PM[:, 0:nk], src, ACT.Exp, scale=MSCALE, bias=stat[:, 32 + u * 8 + h:33 + u * 8 + h],
                              accum_out=stat[:, 64 + u * 8 + h:65 + u * 8 + h]).then_inc(s["pM"], 1)
                        else:
                            nk = 640 if full else 256
                            A(PW[:, 0:nk], PW[:, 0:nk], ACT.Exp, bias=stat[:, 48 + u * 8 + h:49 + u * 8 + h],
                              accum_out=stat[:, 80 + u * 8 + h:81 + u * 8 + h]).then_inc(s["pW"], 1)

                    def copy_chunk(n, c):
                        u, h, k = UN[n]
                        nkt = ((10, 5)[k]) if full else 2
                        dst = (PTM, PTW)[k]
                        a0, a1 = c * 4, min(c * 4 + 4, nkt)
                        act.wait_ge(*s("tr", ch0 + chunk_count(n, full) + c + 1))
                        A(dst[:, a0:a1, :].rearrange("p a b -> p (a b)"), PS[:, 5, 0:(a1 - a0) * P], ACT.Copy).then_inc(s["pt"], 1)

                    expo(0)
                    for n in range(32):
                        u, h, k = UN[n]
                        copy_chunk(n, 0)
                        if n < 31:
                            expo(n + 1)
                        if full:
                            copy_chunk(n, 1 if k else 2)
                        if n == 16 or n == 31:
                            fu = 0 if n == 16 else 1
                            act.wait_ge(*s("es", p * 2 + fu + 1))
                            A(stat[:, 16:24], stat[:, 8:16], ACT.Exp).then_inc(s["tot"], 1)
                        if n == 18 or n == 31:
                            fu = 0 if n == 18 else 1
                            for kk in range(2):
                                act.wait_ge(*s("fT", (p * 2 + fu) * 2 + kk + 1))
                                dst = (obT, oaT)[kk]
                                A(dst[:, :, ds((t0 + fu) * P, P)], PS[:, 5, :].rearrange("p (a b) -> p a b", a=4), ACT.Copy).then_inc(s["fcp"], 1)
                pairs(act, l, pair)

                def merge_block(f, u):
                    for ci, (c0, cn) in enumerate(CH[l]):
                        q = f * NCH[l] + ci
                        set_ = (u * NCH[l] + ci) % 2
                        act.wait_ge(*s("g", q + 1))
                        if not isinstance(f, int) or q >= 2:
                            act.wait_ge(*s("mrg", q - 1))
                        A(sg[:, set_, 0, 0:cn], PS[:, set_ * 4 + 2, 0:cn], ACT.Sigmoid)
                        A(sg[:, set_, 1, 0:cn], PS[:, set_ * 4 + 3, 0:cn], ACT.Sigmoid).then_inc(s["sg"], 1)
                for u in range(2):
                    merge_block(u, u)
                with act.Fori(1, 4) as i:
                    for u in range(2):
                        merge_block(i * 2 + u, u)

                def ln_a(t):
                    n = t - TL[l][0]
                    act.wait_ge(*s("lnv", n + 1))
                    A(stat[:, 7:8], stat[:, 9:10], ACT.Sqrt, bias=epsc[:, 0:1]).then_inc(s["lnr"], 1)
                    act.wait_ge(*s("lnb", n + 1))
                    A(xn, zt, ACT.Identity, scale=stat[:, 10:11], bias=stat[:, 11:12]).then_inc(s["lnn"], 1)

                def tr_a(t):
                    n = t - TL[l][0]
                    v = kind(t)
                    act.wait_ge(*s("x1T", 2 * n + 1))
                    if not (isinstance(n, int) and n == 0):
                        act.wait_ge(*s("rt", n))
                    for k in range(4):
                        m = A(h2t[:, k, :], PS[:, 2, k * P:(k + 1) * P], ACT.Identity,
                              scale=modT[:, l, v, 4, k:k + 1], bias=modT[:, l, v, 3, k:k + 1])
                    m.then_inc(s["h2a"], 1)
                    act.wait_ge(*s("rt", n + 1))
                    A(logit[:, ds(t, 1), :].rearrange("p o e -> p (o e)"), PS[:, 4, 0:E], ACT.Copy).then_inc(s["rt_cp"], 1)
                ln_a(TL[l][0])
                if l == 0:
                    tr_a(0)
                    ln_a(1)
                    tr_a(1)
                    ln_a(2)
                with act.Fori(TC + 1, TT) as t:
                    tr_a(t - 1)
                    ln_a(t)
                tr_a(TT - 1)
                tl = TL[l][0]
                act.wait_ge(*s("sm_m", 1))
                A(afft[:, tl:TT, :], afft[:, tl:TT, :], ACT.Exp).then_inc(s["sm_e"], 1)
                act.wait_ge(*s("sel", 1))

                N = NN[l]

                def rows_a(e):
                    act.wait_ge(*s("xgT", 2 * e + 1))
                    if not (isinstance(e, int) and e == 0):
                        act.wait_ge(*s("au", e * 8))
                    for k in range(4):
                        m = A(xgT[:, k, 0:P], PS[:, 0, k * P:(k + 1) * P], ACT.Identity,
                              scale=modT[:, l, 0, 4, k:k + 1], bias=modT[:, l, 0, 3, k:k + 1])
                    if l == 0:
                        act.wait_ge(*s("xgT", 2 * e + 2))
                        for k in range(KD):
                            m = A(xgT[:, k, P:N], PS[:, 2, k * 32:(k + 1) * 32], ACT.Identity,
                                  scale=modT[:, l, 1, 4, k:k + 1], bias=modT[:, l, 1, 3, k:k + 1])
                    m.then_inc(s["xa"], 1)

                def expert(e, last):
                    for f in range(KD):
                        act.wait_ge(*s("au", e * 8 + f + 1))
                        if not (isinstance(e, int) and e == 0 and f < 2):
                            act.wait_ge(*s("act", e * 8 + f - 1))
                        A(silb[:, f % 2, 0:N], PS[:, 3 + f % 2, 0:N], ACT.Silu).then_inc(s["sil"], 1)
                    for d in range(0, KD, 2):
                        act.wait_ge(*s("yt", e * 8 + d + 1))
                        if d == 0 and not (isinstance(e, int) and e == 0):
                            act.wait_ge(*s("bk", 2 * e))
                        A(yT[:, d, 0:N], PS[:, 5, 0:N], ACT.Copy).then_inc(s["yc_a"], 1)
                    if not last:
                        rows_a(e + 1)
                rows_a(0)
                with_first(act, expert)

                def norm_pair(i):
                    for u in range(2):
                        n = i * 2 + u
                        act.wait_ge(*s("st2", n + 1))
                        A(stat[:, 24 + u:25 + u], stat[:, 27 + 2 * u:28 + 2 * u], ACT.Sqrt, bias=epsc[:, 0:1]).then_inc(s["sq2"], 1)
                        act.wait_ge(*s("rs2", n + 1))
                        if u == 0 and not isinstance(i, int):
                            act.wait_ge(*s("out_st", i * 32))
                        A(o2[:, u, :], z2[:, u, :], ACT.Identity, scale=stat[:, 12 + 2 * u:13 + 2 * u], bias=stat[:, 13 + 2 * u:14 + 2 * u]).then_inc(s["n2"], 1)

                    for u in range(2):
                        n = i * 2 + u
                        act.wait_ge(*s("g2", n + 1))
                        dst = xs_d[ds(n * P, P), :] if l < DEPTH - 1 else out[0, ds(n * P, P), :]
                        act.dma_start(dst, o2[:, u, :]).then_inc(s["out_st"], 16)
                peeled(act, NPAIR[l], norm_pair)
            act.wait_ge(*L[DEPTH - 1]("out_st", 16 * NT[DEPTH - 1]))

        @block.vector
        def _(dve):
            def TTR(o, x, y, op):
                return dve.tensor_tensor(o, x, y, op)

            dve.memset(ones1, 1.0).then_inc(G["silc"], 1)
            dve.memset(epsc[:, 0:1], LN_EPS)
            dve.memset(epsc[:, 1:2], RMS_EPS).then_inc(G["bars"], 1)
            dve.wait_ge(G["const_in"], 16 * 7)
            for l in range(DEPTH):
                dve.tensor_scalar(sinks[:, l, 1, :], sinks[:, l, 0, :], -1.0, None, ALU.mult).then_inc(G["bars"], 1)

            def row(i):
                for u in range(2):
                    dve.wait_ge(G["ada"], i * 2 + u + 1)
                    if not isinstance(i, int):
                        dve.wait_ge(G["mod_st"], i * 32)
                    dve.tensor_copy(adar[0:2, u, :], PS[0:2, u, :]).then_inc(G["rowc"], 1)
            peeled(dve, 12, row)
            dve.wait_ge(G["modT_cp"], 1)
            for l in range(DEPTH):
                for v in range(2):
                    for part in (1, 4):
                        m = dve.tensor_scalar(modT[:, l, v, part, :], modT[:, l, v, part, :], 1.0, None, ALU.add)
            m.then_inc(G["mod1"], 1)

            def rope(dst, src, table, h, half, tmp):
                w = 4 * half
                C = table[:, 0:w]
                S = table[:, w:2 * w]
                x = src.rearrange("p h (a s n) -> p h a s n", a=2, s=2)
                t = tmp.rearrange("p h (a s n) -> p h a s n", a=2, s=2)
                Sv = S.rearrange("p (a s n) -> p a s n", a=2, s=2)
                TTR(dst, src, C.unsqueeze(1).to_broadcast([P, h, w]), ALU.mult)
                for i in range(2):
                    if h == 1:
                        TTR(t[:, 0, :, i, :], x[:, 0, :, 1 - i, :], Sv[:, :, i, :], ALU.mult)
                    else:
                        TTR(t[:, :, :, i, :], x[:, :, :, 1 - i, :], Sv[:, :, i, :].unsqueeze(1).to_broadcast([P, h, 2, half]), ALU.mult)
                dve.drain()
                return TTR(dst, dst, tmp, ALU.add)

            for l in range(DEPTH):
                s = L[l]
                if l:
                    dve.wait_ge(*L[l - 1]("sc", 16 * E * 2))
                if l:
                    dve.wait_ge(*L[l - 1]("g2", NT[l - 1]))
                dve.memset(kaZ.rearrange("p a b -> p (a b)"), 0.0)
                dve.memset(va[:, TT, :], 0.0)
                dve.drain()

                def h_half(t):
                    v = kind(t)
                    dve.wait_ge(*s("xT", 2 * t + 2))
                    if not (isinstance(t, int) and t == 0):
                        dve.wait_ge(*s("h_st", 16 * t))
                        dve.wait_ge(*s("p0", t))
                    for k in range(4):
                        m = dve.tensor_scalar(hts[:, 4 + k, :], PS[:, 5, k * P:(k + 1) * P], modT[:, l, v, 1, 4 + k:5 + k],
                                              modT[:, l, v, 0, 4 + k:5 + k], ALU.mult, ALU.add)
                    m.then_inc(s["h_d"], 1)
                h_half(0)
                dve.wait_ge(*s("wp_in", 16 * 14))

                def step(t, n, last):
                    tab = tabs[:, ds(t, 1), :].rearrange("p o n -> p (o n)")
                    dve.wait_ge(*s("rms", t + 1))
                    dve.reciprocal(stat[:, 4:6], stat[:, 2:4]).then_inc(s["rstd"], 1)
                    dve.wait_ge(*s("latT", t + 1))
                    for k in range(3):
                        m = dve.tensor_scalar(latTt[:, 2 + k, :], PS[:, 3, k * P:(k + 1) * P], gcol[:, l, 2 + k:3 + k], None, ALU.mult)
                    m.then_inc(s["latc_d"], 1)
                    if not last:
                        h_half(t + 1)
                    dve.wait_ge(*s("p0", t + 1))
                    if not (isinstance(t, int) and t == 0):
                        dve.wait_ge(*s("tW", t))
                    dve.tensor_copy(va[:, ds(t, 1), :].rearrange("p o n -> p (o n)"), PS[:, 1, P:2 * P])
                    src = PS[:, 0:2, :].rearrange("p b n -> p (b n)")[:, 0:640].rearrange("p (h c) -> p h c", c=WD)
                    rope(rW, src, tab[:, 0:128], 10, 16, rC).then_inc(s["ropeW"], 1)
                    rope(krr.unsqueeze(1), PS[:, 2, QR:QR + ROPE].unsqueeze(1), tab[:, 128:192], 1, 8, krt.unsqueeze(1)).then_inc(s["used_d"], 1)
                    dve.drain()
                    if not (isinstance(t, int) and t == 0):
                        dve.wait_ge(*s("tK", 2 * t))
                    dve.tensor_copy(ksb[:, :, NOPE:], krr.unsqueeze(1).to_broadcast([P, MH, ROPE])).then_inc(s["kr"], 1)
                    if not (isinstance(t, int) and t == 0):
                        dve.wait_ge(*s("tQ", 2 * t))
                    for g in range(2):
                        dve.wait_ge(*s("uq", 2 * t + g + 1))
                        src = PS[:, 3 + g, 0:384].rearrange("p (h c) -> p h c", h=4)
                        dve.tensor_copy(qsb[:, g * 4:(g + 1) * 4, 0:NOPE], src[:, :, 0:NOPE])
                        m = rope(qsb[:, g * 4:(g + 1) * 4, NOPE:], src[:, :, NOPE:], tab[:, 128:192], 4, 8, tmpm)
                        dve.drain() if g == 0 else None
                    m.then_inc(s["qro"], 1)
                    dve.wait_ge(*s("tW", t + 1))
                    for g in range(2):
                        m = dve.tensor_copy(kaZ[g * 64:(g + 1) * 64, g, ds(t * P, P)], PS[g * 64:(g + 1) * 64, 1, 0:P])
                    m.then_inc(s["ka_cp"], 1)
                    if not (isinstance(t, int) and t == 0):
                        dve.wait_ge(*s("qM_st", 16 * t))
                    for g in range(2):
                        dve.wait_ge(*s("tQ", 2 * t + g + 1))
                        dve.tensor_copy(qMs[0:MQ, g * 4:(g + 1) * 4, :].rearrange("p a b -> p (a b)"), PS[0:MQ, 3 + g, :]).then_inc(s["qM_cp"], 1)
                tiles(dve, step)

                dve.wait_ge(*s("m_in", 32))

                def pair(p, t0, lp):
                    full = lp is not None
                    ch0 = chunks_before(l, p, lp)

                    def stats(n):
                        u, h, k = UN[n]
                        cnt = p * 16 + n // 2
                        if k == 0:
                            nk = 1280 if full else 256
                            dve.wait_ge(*s("sM", cnt + 1))
                            src = PS[:, 0:3, :].rearrange("p b n -> p (b n)")[:, 0:nk]
                            dve.tensor_reduce(stat[:, 31:32], src, AX.X, ALU.max, negate=True)
                            dve.drain()
                            dve.tensor_scalar(stat[:, 32 + u * 8 + h:33 + u * 8 + h], stat[:, 31:32], MSCALE, None, ALU.mult).then_inc(s["mxM"], 1)
                        else:
                            nk = 640 if full else 256
                            dve.wait_ge(*s("sW", cnt + 1))
                            dve.wait_ge(*s(f"q_in{u}", p * 48 + 48))
                            if n >= 2 or not (isinstance(p, int) and p == 0):
                                dve.wait_ge(*s("tr", ch0 + chunk_count(n - 1, full) if n >= 2 else ch0))
                            src = PS[:, 3:5, :].rearrange("p b n -> p (b n)")[:, 0:nk]
                            dve.nop(nofuse=True)
                            dve.tensor_tensor_reduce(out=PW[:, 0:nk], in0=src, in1=mask[:, u, 0:nk], scale=WSCALE, scalar=-3.0e38,
                                                     op0=ALU.add, op1=ALU.max, accum_out=stat[:, 30:31])
                            dve.drain()
                            dve.tensor_scalar(stat[:, 48 + u * 8 + h:49 + u * 8 + h], stat[:, 30:31], -1.0, sinks[:, l, 1, h:h + 1], ALU.mult, ALU.min).then_inc(s["mxW"], 1)

                    def copy_chunk(n, c):
                        dve.wait_ge(*s("tr", ch0 + chunk_count(n, full) + c + 1))
                        dve.tensor_copy(PTM[:, 4:8, :].rearrange("p a b -> p (a b)"), PS[:, 5, :]).then_inc(s["pt"], 1)

                    def finish(u):
                        dve.wait_ge(*s("pW", p * 16 + 8 * u + 8))
                        TTR(stat[:, 8:16], stat[:, 48 + u * 8:56 + u * 8], sinks[:, l, 0, :], ALU.add).then_inc(s["es"], 1)
                        dve.wait_ge(*s("tot", p * 2 + u + 1))
                        TTR(stat[:, 80 + u * 8:88 + u * 8], stat[:, 80 + u * 8:88 + u * 8], stat[:, 16:24], ALU.add)
                        dve.drain()
                        dve.reciprocal(stat[:, 80 + u * 8:88 + u * 8], stat[:, 80 + u * 8:88 + u * 8])
                        dve.reciprocal(stat[:, 64 + u * 8:72 + u * 8], stat[:, 64 + u * 8:72 + u * 8])
                        dve.drain()
                        dve.wait_ge(*s("pv", p * 32 + 16 * u + 16))
                        if u or not (isinstance(p, int) and p == 0):
                            dve.wait_ge(*s("fT", (p * 2 + u) * 2))
                        for kk, c in ((0, 64), (1, 80)):
                            r = stat[:, c + u * 8:c + 8 + u * 8].unsqueeze(2).to_broadcast([P, 8, 64])
                            TTR(osb[:, kk, :].rearrange("p (h d) -> p h d", h=8), PS[:, 6 + kk, :].rearrange("p (h d) -> p h d", h=8), r, ALU.mult).then_inc(s["osb"], 1)

                    stats(0)
                    for n in range(32):
                        if n < 31:
                            stats(n + 1)
                        if full and UN[n][2] == 0:
                            copy_chunk(n, 1)
                        if n == 16:
                            finish(0)
                    finish(1)
                pairs(dve, l, pair)

                def merge_block(f, u):
                    for ci, (c0, cn) in enumerate(CH[l]):
                        q = f * NCH[l] + ci
                        set_ = (u * NCH[l] + ci) % 2
                        dve.wait_ge(*s("sg", q + 1))
                        for j in range(2):
                            TTR(sg[:, set_, j, 0:cn], sg[:, set_, j, 0:cn], PS[:, set_ * 4 + j, 0:cn], ALU.mult)
                        dve.drain()
                        TTR(mrgT[:, ds(f, 1), c0:c0 + cn].rearrange("p o n -> p (o n)"), sg[:, set_, 0, 0:cn], sg[:, set_, 1, 0:cn], ALU.add).then_inc(s["mrg"], 1)
                for u in range(2):
                    merge_block(u, u)
                with dve.Fori(1, 4) as i:
                    for u in range(2):
                        merge_block(i * 2 + u, u)

                dve.wait_ge(*s("lnc_in", 16 * 5))

                def ln_d(t):
                    n = t - TL[l][0]
                    v = kind(t)
                    dve.wait_ge(*s("y", n + 1))
                    TTR(zt, PS[:, 0:2, :].rearrange("p b n -> p (b n)"), m2b[:, v, :], ALU.mult).then_inc(s["y_used"], 1)
                    dve.drain()
                    dve.wait_ge(*s("xr_in", (n + 1) * 16))
                    dve.scalar_tensor_tensor(out=zt, in0=xr, scalar=ALPHA, in1=zt, op0=ALU.mult, op1=ALU.add).then_inc(s["zs"], 1)
                    dve.drain()
                    for h in range(2):
                        dve.bn_stats(stat[:, 12 + 6 * h:18 + 6 * h], zt[:, h * 512:(h + 1) * 512])
                    dve.drain()
                    dve.bn_aggr(stat[:, 8:10], stat[:, 12:24]).then_inc(s["lnv"], 1)
                    dve.wait_ge(*s("lnr", n + 1))
                    dve.reciprocal(stat[:, 10:11], stat[:, 7:8])
                    dve.drain()
                    dve.tensor_scalar(stat[:, 11:12], stat[:, 8:9], stat[:, 10:11], -1.0, ALU.mult, ALU.mult).then_inc(s["lnb"], 1)
                    dve.wait_ge(*s("lnn", n + 1))
                    TTR(xn, xn, gb1[:, 0, :], ALU.mult)
                    dve.drain()
                    if not (isinstance(n, int) and n == 0):
                        dve.wait_ge(*s("x1T", 2 * n))
                        dve.wait_ge(*s("x1_st", 16 * n))
                        dve.wait_ge(*s("z_set", n))
                    TTR(x1t, xn, gb1[:, 1, :], ALU.add).then_inc(s["x1"], 1)

                def tr_d(t):
                    n = t - TL[l][0]
                    v = kind(t)
                    dve.wait_ge(*s("x1T", 2 * n + 2))
                    if not (isinstance(n, int) and n == 0):
                        dve.wait_ge(*s("rt", n))
                    for k in range(4):
                        m = dve.tensor_scalar(h2t[:, 4 + k, :], PS[:, 3, k * P:(k + 1) * P], modT[:, l, v, 4, 4 + k:5 + k],
                                              modT[:, l, v, 3, 4 + k:5 + k], ALU.mult, ALU.add)
                    m.then_inc(s["h2d"], 1)
                ln_d(TL[l][0])
                if l == 0:
                    tr_d(0)
                    ln_d(1)
                    tr_d(1)
                    ln_d(2)
                with dve.Fori(TC + 1, TT) as t:
                    tr_d(t - 1)
                    ln_d(t)
                tr_d(TT - 1)

                tl = TL[l][0]
                nt = NT[l]
                dve.wait_ge(*s("rt_cp", nt))
                lg = logit[:, tl:TT, :]
                av = afft[:, tl:TT, :]
                dve.tensor_reduce(stat[:, 32:32 + nt], lg, AX.X, ALU.max)
                dve.drain()
                TTR(av, lg, stat[:, 32:32 + nt].unsqueeze(2).to_broadcast([P, nt, E]), ALU.subtract).then_inc(s["sm_m"], 1)
                dve.wait_ge(*s("sm_e", 1))
                dve.tensor_reduce(stat[:, 32:32 + nt], av, AX.X, ALU.add)
                dve.drain()
                dve.reciprocal(stat[:, 32:32 + nt], stat[:, 32:32 + nt])
                dve.drain()
                TTR(av, av, stat[:, 32:32 + nt].unsqueeze(2).to_broadcast([P, nt, E]), ALU.mult).then_inc(s["aff"], 1)
                dve.wait_ge(*s("affT", 1))
                dve.tensor_copy(affT[0:E, tl * P:TOK], PS[0:E, 5:8, :].rearrange("p b n -> p (b n)")[:, tl * P:TOK])
                dve.drain()
                for src0, vv, ii, ff, cap, base in (
                        [(CTX, vals, idx8, idxf, CAP_L, CTX)] + ([(0, valc, idc8, idcf, CAP_C, 0)] if l == 0 else [])):
                    n = SEQ if src0 else CTX
                    cur = affT[0:E, src0:src0 + n]
                    for r in range(cap // 8):
                        o8 = vv[0:E, r * 8:(r + 1) * 8]
                        dve.max(o8, cur)
                        dve.drain()
                        dve.max_index(ii[0:E, r * 8:(r + 1) * 8], o8, cur)
                        if r < cap // 8 - 1:
                            nx = wk[0:E, 0:n]
                            dve.drain()
                            dve.match_replace(nx, o8, cur, -1.0)
                            dve.drain()
                            cur = nx
                    dve.drain()
                    dve.tensor_scalar(ff[0:E, :], ii[0:E, :], float(base), None, ALU.add)
                    dve.drain()
                dve.drain().then_inc(s["topk"], 1)
                dve.wait_ge(*s("sel", 1))
                dve.tensor_copy(idxT[:, 0, :], PS[:, 0, 0:E])
                m = dve.tensor_copy(affS[:, 0, :], PS[:, 0, E:2 * E])
                if l == 0:
                    dve.tensor_copy(idxT[0:CAP_C, 1, :], PS[0:CAP_C, 0, 2 * E:3 * E])
                    m = dve.tensor_copy(affS[0:CAP_C, 1, :], PS[0:CAP_C, 0, 3 * E:4 * E])
                m.then_inc(s["sel_cp"], 1)
                dve.wait_ge(*s("m5_in", 32))
                dve.drain()

                N = NN[l]

                def stage(e, j, sem):
                    m = dve.tensor_copy(icur[:, j:j + 1], idxT[:, 0, ds(e, 1)])
                    if l == 0:
                        m = dve.tensor_copy(icur[0:CAP_C, j + 1:j + 2], idxT[0:CAP_C, 1, ds(e, 1)])
                    m.then_inc(s[sem], 1)

                def rows_d(e):
                    dve.wait_ge(*s("xgT", 2 * e + 2))
                    if not (isinstance(e, int) and e == 0):
                        dve.wait_ge(*s("au", e * 8))
                    for k in range(4, 8):
                        m = dve.tensor_scalar(xgT[:, k, 0:P], PS[:, 1, (k - 4) * P:(k - 3) * P], modT[:, l, 0, 4, k:k + 1],
                                              modT[:, l, 0, 3, k:k + 1], ALU.mult, ALU.add)
                    m.then_inc(s["xd"], 1)

                def expert(e, last):
                    if not last:
                        dve.wait_ge(*s("gat", (e + 1) * 16 * (2 - l)))
                        stage(e + 1, 0, "stage_g")
                    for f in range(KD):
                        dve.wait_ge(*s("sil", e * 8 + f + 1))
                        TTR(actT[:, f, 0:N], silb[:, f % 2, 0:N], PS[:, 3 + f % 2, N:2 * N], ALU.mult).then_inc(s["act"], 1)
                    for d in range(1, KD, 2):
                        dve.wait_ge(*s("yt", e * 8 + d + 1))
                        if d == 1 and not (isinstance(e, int) and e == 0):
                            dve.wait_ge(*s("bk", 2 * e))
                        dve.tensor_copy(yT[:, d, 0:N], PS[:, 6, 0:N]).then_inc(s["yc_d"], 1)
                    if not (isinstance(e, int) and e == 0):
                        dve.wait_ge(*s("sc", e * 16 * (2 - l)))
                    stage(e, 2, "stage_s")
                    for r in range(2):
                        dve.wait_ge(*s("bk", 2 * e + r + 1))
                        dve.scalar_tensor_tensor(out=Y[:, r * 512:(r + 1) * 512], in0=PS[:, (7, 0)[r], :], scalar=affS[:, 0, ds(e, 1)],
                                                 in1=m5b[:, 0, r * 512:(r + 1) * 512], op0=ALU.mult, op1=ALU.mult).then_inc(s["ylat"], 1)
                        if l == 0:
                            dve.scalar_tensor_tensor(out=Yc[0:CAP_C, r * 512:(r + 1) * 512], in0=PS[0:CAP_C, 1 + r, :],
                                                     scalar=affS[0:CAP_C, 1, ds(e, 1)], in1=m5b[0:CAP_C, 1, r * 512:(r + 1) * 512],
                                                     op0=ALU.mult, op1=ALU.mult).then_inc(s["yctx"], 1)
                    if not last:
                        rows_d(e + 1)
                stage(0, 0, "stage_g")
                rows_d(0)
                with_first(dve, expert)

                dve.wait_ge(*s("gb2_in", 32))
                with dve.Fori(0, NPAIR[l]) as i:
                    for u in range(2):
                        n = i * 2 + u
                        dve.wait_ge(*s(f"z_in{u}", (i + 1) * 16))
                        for h in range(2):
                            dve.bn_stats(stat[:, 32 + 6 * h:38 + 6 * h], z2[:, u, h * 512:(h + 1) * 512])
                        dve.drain()
                        dve.bn_aggr(stat[:, 26 + 2 * u:28 + 2 * u], stat[:, 32:44]).then_inc(s["st2"], 1)
                        dve.wait_ge(*s("sq2", n + 1))
                        dve.reciprocal(stat[:, 12 + 2 * u:13 + 2 * u], stat[:, 24 + u:25 + u])
                        dve.drain()
                        dve.tensor_scalar(stat[:, 13 + 2 * u:14 + 2 * u], stat[:, 26 + 2 * u:27 + 2 * u], stat[:, 12 + 2 * u:13 + 2 * u], -1.0,
                                          ALU.mult, ALU.mult).then_inc(s["rs2"], 1)
                    for u in range(2):
                        n = i * 2 + u
                        dve.wait_ge(*s("n2", n + 1))
                        TTR(o2[:, u, :], o2[:, u, :], gb2[:, 0, :], ALU.mult)
                        dve.drain()
                        TTR(o2[:, u, :], o2[:, u, :], gb2[:, 1, :], ALU.add).then_inc(s["g2"], 1)

        @block.gpsimd
        def _(pool):
            for l in range(DEPTH):
                with pool.Fori(0, 6) as i:
                    for u in range(2):
                        j = l * 12 + i * 2 + u
                        pool.wait_ge(G["rowc"], j + 1)
                        dst = mod_d[l].rearrange("(v k) p -> v (k p)", v=2)[:, ds((i * 2 + u) * 512, 512)]
                        pool.dma_start(dst, adar[0:2, u, :]).then_inc(G["mod_st"], 16)
            for l in range(DEPTH):
                s = L[l]
                pool.wait_ge(*s("mrg", 8 * NCH[l]))
                tl = TL[l][0]

                def take(t):
                    n = t - tl
                    if not (isinstance(n, int) and n == 0):
                        pool.wait_ge(*s("y", n))
                    pool.tensor_copy(mst, mrgT[:, :, ds(t * P, P)]).then_inc(s["mst"], 1)

                def scale_x(t):
                    n = t - tl
                    pool.wait_ge(*s("x1", n + 1))
                    if not (isinstance(n, int) and n == 0):
                        pool.wait_ge(*s("z_st", 16 * n))
                    pool.nop(nofuse=True)
                    pool.tensor_scalar(zs, x1t, ALPHA, None, ALU.mult).then_inc(s["z_set"], 1)
                take(tl)
                if l == 0:
                    take(1)
                    scale_x(0)
                    take(2)
                    scale_x(1)
                with pool.Fori(TC + 1, TT) as t:
                    take(t)
                    scale_x(t - 1)
                scale_x(TT - 1)

                pool.wait_ge(*s("x1_st", 16 * NT[l]))
                pool.wait_ge(*s("z_st", 16 * NT[l]))
                pool.wait_ge(*s("y", NT[l]))

                def gather(e):
                    pool.wait_ge(*s("stage_g", e + 1))
                    if not (isinstance(e, int) and e == 0):
                        pool.wait_ge(*s("xgT", 2 * e))
                    pool.nop(nofuse=True)
                    pool.indirect_dma_start(out=xg, out_offset=None, in_=x1_d,
                                            in_offset=bass.IndirectOffsetOnAxis(ap=icur[:, 0:1], axis=0)).then_inc(s["gat"], 16)
                    if l == 0:
                        pool.nop(nofuse=True)
                        pool.indirect_dma_start(out=xgc[0:CAP_C, :], out_offset=None, in_=x1_d,
                                                in_offset=bass.IndirectOffsetOnAxis(ap=icur[0:CAP_C, 1:2], axis=0)).then_inc(s["gat"], 16)

                def expert(e, last):
                    if not last:
                        gather(e + 1)
                    pool.wait_ge(*s("stage_s", e + 1))
                    pool.wait_ge(*s("ylat", 2 * e + 2))
                    if not (isinstance(e, int) and e == 0):
                        pool.wait_ge(*s("sc", e * 16 * (2 - l)))
                    pool.nop(nofuse=True)
                    pool.indirect_dma_start(out=z_d, out_offset=bass.IndirectOffsetOnAxis(ap=icur[:, 2:3], axis=0), in_=Y,
                                            in_offset=None, compute_op=ALU.add).then_inc(s["sc"], 16)
                    if l == 0:
                        pool.wait_ge(*s("yctx", 2 * e + 2))
                        pool.nop(nofuse=True)
                        pool.indirect_dma_start(out=z_d, out_offset=bass.IndirectOffsetOnAxis(ap=icur[0:CAP_C, 3:4], axis=0),
                                                in_=Yc[0:CAP_C, :], in_offset=None, compute_op=ALU.add).then_inc(s["sc"], 16)
                gather(0)
                with_first(pool, expert)


_INS = ["x", "c", "ctx", "c_ctx", "w_ada", "b_ada", "w_in", "attn_sink", "mla_q_norm", "mla_kv_norm", "w_uq", "w_ukv",
        "w_oa", "w_ob", "w_out", "ln1_g", "ln1_b", "w_router", "w_exp_gate", "w_exp_up", "w_exp_down", "ln2_g", "ln2_b"]


def _tables():
    n = np.arange(SEQ)
    pos = np.stack([n // GRID_W, n % GRID_W], 1).astype(np.float32)
    cols = []
    for dim in (WD, ROPE):
        nf = dim // 4
        inv = np.power(np.float32(THETA), -np.arange(nf, dtype=np.float32) / np.float32(nf)).astype(np.float32)
        ang = pos[:, :, None] * inv
        c, s = np.cos(ang), np.sin(ang)
        cols.append(np.stack([c, c], 2).reshape(SEQ, dim))
        cols.append(np.stack([-s, s], 2).reshape(SEQ, dim))
    lat = np.concatenate(cols, 1)
    still = np.concatenate([np.ones((CTX, WD)), np.zeros((CTX, WD)), np.ones((CTX, ROPE)), np.zeros((CTX, ROPE))], 1)
    rope = np.concatenate([still, lat], 0).astype(np.float32)
    i, j = np.arange(P)[:, None], np.arange(P)[None, :]
    off = NEG / WSCALE
    prev = np.where(j >= i, 0.0, off)
    nxt = np.where(j <= i, 0.0, off)
    z = np.zeros((P, P))
    mask = np.concatenate([z, z, prev, z, nxt], 1).astype(np.float32)
    full = np.full((P, P), off)
    edge = np.stack([np.stack([full, prev, prev, prev]), np.stack([nxt, nxt, nxt, full])]).astype(np.float32)
    return {"ident": np.eye(P, dtype=np.float32), "rope": rope, "wmask": mask, "edge": edge}


def kernel(**inputs):
    import numpy as _np
    import concourse.bacc as _bacc
    from concourse import mybir as _mybir
    from concourse.bass_utils import run_bass_kernel_spmd as _run

    nc = _bacc.Bacc("TRN2", target_bir_lowering=False, num_devices=1)
    arrays, args = {}, {}
    everything = {n: _np.ascontiguousarray(inputs[n]) for n in _INS}
    everything.update(_tables())
    for name, v in everything.items():
        arrays[f"in_{name}"] = v
        args[name] = nc.dram_tensor(f"in_{name}", v.shape, _mybir.dt.from_np(v.dtype), kind="ExternalInput").ap()
    out = nc.dram_tensor("out_0", (1, SEQ, D), F32, kind="ExternalOutput").ap()
    build(nc, args, out)
    r = _run(nc, [arrays], core_ids=[0])
    return r.results[0]["out_0"]
```

```python
from contextlib import ExitStack

import concourse.bass as bass
import numpy as np
from concourse import mybir

F32 = mybir.dt.float32
U32 = mybir.dt.uint32
ALU = mybir.AluOpType
ACT = mybir.ActivationFunctionType
AX = mybir.AxisListType

P = 128
D = 1024
KD = D // P
CTX, SEQ = 256, 1024
TOK = CTX + SEQ
TC, TT = CTX // P, TOK // P
DEPTH = 2
GRID_W = 64
WH, WKV, WD = 8, 2, 64
MH, NOPE, ROPE, MV = 8, 64, 32, 64
QR, KVR = 384, 256
MQ = NOPE + ROPE
E, FF = 16, 1024
CAP_L, CAP_C = 2 * SEQ // E, 2 * CTX // E
THETA = 10000.0
LN_EPS, RMS_EPS, NEG = 1e-5, 1e-6, -1e30
ALPHA = float((2 * DEPTH) ** 0.25)
WSCALE = float(WD ** -0.5)
MSCALE = float(MQ ** -0.5)
C_KA, C_CKV, C_KR, C_QA, C_CQ, C_G = 0, 256, 512, 544, 1056, 1440
NPJ = C_G


def ds(i, n):
    return slice(i, i + n) if isinstance(i, int) else bass.ds(i, n)


class Sems:

    def __init__(self, sems, before=None):
        self.sems, self.before = sems, before or {}

    def __getitem__(self, name):
        return self.sems[name]

    def __call__(self, name, n):
        return self.sems[name], n + self.before.get(name, 0)


def layer_counts(tiles, chunks, tr, ctx):
    pairs, g = tiles // 2, 1 + ctx
    n = dict(wp_in=14 * 16, q_in0=pairs * 48, q_in1=pairs * 48, m_in=32, tr=tr, pt=tr, pv=pairs * 32, hT_in0=16, hT_in1=16, hT_in2=16, mw_in0=KD * 32, mw_in1=KD * 32,
             wo_in=16, lnc_in=5 * 16, m5_in=32, z_in0=16 * tiles, z_in1=0, gb2_in=32, out_st=16 * tiles)
    n |= {f"ring{i}": 16 * E * (2 if i < 4 else 1) for i in range(8)}
    n |= {k: 16 * TT for k in "x_in h_st qW_st qM_st".split()}
    n |= {k: TT for k in "h_a h_d p1 p2 p0 rms rstd norm latT latc_a latc_d used_d ropeW kr kn qro tW qW_cp ka_cp".split()}
    n |= {k: 2 * TT for k in "xT ukv uq tK tQ kT_cp qM_cp".split()}
    n |= {k: 16 * pairs for k in "sM sW mxM mxW pM pW".split()}
    n |= {k: KD * chunks for k in "g sg mrg".split()}
    n |= {k: 16 * tiles for k in "xr_in x1_st z_st".split()}
    n |= {k: tiles for k in "es tot mst y y_used lnv lnr lnb lnn x1 h2a h2d zs z_set rt rt_cp st2 sq2 rs2 n2 g2".split()}
    n |= {k: 2 * tiles for k in "osb fT fcp x1T".split()}
    n |= {k: 1 for k in "sm_m sm_e aff affT topk sel sel_cp".split()}
    n |= {k: E for k in "stage_g stage_s xa xd".split()}
    n |= {k: 16 * E * g for k in "gat sc".split()}
    n |= {k: 8 * E for k in "au sil act yt".split()}
    n |= {k: 4 * E for k in "yc_a yc_d".split()}
    n |= {k: 2 * E for k in "xgT bk ylat".split()}
    n["yctx"] = 2 * E * ctx
    return n


def build(nc, a, out):
    with ExitStack() as ctx:
        def dram(name, shape):
            return nc.dram_tensor(name, shape, F32, kind="Internal").ap()

        mod_d = dram("mod_rows", (DEPTH, 96, P))
        hT_d = dram("h_transposed", (P, KD, TOK))
        qM_d = dram("q_latent_attn", (TT, MQ, MH * P))
        qW_d = dram("q_window", (TT, P, 4 * P))
        x1_d = dram("x_mid", (TOK, D))
        z_d = dram("moe_sum", (TOK, D))
        xs_d = dram("x_next", (TOK, D))

        WORDS = 53200
        arena = ctx.enter_context(nc.sbuf_tensor("arena", [P, WORDS], F32))
        PS = ctx.enter_context(nc.psum_tensor("PS", [P, 8, 512], F32))

        def at(off, *dims):
            n = int(np.prod(dims))
            assert off + n <= WORDS, (off, dims)
            v = arena[:, off:off + n]
            if len(dims) == 1:
                return v
            names = "abcd"[:len(dims)]
            return v.rearrange(f"p ({' '.join(names)}) -> p {' '.join(names)}", **{c: d for c, d in zip(names, dims)})

        ident = at(0, P)
        modT = at(128, DEPTH, 2, 6, KD)
        silc = at(320, 2, KD)
        gcol = at(336, DEPTH, 5)
        epsc = at(346, 2)
        sinks = at(352, DEPTH, 2, WH)
        stat = at(384, 96)
        ones1 = at(480, 2)
        R = 512
        RING, SLOT = 12, KD * 256
        O = R + RING * SLOT
        adaw = at(O, 2, KD, 512)
        adab = at(O + 8192, 2, 512)
        adar = at(O + 9216, 2, 512)
        crow = at(O + 18900, P)
        mrow = at(O + 18600, DEPTH, P)
        w_pj = at(R, KD, NPJ)
        w_uq = at(R + 11520, 3, MH * MQ)
        w_ukv = at(R + 13824, 2, MH * (NOPE + MV))
        hts = at(R + 15872, KD, P)
        xb = at(R + 16896, D)
        rW = at(R + 17920, 10, WD)
        rC = at(R + 18560, 10, WD)
        latn = at(R + 19200, KVR + QR)
        latTt = at(R + 19840, 5, P)
        ksb = at(R + 20480, MH, MQ)
        qsb = at(R + 21248, MH, MQ)
        qWs = at(R + 22016, 4, P)
        qMs = at(R + 22528, MH, P)
        tmpm = at(R + 23552, 4, ROPE)
        junk = at(R + 23680, QR)
        krr = at(R + 24064, ROPE)
        krt = at(R + 24096, ROPE)
        kT = at(O, MH, TOK)
        V = at(O + 10240, TT, MH * MV)
        kaZ = at(O + 15360, WKV, TOK + P)
        va = at(O + 18176, TT + 1, WKV * WD)
        tabs = at(O + 25728, TT, 192)
        oaT = at(R, 4, TOK)
        obT = at(R + 5120, 4, TOK)
        PM = at(R + 10240, 1280)
        PW = at(R + 11520, 640)
        PTM = at(R + 12160, 10, P)
        PTW = at(R + 13440, 5, P)
        qMt = at(R + 15360, 2, MH, P)
        qWt = at(R + 17408, 2, 4, P)
        mask = at(R + 18432, 2, 640)
        osb = at(R + 19712, 2, 512)
        hTr = at(O, KD, TOK)
        mrgT = at(O + 10240, KD, TOK)
        mwt = at(O + 20480, 2, 24, P)
        sg = at(R + 10240, 2, 2, 512)
        w_o = at(R + 14336, KD, D)
        xr = at(O, D)
        zt = at(O + 1024, D)
        xn = at(O + 2048, D)
        x1t = at(O + 3072, D)
        mst = at(O + 4096, KD, P)
        h2t = at(O + 5120, KD, P)
        zs = at(O + 6144, D)
        gb1 = at(O + 7168, 2, D)
        m2b = at(O + 20480, 2, D)
        wrt = at(O + 22528, KD, E)
        logit = at(O + 22656, TT, E)
        afft = at(O + 22816, TT, E)
        affT = at(O + 23040, TOK)
        wk = at(O + 24320, SEQ)
        vals = at(O + 25344, CAP_L)
        idx8 = at(O + 25472, CAP_L).bitcast(U32)
        idxf = at(O + 25600, CAP_L)
        valc = at(O + 25728, CAP_C)
        idc8 = at(O + 25760, CAP_C).bitcast(U32)
        idcf = at(O + 25792, CAP_C)
        idxT = at(O + 25824, 2, E).bitcast(U32)
        affS = at(O + 25856, 2, E)
        icur = at(O + 25888, 4).bitcast(U32)
        xg = at(O + 10240, D)
        xgc = at(O + 11264, D)
        xgT = at(O + 12288, KD, 160)
        actT = at(O + 13568, KD, 160)
        yT = at(O + 14848, KD, 160)
        Y = at(O + 16128, D)
        Yc = at(O + 17152, D)
        silb = at(O + 18176, 2, 160)
        m5b = at(O + 26000, 2, D)
        ring = at(R, RING, KD, 256)
        z2 = at(O + 19584, 2, D)
        o2 = at(O + 21632, 2, D)
        gb2 = at(O + 23680, 2, D)

        TL = [list(range(TT)), list(range(TC, TT))]
        NT = [len(t) for t in TL]
        NPAIR = [n // 2 for n in NT]
        CH = [[(0, 256), (256, 512), (768, 512)], [(256, 512), (768, 512)]]
        NCH = [len(c) for c in CH]
        NN = [CAP_L + CAP_C, CAP_L]

        def sems(names):
            return {n: ctx.enter_context(nc.semaphore(n)) for n in names}
        G = Sems(sems("const_in cond_in cT silc ada_in0 ada_in1 ada rowc mod_st0 mod_st1 modr_in modT modT_cp mod1 bars".split()))
        counts = layer_counts(TT, NCH[0], 32 + 4 * 80, 1)
        own = sems(counts)
        L = [Sems(own), Sems(own, counts)]
        block = ctx.enter_context(nc.Block())

        def x_rows(l, t):
            if l:
                return xs_d[ds(t * P, P), :]
            if isinstance(t, int) and t < TC:
                return a["ctx"][0, t * P:(t + 1) * P, :]
            return a["x"][0, ds((t - TC) * P, P), :]

        def tiles(eng, body, first=0):
            for t in range(first, TC):
                body(t, t, False)
            with eng.Fori(TC, TT - 1) as t:
                body(t, t, False)
            body(TT - 1, TT - 1, True)

        def kind(t):
            return 1 if isinstance(t, int) and t < TC else 0

        def mod_bc(l, v, part):
            r = (v * 6 + part) * KD
            return mod_d[l, r:r + KD, :].rearrange("(o k) p -> o (k p)", o=1).to_broadcast([P, D])

        def pairs(eng, l, body):
            if l == 0:
                body(0, 0, None)
                with eng.Fori(0, 4) as i:
                    body(i + 1, TC + i * 2, i)
            else:
                with eng.Fori(0, 4) as i:
                    body(i, TC + i * 2, i)

        HEADS = [(j // 8, j % 8) for j in range(16)]

        def nchunks(k, full):
            return (3, 2)[k] if full else 1

        def chunk_count(j, k, full):
            return j * (nchunks(0, full) + nchunks(1, full)) + k * nchunks(0, full)

        def chunks_before(l, p, lp):
            if lp is None:
                return 0
            return p * 80 if l else (p - 1) * 80 + 32

        def peeled(eng, n, body):
            body(0)
            with eng.Fori(1, n) as i:
                body(i)

        def with_first(eng, body):
            body(0, False)
            body(1, False)
            with eng.Fori(2, E - 1) as e:
                body(e, False)
            body(E - 1, True)

        @block.sync
        def _(sp):
            def ld(dst, src, sem):
                sp.dma_start(dst, src).then_inc(sem, 16)

            ld(ident, a["ident"], G["const_in"])
            ld(crow[0:8, :], a["c"].rearrange("b (k p) -> (b k) p", p=P), G["cond_in"])
            ld(crow[8:16, :], a["c_ctx"].rearrange("(k p) -> k p", p=P), G["cond_in"])
            for l in range(DEPTH):
                with nc.allow_non_contiguous_dma(reason="five short columns"):
                    ld(gcol[:, l, 0:2], a["mla_kv_norm"][l].rearrange("(k p) -> p k", p=P), G["const_in"])
                    ld(gcol[:, l, 2:5], a["mla_q_norm"][l].rearrange("(k p) -> p k", p=P), G["const_in"])
                ld(sinks[:, l, 0, :], a["attn_sink"][l:l + 1, :].to_broadcast([P, WH]), G["const_in"])

            def ada_weights(l):
                def chunk(i):
                    for u in range(2):
                        j = l * 12 + i * 2 + u
                        if not isinstance(j, int) or j >= 2:
                            sp.wait_ge(G["ada"], j - 1)
                        cols = ds((i * 2 + u) * 512, 512)
                        ld(adaw[:, u], a["w_ada"][l].rearrange("(k p) n -> p k n", p=P)[:, :, cols], G[f"ada_in{u}"])
                        ld(adab[0:1, u, :], a["b_ada"][l:l + 1, cols], G[f"ada_in{u}"])
                peeled(sp, 6, chunk)

            def ada_rows(l):
                sp.wait_ge(G["mod_st0"], 16 * 6 * (l + 1))
                sp.wait_ge(G["mod_st1"], 16 * 6 * (l + 1))
                ld(mrow[0:96, l, :], mod_d[l], G["modr_in"])

            ada_weights(0)

            for l in range(DEPTH):
                s = L[l]
                if l:
                    sp.wait_ge(*L[l - 1]("yt", 8 * E))
                w = a["w_in"][l].rearrange("(k p) n -> p k n", p=P)
                for j in range(4):
                    for g in range(2):
                        c0 = C_QA + (g * 4 + j) * WD
                        ld(w_pj[:, :, (2 * j + g) * WD:(2 * j + g + 1) * WD], w[:, :, c0:c0 + WD], s["wp_in"])
                ld(w_pj[:, :, 512:1024], w[:, :, C_KA:C_KR], s["wp_in"])
                ld(w_pj[:, :, 1024:1408], w[:, :, C_CQ:C_G], s["wp_in"])
                ld(w_pj[:, :, 1408:1440], w[:, :, C_KR:C_QA], s["wp_in"])
                ld(w_uq, a["w_uq"][l].rearrange("(k p) n -> p k n", p=P), s["wp_in"])
                ld(w_ukv, a["w_ukv"][l].rearrange("(k p) n -> p k n", p=P), s["wp_in"])
                if l:
                    sp.wait_ge(*L[l - 1]("sc", 32 * E))
                ld(tabs, a["rope"].rearrange("(t p) n -> p t n", p=P), s["wp_in"])
                if l == 0:
                    ld(xb, x_rows(0, 0), s["x_in"])
                    ada_rows(0)

                def keep_x(t):
                    sp.wait_ge(*L[0]("g2", t + 1))
                    ld(xs_d[ds(t * P, P), :], xb, L[0]["out_st"])
                if l:
                    keep_x(0)

                def step(t, n, last):
                    sp.wait_ge(*s("h_a", t + 1))
                    sp.wait_ge(*s("h_d", t + 1))
                    ld(hT_d[:, :, ds(t * P, P)], hts, s["h_st"])
                    if not last and l == 0:
                        sp.wait_ge(*s("xT", 2 * t + 2))
                        ld(xb, x_rows(l, t + 1), s["x_in"])
                    if not last and l:
                        keep_x(t + 1)
                    sp.wait_ge(*s("qW_cp", t + 1))
                    ld(qW_d[ds(t, 1)].rearrange("o p n -> (o p) n"), qWs.rearrange("p a b -> p (a b)"), s["qW_st"])
                    sp.wait_ge(*s("qM_cp", 2 * t + 2))
                    ld(qM_d[ds(t, 1)].rearrange("o p n -> (o p) n"), qMs[0:MQ].rearrange("p a b -> p (a b)"), s["qM_st"])
                tiles(sp, step)

                sp.wait_ge(*s("qM_st", 16 * TT))
                sp.wait_ge(*s("qW_st", 16 * TT))
                for u in range(2):
                    ld(mask[:, u, :], a["wmask"], s["m_in"])
                sp.wait_ge(*s("m_in", 32))

                def pair(p, t0, lp):
                    for u in range(2):
                        if not (isinstance(p, int) and p == 0):
                            sp.wait_ge(*s("sM", p * 16 - 8 + 8 * u))
                            sp.wait_ge(*s("sW", p * 16 - 8 + 8 * u))
                            sp.wait_ge(*s("mxW", p * 16 - 8 + 8 * u))
                        ld(qMt[0:MQ, u].rearrange("p a b -> p (a b)"), qM_d[ds(t0 + u, 1)].rearrange("o p n -> (o p) n"), s[f"q_in{u}"])
                        ld(qWt[:, u].rearrange("p a b -> p (a b)"), qW_d[ds(t0 + u, 1)].rearrange("o p n -> (o p) n"), s[f"q_in{u}"])
                        if lp is None:
                            ld(mask[:, u, 256:384], a["edge"][0, 0], s[f"q_in{u}"])
                        elif u == 0:
                            ld(mask[:, 0, 256:384], a["edge"][0, ds(lp, 1)].rearrange("o p n -> (o p) n"), s[f"q_in{u}"])
                        else:
                            ld(mask[:, 1, 512:640], a["edge"][1, ds(lp, 1)].rearrange("o p n -> (o p) n"), s[f"q_in{u}"])
                pairs(sp, l, pair)

                sp.wait_ge(*s("pv", 32 * NPAIR[l]))
                for ci, (c0, cn) in enumerate(CH[l]):
                    ld(hTr[:, :, c0:c0 + cn], hT_d[:, :, c0:c0 + cn], s[f"hT_in{ci}"])
                def weights(i):
                    for u in range(2):
                        f = i * 2 + u
                        if not isinstance(i, int):
                            sp.wait_ge(*s("g", (f - 1) * NCH[l]))
                        wg = w[:, :, C_G:C_G + 2 * D].rearrange("p k (g n) -> p k g n", g=2)
                        ld(mwt[:, u, 0:8, :], wg[:, :, 0, ds(f * P, P)], s[f"mw_in{u}"])
                        ld(mwt[:, u, 8:16, :], wg[:, :, 1, ds(f * P, P)], s[f"mw_in{u}"])
                        ld(mwt[:, u, 16:20, :], a["w_oa"][l].rearrange("(k p) n -> p k n", p=P)[:, :, ds(f * P, P)], s[f"mw_in{u}"])
                        ld(mwt[:, u, 20:24, :], a["w_ob"][l].rearrange("(k p) n -> p k n", p=P)[:, :, ds(f * P, P)], s[f"mw_in{u}"])
                peeled(sp, 4, weights)
                ld(w_o, a["w_out"][l].rearrange("(k p) n -> p k n", p=P), s["wo_in"])

                sp.wait_ge(*s("mrg", 8 * NCH[l]))
                ld(gb1[:, 0, :], a["ln1_g"][l:l + 1, :].to_broadcast([P, D]), s["lnc_in"])
                ld(gb1[:, 1, :], a["ln1_b"][l:l + 1, :].to_broadcast([P, D]), s["lnc_in"])
                for v in range(2):
                    ld(m2b[:, v, :], mod_bc(l, v, 2), s["lnc_in"])
                ld(wrt, a["w_router"][l].rearrange("(k p) e -> p k e", p=P), s["lnc_in"])
                for v in range(2):
                    ld(m5b[:, v, :], mod_bc(l, v, 5), s["m5_in"])
                ld(xr, x_rows(l, TL[l][0]), s["xr_in"])

                def step1(t, n, last):
                    n = t - TL[l][0]
                    if not last:
                        sp.wait_ge(*s("zs", n + 1))
                        ld(xr, x_rows(l, t + 1), s["xr_in"])
                    sp.wait_ge(*s("x1", n + 1))
                    ld(x1_d[ds(t * P, P), :], x1t, s["x1_st"])
                    sp.wait_ge(*s("z_set", n + 1))
                    ld(z_d[ds(t * P, P), :], zs, s["z_st"])
                tiles(sp, step1, TL[l][0])

                gw = a["w_exp_gate"][l]
                uw = a["w_exp_up"][l]
                dw = a["w_exp_down"][l]

                def experts(e):
                    first = isinstance(e, int)
                    for c in range(RING):
                        if first:
                            if c == 0:
                                sp.wait_ge(*s("mrg", 8 * NCH[l]))
                            if c == 7:
                                sp.wait_ge(*s("y", NT[l]))
                        elif c < 8:
                            sp.wait_ge(*s("au", (e - 1) * 8 + (c // 2) * 2 + 2))
                        else:
                            sp.wait_ge(*s("yt", (e - 1) * 8 + (c - 8) * 2 + 2))
                        if c < 8:
                            src, blk = (uw if c % 2 else gw), c // 2
                        else:
                            src, blk = dw, c - 8
                        v = src[ds(e, 1)].rearrange("o (k p) n -> p (o k) n", p=P)
                        ld(ring[:, c], v[:, :, blk * 256:(blk + 1) * 256], s[f"ring{c // 2 if c < 8 else c - 4}"])
                experts(0)
                if l + 1 < DEPTH:
                    sp.wait_ge(*s("rt", NT[l]))
                    sp.wait_ge(*s("x1_st", 16 * NT[l]))
                    sp.wait_ge(*s("z_st", 16 * NT[l]))
                    ada_weights(l + 1)
                    ada_rows(l + 1)
                with sp.Fori(1, E) as e:
                    experts(e)

        @block.tensor
        def _(pe):
            def mms(o, pairs_, start=True, stop=True):
                n = len(pairs_)
                for i, (lt, rh) in enumerate(pairs_):
                    m = pe.matmul(o, lt, rh, start=start and i == 0, stop=stop and i == n - 1)
                return m

            def tr(o, i):
                return pe.transpose(o, i, ident)

            pe.wait_ge(G["const_in"], 16 * 7)
            pe.wait_ge(G["cond_in"], 32)
            pe.matmul(PS[:, 7, 0:16], crow[0:16, :], ident[0:16, 0:16], start=True, stop=True).then_inc(G["cT"], 1)
            pe.wait_ge(G["silc"], 2)

            def ada_products(l):
                def chunk(i):
                    for u in range(2):
                        j = l * 12 + i * 2 + u
                        pe.wait_ge(G[f"ada_in{u}"], (l * 6 + i + 1) * 32)
                        if not isinstance(j, int) or j >= 2:
                            pe.wait_ge(G["rowc"], j - 1)
                        mms(PS[0:2, u, :], [(silc[:, :, k], adaw[:, u, k, :]) for k in range(KD)], stop=False)
                        pe.matmul(PS[0:2, u, :], ones1[0:1, :], adab[0:1, u, :], start=False, stop=True).then_inc(G["ada"], 1)
                peeled(pe, 6, chunk)
                pe.wait_ge(G["modr_in"], 16 * (l + 1))
                pe.matmul(PS[:, 3, 0:96], mrow[0:96, l, :], ident[0:96, 0:96], start=True, stop=True).then_inc(G["modT"], 1)
            ada_products(0)

            for l in range(DEPTH):
                s = L[l]

                def x_transposes(t):
                    if l:
                        pe.wait_ge(*L[0]("g2", t + 1))
                    else:
                        pe.wait_ge(*s("x_in", (t + 1) * 16))
                    for c in range(2):
                        for k in range(4):
                            m = tr(PS[:, 4 + c, k * P:(k + 1) * P], xb[:, (c * 4 + k) * P:(c * 4 + k + 1) * P])
                        m.then_inc(s["xT"], 1)

                if l == 0:
                    pe.wait_ge(G["mod1"], 1)
                x_transposes(0)
                pe.wait_ge(*s("wp_in", 16 * 14))

                def step(t, n, last):
                    pe.wait_ge(*s("h_a", t + 1))
                    pe.wait_ge(*s("h_d", t + 1))
                    if not (isinstance(t, int) and t == 0):
                        pe.wait_ge(*s("norm", t))
                        pe.wait_ge(*s("used_d", t))
                        pe.wait_ge(*s("ka_cp", t))
                    mms(PS[:, 1, :], [(hts[:, k, :], w_pj[:, k, 512:1024]) for k in range(KD)]).then_inc(s["p1"], 1)
                    mms(PS[:, 2, 0:416], [(hts[:, k, :], w_pj[:, k, 1024:1440]) for k in range(KD)]).then_inc(s["p2"], 1)
                    mms(PS[:, 0, :], [(hts[:, k, :], w_pj[:, k, 0:512]) for k in range(KD)]).then_inc(s["p0"], 1)
                    pe.wait_ge(*s("norm", t + 1))
                    if not (isinstance(t, int) and t == 0):
                        pe.wait_ge(*s("qW_cp", t))
                        pe.wait_ge(*s("qM_cp", 2 * t))
                        pe.wait_ge(*s("kT_cp", 2 * t))
                    for k in range(2):
                        tr(PS[:, 7, k * P:(k + 1) * P], latn[:, k * P:(k + 1) * P])
                    for k in range(3):
                        m = tr(PS[:, 3, k * P:(k + 1) * P], latn[:, KVR + k * P:KVR + (k + 1) * P])
                    m.then_inc(s["latT"], 1)
                    if not last:
                        x_transposes(t + 1)
                    pe.wait_ge(*s("latc_a", t + 1))
                    mms(PS[:, 6, :], [(latTt[:, k, :], w_ukv[:, k, 512:1024]) for k in range(2)]).then_inc(s["ukv"], 1)
                    if not last:
                        pe.wait_ge(*s("h_d", t + 2))
                        pe.wait_ge(*s("h_a", t + 2))
                    mms(PS[:, 5, :], [(latTt[:, k, :], w_ukv[:, k, 0:512]) for k in range(2)]).then_inc(s["ukv"], 1)
                    pe.wait_ge(*s("latc_d", t + 1))
                    for h in range(2):
                        mms(PS[:, 3 + h, 0:384], [(latTt[:, 2 + k, :], w_uq[:, k, h * 384:(h + 1) * 384]) for k in range(3)]).then_inc(s["uq"], 1)
                    pe.wait_ge(*s("ropeW", t + 1))
                    for k in range(4):
                        tr(PS[:, 7, k * P:(k + 1) * P], rW[:, 2 * k:2 * k + 2, :])
                    tr(PS[:, 1, 0:P], rW[:, 8:10, :]).then_inc(s["tW"], 1)
                    pe.wait_ge(*s("kr", t + 1))
                    pe.wait_ge(*s("kn", t + 1))
                    for g in (1, 0):
                        for h in range(4):
                            m = tr(PS[0:MQ, 5 + g, h * P:(h + 1) * P], ksb[:, g * 4 + h, :])
                        m.then_inc(s["tK"], 1)
                    pe.wait_ge(*s("qro", t + 1))
                    for g in range(2):
                        for h in range(4):
                            m = tr(PS[0:MQ, 3 + g, h * P:(h + 1) * P], qsb[:, g * 4 + h, :])
                        m.then_inc(s["tQ"], 1)
                tiles(pe, step)

                pe.wait_ge(*s("kT_cp", 2 * TT))
                pe.wait_ge(*s("qM_cp", 2 * TT))
                pe.wait_ge(*s("qW_cp", TT))
                pe.wait_ge(*s("ka_cp", TT))
                pe.wait_ge(*s("used_d", TT))

                def pair(p, t0, lp):
                    full = lp is not None
                    ch0 = chunks_before(l, p, lp)
                    start = isinstance(p, int) and p == 0

                    def scores(j, k):
                        u, h = HEADS[j]
                        cnt = p * 16 + j

                        def first():
                            if h == 0 and k == 0:
                                pe.wait_ge(*s(f"q_in{u}", p * 48 + 48))
                            if j or not start:
                                pe.wait_ge(*s("mxW" if k else "pM", cnt))

                        parts = []
                        if k == 0:
                            nk = TOK if full else CTX
                            for b, c0 in enumerate(range(0, nk, 512)):
                                cn = min(512, nk - c0)
                                parts.append([(PS[:, b, 0:cn], kT[0:MQ, h, c0:c0 + cn])])
                            q = qMt[0:MQ, u, h, :]
                        else:
                            q = qWt[:, u, h % 4, :]
                            kz = kaZ[:, h // 4, :]
                            parts.append([(PS[:, 3, 0:CTX], kz[:, 0:CTX])])
                            if full:
                                parts[0].append((PS[:, 3, CTX:512], kz[:, ds((lp * 2 + u + 1) * P, 2 * P)]))
                                parts.append([(PS[:, 4, 0:P], kz[:, ds((lp * 2 + u + 3) * P, P)])])

                        def part(i):
                            if i == 0:
                                first()
                            for o, keys in parts[i]:
                                m = pe.matmul(o, q, keys, start=True, stop=True)
                            if i == len(parts) - 1:
                                m.then_inc(s["sW" if k else "sM"], 1)
                        return [lambda i=i: part(i) for i in range(len(parts))]

                    def transposes(j, k, c):
                        nkt = ((10, 5)[k]) if full else 2
                        cc = ch0 + chunk_count(j, k, full) + c
                        if c == 0:
                            pe.wait_ge(*s("pW" if k else "pM", p * 16 + j + 1))
                        if not (isinstance(cc, int) and cc == 0):
                            pe.wait_ge(*s("pt", cc))
                        for kt in range(c * 4, min(c * 4 + 4, nkt)):
                            m = tr(PS[:, 5, (kt - c * 4) * P:(kt - c * 4 + 1) * P], (PM, PW)[k][:, kt * P:(kt + 1) * P])
                        m.then_inc(s["tr"], 1)

                    def outputs(j, k):
                        u, h = HEADS[j]
                        nkt = ((10, 5)[k]) if full else 2
                        pe.wait_ge(*s("pt", ch0 + chunk_count(j, k, full) + nchunks(k, full)))
                        if h == 0 and not (start and u == 0):
                            pe.wait_ge(*s("osb", (p * 2 + u) * 2))
                        if k == 0:
                            vs = [V[:, kt, h * MV:(h + 1) * MV] for kt in range(nkt)]
                        else:
                            g = h // 4
                            vs = [va[:, kt, g * WD:(g + 1) * WD] for kt in range(2)]
                            if full:
                                vs += [va[:, ds(lp * 2 + u + 1 + i, 1), g * WD:(g + 1) * WD].rearrange("p o d -> p (o d)") for i in range(3)]
                        mms(PS[:, 6 + k, h * 64:(h + 1) * 64], [((PTM, PTW)[k][:, kt, :], vs[kt]) for kt in range(nkt)]).then_inc(s["pv"], 1)

                    def turn(u, j):
                        for kk in range(2):
                            pe.wait_ge(*s("osb", (p * 2 + u) * 2 + kk + 1))
                            pe.wait_ge(*s("pt", ch0 + chunk_count(j + 1, 0, full)))
                            if kk or u or not start:
                                pe.wait_ge(*s("fcp", (p * 2 + u) * 2 + kk))
                            for i in range(4):
                                m = tr(PS[:, 5, i * P:(i + 1) * P], osb[:, kk, i * P:(i + 1) * P])
                            m.then_inc(s["fT"], 1)
                        pe.wait_ge(*s("fcp", (p * 2 + u) * 2 + 2))

                    for k in range(2):
                        for f in scores(0, k):
                            f()
                    for j in range(16):
                        for k in range(2):
                            nxt = scores(j + 1, k) if j < 15 else []
                            for c in range(max(nchunks(k, full), len(nxt))):
                                if c < nchunks(k, full):
                                    transposes(j, k, c)
                                if c < len(nxt):
                                    nxt[c]()
                        outputs(j, 0)
                        outputs(j, 1)
                        if j in (8, 15):
                            turn(j // 15, j)
                pairs(pe, l, pair)

                def merge_block(i, u):
                    f = i * 2 + u
                    for ci, (c0, cn) in enumerate(CH[l]):
                        q = f * NCH[l] + ci
                        set_ = (u * NCH[l] + ci) % 2 * 4
                        if not isinstance(q, int) or q >= 2:
                            pe.wait_ge(*s("mrg", q - 1))
                        if ci == 0:
                            pe.wait_ge(*s(f"mw_in{u}", (i + 1) * 64))
                        mms(PS[:, set_, 0:cn], [(mwt[:, u, 16 + k, :], oaT[:, k, c0:c0 + cn]) for k in range(4)])
                        mms(PS[:, set_ + 1, 0:cn], [(mwt[:, u, 20 + k, :], obT[:, k, c0:c0 + cn]) for k in range(4)])
                        pe.wait_ge(*s(f"hT_in{ci}", 16))
                        mms(PS[:, set_ + 2, 0:cn], [(mwt[:, u, k, :], hTr[:, k, c0:c0 + cn]) for k in range(KD)])
                        mms(PS[:, set_ + 3, 0:cn], [(mwt[:, u, 8 + k, :], hTr[:, k, c0:c0 + cn]) for k in range(KD)]).then_inc(s["g"], 1)
                for u in range(2):
                    merge_block(0, u)
                with pe.Fori(1, 4) as i:
                    for u in range(2):
                        merge_block(i, u)

                pe.wait_ge(*s("mrg", 8 * NCH[l]))
                pe.wait_ge(*s("wo_in", 16))
                pe.wait_ge(*s("lnc_in", 16 * 5))

                def y_tile(t):
                    n = t - TL[l][0]
                    pe.wait_ge(*s("mst", n + 1))
                    if not (isinstance(n, int) and n == 0):
                        pe.wait_ge(*s("y_used", n))
                    for h in range(2):
                        m = mms(PS[:, h, :], [(mst[:, k, :], w_o[:, k, h * 512:(h + 1) * 512]) for k in range(KD)])
                    m.then_inc(s["y"], 1)

                def x1_transposes(t):
                    n = t - TL[l][0]
                    pe.wait_ge(*s("x1", n + 1))
                    if not (isinstance(n, int) and n == 0):
                        pe.wait_ge(*s("h2a", n))
                        pe.wait_ge(*s("h2d", n))
                    for c in range(2):
                        for k in range(4):
                            m = tr(PS[:, 2 + c, k * P:(k + 1) * P], x1t[:, (c * 4 + k) * P:(c * 4 + k + 1) * P])
                        m.then_inc(s["x1T"], 1)
                    pe.wait_ge(*s("h2a", n + 1))
                    pe.wait_ge(*s("h2d", n + 1))
                    if not (isinstance(n, int) and n == 0):
                        pe.wait_ge(*s("rt_cp", n))
                    mms(PS[:, 4, 0:E], [(h2t[:, k, :], wrt[:, k, :]) for k in range(KD)]).then_inc(s["rt"], 1)

                t0 = TL[l][0]
                y_tile(t0)
                if l == 0:
                    y_tile(1)
                    x1_transposes(0)
                    y_tile(2)
                    x1_transposes(1)
                with pe.Fori(TC + 1, TT) as t:
                    y_tile(t)
                    x1_transposes(t - 1)
                x1_transposes(TT - 1)

                pe.wait_ge(*s("aff", 1))
                for i, t in enumerate(TL[l]):
                    m = pe.matmul(PS[0:E, 5 + t // 4, (t % 4) * P:(t % 4 + 1) * P], afft[:, t, :], ident, start=True, stop=True)
                m.then_inc(s["affT"], 1)
                if l + 1 < DEPTH:
                    pe.wait_ge(*s("y_used", NT[l]))
                    pe.wait_ge(*s("h2d", NT[l]))
                    ada_products(l + 1)
                pe.wait_ge(*s("topk", 1))
                pe.matmul(PS[:, 2, 0:E], idxf[0:E, :], ident[0:E, 0:E], start=True, stop=True)
                m = pe.matmul(PS[:, 2, E:2 * E], vals[0:E, :], ident[0:E, 0:E], start=True, stop=True)
                if l == 0:
                    pe.matmul(PS[0:CAP_C, 2, 2 * E:3 * E], idcf[0:E, :], ident[0:E, 0:E], start=True, stop=True)
                    m = pe.matmul(PS[0:CAP_C, 2, 3 * E:4 * E], valc[0:E, :], ident[0:E, 0:E], start=True, stop=True)
                m.then_inc(s["sel"], 1)

                N = NN[l]

                def xg_transposes(e):
                    pe.wait_ge(*s("gat", (e + 1) * 16 * (2 - l)))
                    if l == 0 and not (isinstance(e, int) and e <= 1):
                        pe.wait_ge(*s("ylat", 2 * (e - 1)))
                        pe.wait_ge(*s("yctx", 2 * (e - 1)))
                    for c in range(2):
                        for k in range(4):
                            m = tr(PS[:, c, k * P:(k + 1) * P], xg[:, (c * 4 + k) * P:(c * 4 + k + 1) * P])
                        if l or c == 0:
                            m.then_inc(s["xgT"], 1)
                    if l == 0:
                        for k in range(KD):
                            m = pe.matmul(PS[:, 2, k * 32:(k + 1) * 32], xgc[0:CAP_C, k * P:(k + 1) * P], ident[0:CAP_C, 0:CAP_C], start=True, stop=True)
                        m.then_inc(s["xgT"], 1)

                def back(e):
                    pe.wait_ge(*s("yc_a", e * 4 + 4))
                    pe.wait_ge(*s("yc_d", e * 4 + 4))
                    for r in range(2):
                        for j in range(4):
                            m = tr(PS[:, (7, 0)[r], j * P:(j + 1) * P], yT[:, r * 4 + j, 0:P])
                        for j in range(4):
                            m = pe.matmul(PS[0:CAP_C, 1 + r, j * P:(j + 1) * P], yT[:, r * 4 + j, P:P + CAP_C], ident, start=True, stop=True)
                        m.then_inc(s["bk"], 1)

                def expert(e, last):
                    first = isinstance(e, int) and e == 0
                    pe.wait_ge(*s("xa", e + 1))
                    pe.wait_ge(*s("xd", e + 1))
                    for f in range(KD):
                        if f % 2 == 0:
                            pe.wait_ge(*s(f"ring{f // 2}", (e + 1) * 32))
                        if not (first and f < 2):
                            pe.wait_ge(*s("act", e * 8 + f - 1))
                        for h in range(2):
                            m = mms(PS[:, 3 + f % 2, h * N:(h + 1) * N],
                                    [(ring[:, (f // 2) * 2 + h, k, (f % 2) * P:(f % 2 + 1) * P], xgT[:, k, 0:N]) for k in range(KD)])
                        m.then_inc(s["au"], 1)
                        if f == 1 and l == 0 and not first:
                            back(e - 1)
                    if not last:
                        xg_transposes(e + 1)
                    pe.wait_ge(*s("act", (e + 1) * 8))
                    if l == 0:
                        for d in range(KD):
                            if d % 2 == 0:
                                pe.wait_ge(*s(f"ring{4 + d // 2}", (e + 1) * 16))
                            if not (first and d < 2):
                                pe.wait_ge(*s("yc_d" if d % 2 else "yc_a", e * 4 + d // 2))
                            mms(PS[:, 5 + d % 2, 0:N], [(ring[:, 8 + d // 2, k, (d % 2) * P:(d % 2 + 1) * P], actT[:, k, 0:N]) for k in range(KD)]).then_inc(s["yt"], 1)
                    else:
                        for c in range(4):
                            pe.wait_ge(*s(f"ring{4 + c}", (e + 1) * 16))
                            if c % 2 == 0 and not first:
                                pe.wait_ge(*s("ylat", 2 * e - 1 + c // 2))
                            mms(PS[:, 5 + c // 2, (c % 2) * 256:(c % 2 + 1) * 256],
                                [(actT[:, k, 0:P], ring[:, 8 + c, k, :]) for k in range(KD)]).then_inc(s["yt"], 2)
                pe.wait_ge(*s("sel_cp", 1))
                xg_transposes(0)
                with_first(pe, expert)
                if l == 0:
                    back(E - 1)

        @block.scalar
        def _(act):
            A = act.activation
            act.wait_ge(G["cT"], 1)
            A(silc.rearrange("p v k -> p (v k)"), PS[:, 7, 0:16], ACT.Silu).then_inc(G["silc"], 1)

            def ada_copies(l):
                def row(i):
                    for u in range(2):
                        j = l * 12 + i * 2 + u
                        act.wait_ge(G["ada"], j + 1)
                        if not isinstance(j, int) or j >= 2:
                            act.wait_ge(G[f"mod_st{u}"], (l * 6 + i) * 16)
                        A(adar[0:2, u, :], PS[0:2, u, :], ACT.Copy).then_inc(G["rowc"], 1)
                peeled(act, 6, row)
                act.wait_ge(G["modT"], l + 1)
                A(arena[:, 128 + 96 * l:224 + 96 * l], PS[:, 3, 0:96], ACT.Copy).then_inc(G["modT_cp"], 1)
            ada_copies(0)

            for l in range(DEPTH):
                s = L[l]

                def h_half(t, sem_val=None):
                    v = kind(t)
                    act.wait_ge(*s("xT", 2 * t + 1))
                    if not (isinstance(t, int) and t == 0):
                        act.wait_ge(*s("h_st", 16 * t))
                        act.wait_ge(*s("p0", t))
                    for k in range(4):
                        m = A(hts[:, k, :], PS[:, 4, k * P:(k + 1) * P], ACT.Identity,
                              scale=modT[:, l, v, 1, k:k + 1], bias=modT[:, l, v, 0, k:k + 1])
                    m.then_inc(s["h_a"], 1)

                def norm_x(t):
                    q = L[0]
                    act.wait_ge(*q("st2", t + 1))
                    A(stat[:, 24:25], stat[:, 27:28], ACT.Sqrt, bias=epsc[:, 0:1]).then_inc(q["sq2"], 1)
                    act.wait_ge(*q("rs2", t + 1))
                    A(o2[:, 0, :], z2[:, 0, :], ACT.Identity, scale=stat[:, 12:13], bias=stat[:, 13:14]).then_inc(q["n2"], 1)
                act.wait_ge(G["mod1"], 1 + l)
                act.wait_ge(G["bars"], 3)
                if l:
                    norm_x(0)
                h_half(0)

                def step(t, n, last):
                    if l and not last:
                        norm_x(t + 1)
                    act.wait_ge(*s("p1", t + 1))
                    A(junk[:, 0:KVR], PS[:, 1, 256:512], ACT.Square, accum_out=stat[:, 0:1])
                    act.drain()
                    act.wait_ge(*s("p2", t + 1))
                    A(junk[:, 0:QR], PS[:, 2, 0:QR], ACT.Square, accum_out=stat[:, 1:2])
                    act.drain()
                    A(stat[:, 2:3], stat[:, 0:1], ACT.Sqrt, scale=1.0 / KVR, bias=epsc[:, 1:2])
                    A(stat[:, 3:4], stat[:, 1:2], ACT.Sqrt, scale=1.0 / QR, bias=epsc[:, 1:2]).then_inc(s["rms"], 1)
                    act.wait_ge(*s("rstd", t + 1))
                    if not (isinstance(t, int) and t == 0):
                        act.wait_ge(*s("latT", t))
                    A(latn[:, 0:KVR], PS[:, 1, 256:512], ACT.Copy, scale=stat[:, 4:5])
                    A(latn[:, KVR:], PS[:, 2, 0:QR], ACT.Copy, scale=stat[:, 5:6]).then_inc(s["norm"], 1)
                    act.wait_ge(*s("latT", t + 1))
                    for k in range(2):
                        m = A(latTt[:, k, :], PS[:, 7, k * P:(k + 1) * P], ACT.Copy, scale=gcol[:, l, k:k + 1])
                    m.then_inc(s["latc_a"], 1)
                    if not last:
                        h_half(t + 1)
                    for i, g in enumerate((1, 0)):
                        act.wait_ge(*s("ukv", 2 * t + i + 1))
                        if i == 0 and not (isinstance(t, int) and t == 0):
                            act.wait_ge(*s("tK", 2 * t))
                        src = PS[:, 5 + g, :].rearrange("p (h c) -> p h c", h=4)
                        A(V[:, ds(t, 1), g * 256:(g + 1) * 256].rearrange("p o (h c) -> p (o h) c", h=4), src[:, :, NOPE:], ACT.Copy)
                        m = A(ksb[:, g * 4:(g + 1) * 4, 0:NOPE], src[:, :, 0:NOPE], ACT.Copy)
                    m.then_inc(s["kn"], 1)
                    act.wait_ge(*s("tW", t + 1))
                    if not (isinstance(t, int) and t == 0):
                        act.wait_ge(*s("qW_st", 16 * t))
                    A(qWs.rearrange("p a b -> p (a b)"), PS[:, 7, :], ACT.Copy).then_inc(s["qW_cp"], 1)
                    for i, g in enumerate((1, 0)):
                        act.wait_ge(*s("tK", 2 * t + i + 1))
                        A(kT[0:MQ, g * 4:(g + 1) * 4, ds(t * P, P)], PS[0:MQ, 5 + g, :].rearrange("p (h c) -> p h c", h=4), ACT.Copy).then_inc(s["kT_cp"], 1)
                tiles(act, step)

                def pair(p, t0, lp):
                    full = lp is not None
                    ch0 = chunks_before(l, p, lp)
                    start = isinstance(p, int) and p == 0

                    def expo(j, k):
                        u, h = HEADS[j]
                        act.wait_ge(*s("mxW" if k else "mxM", p * 16 + j + 1))
                        if k == 0:
                            nk = TOK if full else CTX
                            if j or not start:
                                act.wait_ge(*s("tr", ch0 + (chunk_count(j - 1, 1, full) if j else 0)))
                            A(PM[:, 0:nk], PS[:, 0:3, :].rearrange("p b n -> p (b n)")[:, 0:nk], ACT.Exp, scale=MSCALE,
                              bias=stat[:, 32 + u * 8 + h:33 + u * 8 + h], accum_out=stat[:, 64 + u * 8 + h:65 + u * 8 + h]).then_inc(s["pM"], 1)
                        else:
                            nk = 640 if full else CTX
                            A(PW[:, 0:nk], PW[:, 0:nk], ACT.Exp, bias=stat[:, 48 + u * 8 + h:49 + u * 8 + h],
                              accum_out=stat[:, 80 + u * 8 + h:81 + u * 8 + h]).then_inc(s["pW"], 1)

                    def copy_chunk(j, k, c):
                        nkt = ((10, 5)[k]) if full else 2
                        a0, a1 = c * 4, min(c * 4 + 4, nkt)
                        act.wait_ge(*s("tr", ch0 + chunk_count(j, k, full) + c + 1))
                        A((PTM, PTW)[k][:, a0:a1, :].rearrange("p a b -> p (a b)"), PS[:, 5, 0:(a1 - a0) * P], ACT.Copy).then_inc(s["pt"], 1)

                    def turn(u):
                        for kk in range(2):
                            act.wait_ge(*s("fT", (p * 2 + u) * 2 + kk + 1))
                            A((obT, oaT)[kk][:, :, ds((t0 + u) * P, P)], PS[:, 5, :].rearrange("p (a b) -> p a b", a=4), ACT.Copy).then_inc(s["fcp"], 1)

                    expo(0, 0)
                    expo(0, 1)
                    for j in range(16):
                        copy_chunk(j, 0, 0)
                        if full:
                            copy_chunk(j, 0, 2)
                        copy_chunk(j, 1, 0)
                        if full:
                            copy_chunk(j, 1, 1)
                        if j < 15:
                            expo(j + 1, 0)
                            expo(j + 1, 1)
                        if j in (7, 15):
                            act.wait_ge(*s("es", p * 2 + j // 8 + 1))
                            A(stat[:, 16:24], stat[:, 8:16], ACT.Exp).then_inc(s["tot"], 1)
                        if j in (8, 15):
                            turn(j // 15)
                pairs(act, l, pair)

                def merge_block(f, u):
                    for ci, (c0, cn) in enumerate(CH[l]):
                        q = f * NCH[l] + ci
                        set_ = (u * NCH[l] + ci) % 2
                        act.wait_ge(*s("g", q + 1))
                        if not isinstance(f, int) or q >= 2:
                            act.wait_ge(*s("mrg", q - 1))
                        A(sg[:, set_, 0, 0:cn], PS[:, set_ * 4 + 2, 0:cn], ACT.Sigmoid)
                        A(sg[:, set_, 1, 0:cn], PS[:, set_ * 4 + 3, 0:cn], ACT.Sigmoid).then_inc(s["sg"], 1)
                for u in range(2):
                    merge_block(u, u)
                with act.Fori(1, 4) as i:
                    for u in range(2):
                        merge_block(i * 2 + u, u)

                def ln_a(t):
                    n = t - TL[l][0]
                    act.wait_ge(*s("lnv", n + 1))
                    A(stat[:, 7:8], stat[:, 9:10], ACT.Sqrt, bias=epsc[:, 0:1]).then_inc(s["lnr"], 1)
                    act.wait_ge(*s("lnb", n + 1))
                    A(xn, zt, ACT.Identity, scale=stat[:, 10:11], bias=stat[:, 11:12]).then_inc(s["lnn"], 1)

                def tr_a(t):
                    n = t - TL[l][0]
                    v = kind(t)
                    act.wait_ge(*s("x1T", 2 * n + 1))
                    if not (isinstance(n, int) and n == 0):
                        act.wait_ge(*s("rt", n))
                    for k in range(4):
                        m = A(h2t[:, k, :], PS[:, 2, k * P:(k + 1) * P], ACT.Identity,
                              scale=modT[:, l, v, 4, k:k + 1], bias=modT[:, l, v, 3, k:k + 1])
                    m.then_inc(s["h2a"], 1)
                    act.wait_ge(*s("rt", n + 1))
                    A(logit[:, ds(t, 1), :].rearrange("p o e -> p (o e)"), PS[:, 4, 0:E], ACT.Copy).then_inc(s["rt_cp"], 1)
                ln_a(TL[l][0])
                if l == 0:
                    tr_a(0)
                    ln_a(1)
                    tr_a(1)
                    ln_a(2)
                with act.Fori(TC + 1, TT) as t:
                    tr_a(t - 1)
                    ln_a(t)
                tr_a(TT - 1)
                tl = TL[l][0]
                act.wait_ge(*s("sm_m", 1))
                A(afft[:, tl:TT, :], afft[:, tl:TT, :], ACT.Exp).then_inc(s["sm_e"], 1)
                if l + 1 < DEPTH:
                    ada_copies(l + 1)
                act.wait_ge(*s("sel", 1))

                N = NN[l]

                def rows_a(e):
                    act.wait_ge(*s("xgT", 2 * e + 1))
                    if not (isinstance(e, int) and e == 0):
                        act.wait_ge(*s("au", e * 8))
                    for k in range(4):
                        m = A(xgT[:, k, 0:P], PS[:, 0, k * P:(k + 1) * P], ACT.Identity,
                              scale=modT[:, l, 0, 4, k:k + 1], bias=modT[:, l, 0, 3, k:k + 1])
                    if l == 0:
                        act.wait_ge(*s("xgT", 2 * e + 2))
                        for k in range(KD):
                            m = A(xgT[:, k, P:N], PS[:, 2, k * 32:(k + 1) * 32], ACT.Identity,
                                  scale=modT[:, l, 1, 4, k:k + 1], bias=modT[:, l, 1, 3, k:k + 1])
                    m.then_inc(s["xa"], 1)

                def expert(e, last):
                    for f in range(KD):
                        act.wait_ge(*s("au", e * 8 + f + 1))
                        if not (isinstance(e, int) and e == 0 and f < 2):
                            act.wait_ge(*s("act", e * 8 + f - 1))
                        A(silb[:, f % 2, 0:N], PS[:, 3 + f % 2, 0:N], ACT.Silu).then_inc(s["sil"], 1)
                    if not last:
                        rows_a(e + 1)
                    for d in range(0, KD if l == 0 else 0, 2):
                        act.wait_ge(*s("yt", e * 8 + d + 1))
                        if d == 0 and not (isinstance(e, int) and e == 0):
                            act.wait_ge(*s("bk", 2 * e))
                        A(yT[:, d, 0:N], PS[:, 5, 0:N], ACT.Copy).then_inc(s["yc_a"], 1)
                rows_a(0)
                with_first(act, expert)

                if l < DEPTH - 1:
                    continue

                def norm_pair(i):
                    for u in range(2):
                        n = i * 2 + u
                        act.wait_ge(*s("st2", n + 1))
                        A(stat[:, 24 + u:25 + u], stat[:, 27 + 2 * u:28 + 2 * u], ACT.Sqrt, bias=epsc[:, 0:1]).then_inc(s["sq2"], 1)
                        act.wait_ge(*s("rs2", n + 1))
                        if u == 0 and not isinstance(i, int):
                            act.wait_ge(*s("out_st", i * 32))
                        A(o2[:, u, :], z2[:, u, :], ACT.Identity, scale=stat[:, 12 + 2 * u:13 + 2 * u], bias=stat[:, 13 + 2 * u:14 + 2 * u]).then_inc(s["n2"], 1)

                    for u in range(2):
                        n = i * 2 + u
                        act.wait_ge(*s("g2", n + 1))
                        act.dma_start(out[0, ds(n * P, P), :], o2[:, u, :]).then_inc(s["out_st"], 16)
                peeled(act, NPAIR[l], norm_pair)
            act.wait_ge(*L[DEPTH - 1]("out_st", 16 * NT[DEPTH - 1]))

        @block.vector
        def _(dve):
            def TTR(o, x, y, op):
                return dve.tensor_tensor(o, x, y, op)

            dve.memset(ones1, 1.0).then_inc(G["silc"], 1)
            dve.memset(epsc[:, 0:1], LN_EPS)
            dve.memset(epsc[:, 1:2], RMS_EPS).then_inc(G["bars"], 1)
            dve.wait_ge(G["const_in"], 16 * 7)
            for l in range(DEPTH):
                dve.tensor_scalar(sinks[:, l, 1, :], sinks[:, l, 0, :], -1.0, None, ALU.mult).then_inc(G["bars"], 1)

            def ada_scales(l):
                dve.wait_ge(G["modT_cp"], l + 1)
                for v in range(2):
                    for part in (1, 4):
                        m = dve.tensor_scalar(modT[:, l, v, part, :], modT[:, l, v, part, :], 1.0, None, ALU.add)
                m.then_inc(G["mod1"], 1)
            ada_scales(0)

            def rope(dst, src, table, h, half, tmp):
                w = 4 * half
                C = table[:, 0:w]
                S = table[:, w:2 * w]
                x = src.rearrange("p h (a s n) -> p h a s n", a=2, s=2)
                t = tmp.rearrange("p h (a s n) -> p h a s n", a=2, s=2)
                Sv = S.rearrange("p (a s n) -> p a s n", a=2, s=2)
                TTR(dst, src, C.unsqueeze(1).to_broadcast([P, h, w]), ALU.mult)
                for i in range(2):
                    if h == 1:
                        TTR(t[:, 0, :, i, :], x[:, 0, :, 1 - i, :], Sv[:, :, i, :], ALU.mult)
                    else:
                        TTR(t[:, :, :, i, :], x[:, :, :, 1 - i, :], Sv[:, :, i, :].unsqueeze(1).to_broadcast([P, h, 2, half]), ALU.mult)
                dve.drain()
                return TTR(dst, dst, tmp, ALU.add)

            for l in range(DEPTH):
                s = L[l]
                if l:
                    dve.wait_ge(*L[l - 1]("sc", 16 * E * 2))
                dve.memset(kaZ.rearrange("p a b -> p (a b)"), 0.0)
                dve.memset(va[:, TT, :], 0.0)
                dve.drain()

                def h_half(t):
                    v = kind(t)
                    dve.wait_ge(*s("xT", 2 * t + 2))
                    if not (isinstance(t, int) and t == 0):
                        dve.wait_ge(*s("h_st", 16 * t))
                        dve.wait_ge(*s("p0", t))
                    for k in range(4):
                        m = dve.tensor_scalar(hts[:, 4 + k, :], PS[:, 5, k * P:(k + 1) * P], modT[:, l, v, 1, 4 + k:5 + k],
                                              modT[:, l, v, 0, 4 + k:5 + k], ALU.mult, ALU.add)
                    m.then_inc(s["h_d"], 1)

                def norm_x(t):
                    q = L[0]
                    dve.wait_ge(*q("z_in0", (t + 1) * 16))
                    for h in range(2):
                        dve.bn_stats(stat[:, 32 + 6 * h:38 + 6 * h], z2[:, 0, h * 512:(h + 1) * 512])
                    dve.drain()
                    dve.bn_aggr(stat[:, 26:28], stat[:, 32:44]).then_inc(q["st2"], 1)
                    dve.wait_ge(*q("sq2", t + 1))
                    dve.reciprocal(stat[:, 12:13], stat[:, 24:25])
                    dve.drain()
                    dve.tensor_scalar(stat[:, 13:14], stat[:, 26:27], stat[:, 12:13], -1.0, ALU.mult, ALU.mult).then_inc(q["rs2"], 1)
                    dve.wait_ge(*q("n2", t + 1))
                    TTR(o2[:, 0, :], o2[:, 0, :], gb2[:, 0, :], ALU.mult)
                    dve.drain()
                    if not (isinstance(t, int) and t == 0):
                        dve.wait_ge(*s("xT", 2 * t))
                        dve.wait_ge(*q("out_st", 16 * t))
                    TTR(xb, o2[:, 0, :], gb2[:, 1, :], ALU.add).then_inc(q["g2"], 1)
                if l:
                    dve.wait_ge(*L[0]("gb2_in", 32))
                    norm_x(0)
                h_half(0)
                dve.wait_ge(*s("wp_in", 16 * 14))

                def step(t, n, last):
                    tab = tabs[:, ds(t, 1), :].rearrange("p o n -> p (o n)")
                    if l and not last:
                        norm_x(t + 1)
                    dve.wait_ge(*s("rms", t + 1))
                    dve.reciprocal(stat[:, 4:6], stat[:, 2:4]).then_inc(s["rstd"], 1)
                    dve.wait_ge(*s("latT", t + 1))
                    for k in range(3):
                        m = dve.tensor_scalar(latTt[:, 2 + k, :], PS[:, 3, k * P:(k + 1) * P], gcol[:, l, 2 + k:3 + k], None, ALU.mult)
                    m.then_inc(s["latc_d"], 1)
                    if not last:
                        h_half(t + 1)
                    dve.wait_ge(*s("p0", t + 1))
                    if not (isinstance(t, int) and t == 0):
                        dve.wait_ge(*s("tW", t))
                    dve.tensor_copy(va[:, ds(t, 1), :].rearrange("p o n -> p (o n)"), PS[:, 1, P:2 * P])
                    src = PS[:, 0:2, :].rearrange("p b n -> p (b n)")[:, 0:640].rearrange("p (h c) -> p h c", c=WD)
                    rope(rW, src, tab[:, 0:128], 10, 16, rC).then_inc(s["ropeW"], 1)
                    rope(krr.unsqueeze(1), PS[:, 2, QR:QR + ROPE].unsqueeze(1), tab[:, 128:192], 1, 8, krt.unsqueeze(1)).then_inc(s["used_d"], 1)
                    dve.drain()
                    if not (isinstance(t, int) and t == 0):
                        dve.wait_ge(*s("tK", 2 * t))
                    dve.tensor_copy(ksb[:, :, NOPE:], krr.unsqueeze(1).to_broadcast([P, MH, ROPE])).then_inc(s["kr"], 1)
                    if not (isinstance(t, int) and t == 0):
                        dve.wait_ge(*s("tQ", 2 * t))
                    for g in range(2):
                        dve.wait_ge(*s("uq", 2 * t + g + 1))
                        src = PS[:, 3 + g, 0:384].rearrange("p (h c) -> p h c", h=4)
                        dve.tensor_copy(qsb[:, g * 4:(g + 1) * 4, 0:NOPE], src[:, :, 0:NOPE])
                        m = rope(qsb[:, g * 4:(g + 1) * 4, NOPE:], src[:, :, NOPE:], tab[:, 128:192], 4, 8, tmpm)
                        dve.drain() if g == 0 else None
                    m.then_inc(s["qro"], 1)
                    dve.wait_ge(*s("tW", t + 1))
                    for g in range(2):
                        m = dve.tensor_copy(kaZ[g * 64:(g + 1) * 64, g, ds(t * P, P)], PS[g * 64:(g + 1) * 64, 1, 0:P])
                    m.then_inc(s["ka_cp"], 1)
                    if not (isinstance(t, int) and t == 0):
                        dve.wait_ge(*s("qM_st", 16 * t))
                    for g in range(2):
                        dve.wait_ge(*s("tQ", 2 * t + g + 1))
                        dve.tensor_copy(qMs[0:MQ, g * 4:(g + 1) * 4, :].rearrange("p a b -> p (a b)"), PS[0:MQ, 3 + g, :]).then_inc(s["qM_cp"], 1)
                tiles(dve, step)

                dve.wait_ge(*s("m_in", 32))

                def pair(p, t0, lp):
                    full = lp is not None
                    ch0 = chunks_before(l, p, lp)
                    start = isinstance(p, int) and p == 0

                    def stats(j, k):
                        u, h = HEADS[j]
                        if k == 0:
                            nk = TOK if full else CTX
                            dve.wait_ge(*s("sM", p * 16 + j + 1))
                            dve.tensor_reduce(stat[:, 31:32], PS[:, 0:3, :].rearrange("p b n -> p (b n)")[:, 0:nk], AX.X, ALU.max, negate=True)
                            dve.drain()
                            dve.tensor_scalar(stat[:, 32 + u * 8 + h:33 + u * 8 + h], stat[:, 31:32], MSCALE, None, ALU.mult).then_inc(s["mxM"], 1)
                        else:
                            nk = 640 if full else CTX
                            dve.wait_ge(*s("sW", p * 16 + j + 1))
                            if h == 0:
                                dve.wait_ge(*s(f"q_in{u}", p * 48 + 48))
                            if j or not start:
                                dve.wait_ge(*s("tr", ch0 + chunk_count(j, 0, full)))
                            dve.nop(nofuse=True)
                            dve.tensor_tensor_reduce(out=PW[:, 0:nk], in0=PS[:, 3:5, :].rearrange("p b n -> p (b n)")[:, 0:nk],
                                                     in1=mask[:, u, 0:nk], scale=WSCALE, scalar=-3.0e38,
                                                     op0=ALU.add, op1=ALU.max, accum_out=stat[:, 30:31])
                            dve.drain()
                            dve.tensor_scalar(stat[:, 48 + u * 8 + h:49 + u * 8 + h], stat[:, 30:31], -1.0, sinks[:, l, 1, h:h + 1],
                                              ALU.mult, ALU.min).then_inc(s["mxW"], 1)

                    def copy_chunk(j):
                        dve.wait_ge(*s("tr", ch0 + chunk_count(j, 0, full) + 2))
                        dve.tensor_copy(PTM[:, 4:8, :].rearrange("p a b -> p (a b)"), PS[:, 5, :]).then_inc(s["pt"], 1)

                    def finish(u):
                        dve.wait_ge(*s("pW", p * 16 + 8 * u + 8))
                        TTR(stat[:, 8:16], stat[:, 48 + u * 8:56 + u * 8], sinks[:, l, 0, :], ALU.add).then_inc(s["es"], 1)
                        dve.wait_ge(*s("tot", p * 2 + u + 1))
                        TTR(stat[:, 80 + u * 8:88 + u * 8], stat[:, 80 + u * 8:88 + u * 8], stat[:, 16:24], ALU.add)
                        dve.drain()
                        dve.reciprocal(stat[:, 80 + u * 8:88 + u * 8], stat[:, 80 + u * 8:88 + u * 8])
                        dve.reciprocal(stat[:, 64 + u * 8:72 + u * 8], stat[:, 64 + u * 8:72 + u * 8])
                        dve.drain()
                        dve.wait_ge(*s("pv", p * 32 + 16 * u + 16))
                        if u or not start:
                            dve.wait_ge(*s("fT", (p * 2 + u) * 2))
                        for kk, c in ((0, 64), (1, 80)):
                            r = stat[:, c + u * 8:c + 8 + u * 8].unsqueeze(2).to_broadcast([P, 8, 64])
                            TTR(osb[:, kk, :].rearrange("p (h d) -> p h d", h=8), PS[:, 6 + kk, :].rearrange("p (h d) -> p h d", h=8), r, ALU.mult).then_inc(s["osb"], 1)

                    stats(0, 0)
                    stats(0, 1)
                    for j in range(16):
                        if full:
                            copy_chunk(j)
                        if j < 15:
                            stats(j + 1, 0)
                            stats(j + 1, 1)
                        if j in (7, 15):
                            finish(j // 8)
                pairs(dve, l, pair)

                def merge_block(f, u):
                    for ci, (c0, cn) in enumerate(CH[l]):
                        q = f * NCH[l] + ci
                        set_ = (u * NCH[l] + ci) % 2
                        dve.wait_ge(*s("sg", q + 1))
                        for j in range(2):
                            TTR(sg[:, set_, j, 0:cn], sg[:, set_, j, 0:cn], PS[:, set_ * 4 + j, 0:cn], ALU.mult)
                        dve.drain()
                        TTR(mrgT[:, ds(f, 1), c0:c0 + cn].rearrange("p o n -> p (o n)"), sg[:, set_, 0, 0:cn], sg[:, set_, 1, 0:cn], ALU.add).then_inc(s["mrg"], 1)
                for u in range(2):
                    merge_block(u, u)
                with dve.Fori(1, 4) as i:
                    for u in range(2):
                        merge_block(i * 2 + u, u)

                dve.wait_ge(*s("lnc_in", 16 * 5))

                def ln_d(t):
                    n = t - TL[l][0]
                    v = kind(t)
                    dve.wait_ge(*s("y", n + 1))
                    TTR(zt, PS[:, 0:2, :].rearrange("p b n -> p (b n)"), m2b[:, v, :], ALU.mult).then_inc(s["y_used"], 1)
                    dve.drain()
                    dve.wait_ge(*s("xr_in", (n + 1) * 16))
                    dve.scalar_tensor_tensor(out=zt, in0=xr, scalar=ALPHA, in1=zt, op0=ALU.mult, op1=ALU.add).then_inc(s["zs"], 1)
                    dve.drain()
                    for h in range(2):
                        dve.bn_stats(stat[:, 12 + 6 * h:18 + 6 * h], zt[:, h * 512:(h + 1) * 512])
                    dve.drain()
                    dve.bn_aggr(stat[:, 8:10], stat[:, 12:24]).then_inc(s["lnv"], 1)
                    dve.wait_ge(*s("lnr", n + 1))
                    dve.reciprocal(stat[:, 10:11], stat[:, 7:8])
                    dve.drain()
                    dve.tensor_scalar(stat[:, 11:12], stat[:, 8:9], stat[:, 10:11], -1.0, ALU.mult, ALU.mult).then_inc(s["lnb"], 1)
                    dve.wait_ge(*s("lnn", n + 1))
                    TTR(xn, xn, gb1[:, 0, :], ALU.mult)
                    dve.drain()
                    if not (isinstance(n, int) and n == 0):
                        dve.wait_ge(*s("x1T", 2 * n))
                        dve.wait_ge(*s("x1_st", 16 * n))
                        dve.wait_ge(*s("z_set", n))
                    TTR(x1t, xn, gb1[:, 1, :], ALU.add).then_inc(s["x1"], 1)

                def tr_d(t):
                    n = t - TL[l][0]
                    v = kind(t)
                    dve.wait_ge(*s("x1T", 2 * n + 2))
                    if not (isinstance(n, int) and n == 0):
                        dve.wait_ge(*s("rt", n))
                    for k in range(4):
                        m = dve.tensor_scalar(h2t[:, 4 + k, :], PS[:, 3, k * P:(k + 1) * P], modT[:, l, v, 4, 4 + k:5 + k],
                                              modT[:, l, v, 3, 4 + k:5 + k], ALU.mult, ALU.add)
                    m.then_inc(s["h2d"], 1)
                ln_d(TL[l][0])
                if l == 0:
                    tr_d(0)
                    ln_d(1)
                    tr_d(1)
                    ln_d(2)
                with dve.Fori(TC + 1, TT) as t:
                    tr_d(t - 1)
                    ln_d(t)
                tr_d(TT - 1)

                tl = TL[l][0]
                nt = NT[l]
                dve.wait_ge(*s("rt_cp", nt))
                lg = logit[:, tl:TT, :]
                av = afft[:, tl:TT, :]
                dve.tensor_reduce(stat[:, 32:32 + nt], lg, AX.X, ALU.max)
                dve.drain()
                TTR(av, lg, stat[:, 32:32 + nt].unsqueeze(2).to_broadcast([P, nt, E]), ALU.subtract).then_inc(s["sm_m"], 1)
                dve.wait_ge(*s("sm_e", 1))
                dve.tensor_reduce(stat[:, 32:32 + nt], av, AX.X, ALU.add)
                dve.drain()
                dve.reciprocal(stat[:, 32:32 + nt], stat[:, 32:32 + nt])
                dve.drain()
                TTR(av, av, stat[:, 32:32 + nt].unsqueeze(2).to_broadcast([P, nt, E]), ALU.mult).then_inc(s["aff"], 1)
                dve.wait_ge(*s("affT", 1))
                dve.tensor_copy(affT[0:E, tl * P:TOK], PS[0:E, 5:8, :].rearrange("p b n -> p (b n)")[:, tl * P:TOK])
                dve.drain()
                for src0, vv, ii, ff, cap, base in (
                        [(CTX, vals, idx8, idxf, CAP_L, CTX)] + ([(0, valc, idc8, idcf, CAP_C, 0)] if l == 0 else [])):
                    n = SEQ if src0 else CTX
                    cur = affT[0:E, src0:src0 + n]
                    for r in range(cap // 8):
                        o8 = vv[0:E, r * 8:(r + 1) * 8]
                        dve.max(o8, cur)
                        dve.drain()
                        dve.max_index(ii[0:E, r * 8:(r + 1) * 8], o8, cur)
                        if r < cap // 8 - 1:
                            nx = wk[0:E, 0:n]
                            dve.drain()
                            dve.match_replace(nx, o8, cur, -1.0)
                            dve.drain()
                            cur = nx
                    dve.drain()
                    dve.tensor_scalar(ff[0:E, :], ii[0:E, :], float(base), None, ALU.add)
                    dve.drain()
                dve.drain().then_inc(s["topk"], 1)
                dve.wait_ge(*s("sel", 1))
                dve.tensor_copy(idxT[:, 0, :], PS[:, 2, 0:E])
                m = dve.tensor_copy(affS[:, 0, :], PS[:, 2, E:2 * E])
                if l == 0:
                    dve.tensor_copy(idxT[0:CAP_C, 1, :], PS[0:CAP_C, 2, 2 * E:3 * E])
                    m = dve.tensor_copy(affS[0:CAP_C, 1, :], PS[0:CAP_C, 2, 3 * E:4 * E])
                m.then_inc(s["sel_cp"], 1)
                if l + 1 < DEPTH:
                    ada_scales(l + 1)
                dve.wait_ge(*s("m5_in", 32))
                dve.drain()

                N = NN[l]

                def stage(e, j, sem):
                    m = dve.tensor_copy(icur[:, j:j + 1], idxT[:, 0, ds(e, 1)])
                    if l == 0:
                        m = dve.tensor_copy(icur[0:CAP_C, j + 1:j + 2], idxT[0:CAP_C, 1, ds(e, 1)])
                    m.then_inc(s[sem], 1)

                def rows_d(e):
                    dve.wait_ge(*s("xgT", 2 * e + 2))
                    if not (isinstance(e, int) and e == 0):
                        dve.wait_ge(*s("au", e * 8))
                    for k in range(4, 8):
                        m = dve.tensor_scalar(xgT[:, k, 0:P], PS[:, 1, (k - 4) * P:(k - 3) * P], modT[:, l, 0, 4, k:k + 1],
                                              modT[:, l, 0, 3, k:k + 1], ALU.mult, ALU.add)
                    m.then_inc(s["xd"], 1)

                def rows_out(e):
                    if not (isinstance(e, int) and e == 0):
                        dve.wait_ge(*s("sc", e * 16 * (2 - l)))
                    stage(e, 2, "stage_s")
                    for r in range(2):
                        if l == 0:
                            dve.wait_ge(*s("bk", 2 * e + r + 1))
                        else:
                            dve.wait_ge(*s("yt", 8 * e + 4 * r + 4))
                        dve.scalar_tensor_tensor(out=Y[:, r * 512:(r + 1) * 512], in0=PS[:, ((7, 0), (5, 6))[l][r], :], scalar=affS[:, 0, ds(e, 1)],
                                                 in1=m5b[:, 0, r * 512:(r + 1) * 512], op0=ALU.mult, op1=ALU.mult).then_inc(s["ylat"], 1)
                        if l == 0:
                            dve.scalar_tensor_tensor(out=Yc[0:CAP_C, r * 512:(r + 1) * 512], in0=PS[0:CAP_C, 1 + r, :],
                                                     scalar=affS[0:CAP_C, 1, ds(e, 1)], in1=m5b[0:CAP_C, 1, r * 512:(r + 1) * 512],
                                                     op0=ALU.mult, op1=ALU.mult).then_inc(s["yctx"], 1)

                def expert(e, last):
                    first = isinstance(e, int) and e == 0
                    if not last:
                        dve.wait_ge(*s("gat", (e + 1) * 16 * (2 - l)))
                        stage(e + 1, 0, "stage_g")
                    for f in range(KD):
                        dve.wait_ge(*s("sil", e * 8 + f + 1))
                        TTR(actT[:, f, 0:N], silb[:, f % 2, 0:N], PS[:, 3 + f % 2, N:2 * N], ALU.mult).then_inc(s["act"], 1)
                        if f == 1 and l == 0 and not first:
                            rows_out(e - 1)
                    if not last:
                        rows_d(e + 1)
                    for d in range(1, KD if l == 0 else 0, 2):
                        dve.wait_ge(*s("yt", e * 8 + d + 1))
                        if d == 1 and not first:
                            dve.wait_ge(*s("bk", 2 * e))
                        dve.tensor_copy(yT[:, d, 0:N], PS[:, 6, 0:N]).then_inc(s["yc_d"], 1)
                    if l:
                        rows_out(e)
                stage(0, 0, "stage_g")
                rows_d(0)
                with_first(dve, expert)
                if l == 0:
                    rows_out(E - 1)

                if l < DEPTH - 1:
                    continue
                dve.wait_ge(*s("gb2_in", 32))
                with dve.Fori(0, NPAIR[l]) as i:
                    for u in range(2):
                        n = i * 2 + u
                        dve.wait_ge(*s(f"z_in{u}", (i + 1) * 16))
                        for h in range(2):
                            dve.bn_stats(stat[:, 32 + 6 * h:38 + 6 * h], z2[:, u, h * 512:(h + 1) * 512])
                        dve.drain()
                        dve.bn_aggr(stat[:, 26 + 2 * u:28 + 2 * u], stat[:, 32:44]).then_inc(s["st2"], 1)
                        dve.wait_ge(*s("sq2", n + 1))
                        dve.reciprocal(stat[:, 12 + 2 * u:13 + 2 * u], stat[:, 24 + u:25 + u])
                        dve.drain()
                        dve.tensor_scalar(stat[:, 13 + 2 * u:14 + 2 * u], stat[:, 26 + 2 * u:27 + 2 * u], stat[:, 12 + 2 * u:13 + 2 * u], -1.0,
                                          ALU.mult, ALU.mult).then_inc(s["rs2"], 1)
                    for u in range(2):
                        n = i * 2 + u
                        dve.wait_ge(*s("n2", n + 1))
                        TTR(o2[:, u, :], o2[:, u, :], gb2[:, 0, :], ALU.mult)
                        dve.drain()
                        TTR(o2[:, u, :], o2[:, u, :], gb2[:, 1, :], ALU.add).then_inc(s["g2"], 1)

        @block.gpsimd
        def _(pool):
            def ada_stores(l):
                with pool.Fori(0, 6) as i:
                    for u in range(2):
                        pool.wait_ge(G["rowc"], l * 12 + i * 2 + u + 1)
                        dst = mod_d[l].rearrange("(v k) p -> v (k p)", v=2)[:, ds((i * 2 + u) * 512, 512)]
                        pool.dma_start(dst, adar[0:2, u, :]).then_inc(G[f"mod_st{u}"], 16)
            ada_stores(0)
            for l in range(DEPTH):
                s = L[l]
                pool.wait_ge(*s("mrg", 8 * NCH[l]))
                tl = TL[l][0]

                def take(t):
                    n = t - tl
                    if not (isinstance(n, int) and n == 0):
                        pool.wait_ge(*s("y", n))
                    pool.tensor_copy(mst, mrgT[:, :, ds(t * P, P)]).then_inc(s["mst"], 1)

                def scale_x(t):
                    n = t - tl
                    pool.wait_ge(*s("x1", n + 1))
                    if not (isinstance(n, int) and n == 0):
                        pool.wait_ge(*s("z_st", 16 * n))
                    pool.nop(nofuse=True)
                    pool.tensor_scalar(zs, x1t, ALPHA, None, ALU.mult).then_inc(s["z_set"], 1)
                take(tl)
                if l == 0:
                    take(1)
                    scale_x(0)
                    take(2)
                    scale_x(1)
                with pool.Fori(TC + 1, TT) as t:
                    take(t)
                    scale_x(t - 1)
                scale_x(TT - 1)
                if l + 1 < DEPTH:
                    ada_stores(l + 1)

                pool.wait_ge(*s("x1_st", 16 * NT[l]))
                pool.wait_ge(*s("z_st", 16 * NT[l]))
                pool.wait_ge(*s("y", NT[l]))

                def gather(e):
                    pool.wait_ge(*s("stage_g", e + 1))
                    if not (isinstance(e, int) and e == 0):
                        pool.wait_ge(*s("xgT", 2 * e))
                    pool.nop(nofuse=True)
                    pool.indirect_dma_start(out=xg, out_offset=None, in_=x1_d,
                                            in_offset=bass.IndirectOffsetOnAxis(ap=icur[:, 0:1], axis=0)).then_inc(s["gat"], 16)
                    if l == 0:
                        pool.nop(nofuse=True)
                        pool.indirect_dma_start(out=xgc[0:CAP_C, :], out_offset=None, in_=x1_d,
                                                in_offset=bass.IndirectOffsetOnAxis(ap=icur[0:CAP_C, 1:2], axis=0)).then_inc(s["gat"], 16)

                def scatter(e):
                    pool.wait_ge(*s("stage_s", e + 1))
                    pool.wait_ge(*s("ylat", 2 * e + 2))
                    if not (isinstance(e, int) and e == 0):
                        pool.wait_ge(*s("sc", e * 16 * (2 - l)))
                    pool.nop(nofuse=True)
                    pool.indirect_dma_start(out=z_d, out_offset=bass.IndirectOffsetOnAxis(ap=icur[:, 2:3], axis=0), in_=Y,
                                            in_offset=None, compute_op=ALU.add).then_inc(s["sc"], 16)
                    if l == 0:
                        pool.wait_ge(*s("yctx", 2 * e + 2))
                        pool.nop(nofuse=True)
                        pool.indirect_dma_start(out=z_d, out_offset=bass.IndirectOffsetOnAxis(ap=icur[0:CAP_C, 3:4], axis=0),
                                                in_=Yc[0:CAP_C, :], in_offset=None, compute_op=ALU.add).then_inc(s["sc"], 16)

                def expert(e, last):
                    if not last:
                        gather(e + 1)
                    if not (isinstance(e, int) and e == 0):
                        scatter(e - 1)
                gather(0)
                with_first(pool, expert)
                scatter(E - 1)

                pool.wait_ge(*s("sc", 16 * E * (2 - l)))
                pool.dma_start(gb2[:, 0, :], a["ln2_g"][l:l + 1, :].to_broadcast([P, D])).then_inc(s["gb2_in"], 16)
                pool.dma_start(gb2[:, 1, :], a["ln2_b"][l:l + 1, :].to_broadcast([P, D])).then_inc(s["gb2_in"], 16)
                if l == 0:
                    pool.dma_start(z2[:, 0, :], z_d[0:P, :]).then_inc(s["z_in0"], 16)
                    with pool.Fori(1, TT) as t:
                        pool.wait_ge(*s("n2", t))
                        pool.dma_start(z2[:, 0, :], z_d[ds(t * P, P), :]).then_inc(s["z_in0"], 16)
                else:
                    for u in range(2):
                        pool.dma_start(z2[:, u, :], z_d[(tl + u) * P:(tl + u + 1) * P, :]).then_inc(s[f"z_in{u}"], 16)
                    with pool.Fori(0, NPAIR[l] - 1) as i:
                        for u in range(2):
                            pool.wait_ge(*s("n2", i * 2 + u + 1))
                            pool.dma_start(z2[:, u, :], z_d[ds((i * 2 + u + 2 + tl) * P, P), :]).then_inc(s[f"z_in{u}"], 16)


_INS = ["x", "c", "ctx", "c_ctx", "w_ada", "b_ada", "w_in", "attn_sink", "mla_q_norm", "mla_kv_norm", "w_uq", "w_ukv",
        "w_oa", "w_ob", "w_out", "ln1_g", "ln1_b", "w_router", "w_exp_gate", "w_exp_up", "w_exp_down", "ln2_g", "ln2_b"]


def _tables():
    n = np.arange(SEQ)
    pos = np.stack([n // GRID_W, n % GRID_W], 1).astype(np.float32)
    cols = []
    for dim in (WD, ROPE):
        nf = dim // 4
        inv = np.power(np.float32(THETA), -np.arange(nf, dtype=np.float32) / np.float32(nf)).astype(np.float32)
        ang = pos[:, :, None] * inv
        c, s = np.cos(ang), np.sin(ang)
        cols.append(np.stack([c, c], 2).reshape(SEQ, dim))
        cols.append(np.stack([-s, s], 2).reshape(SEQ, dim))
    lat = np.concatenate(cols, 1)
    still = np.concatenate([np.ones((CTX, WD)), np.zeros((CTX, WD)), np.ones((CTX, ROPE)), np.zeros((CTX, ROPE))], 1)
    rope = np.concatenate([still, lat], 0).astype(np.float32)
    i, j = np.arange(P)[:, None], np.arange(P)[None, :]
    off = NEG / WSCALE
    prev = np.where(j >= i, 0.0, off)
    nxt = np.where(j <= i, 0.0, off)
    z = np.zeros((P, P))
    mask = np.concatenate([z, z, prev, z, nxt], 1).astype(np.float32)
    full = np.full((P, P), off)
    edge = np.stack([np.stack([full, prev, prev, prev]), np.stack([nxt, nxt, nxt, full])]).astype(np.float32)
    return {"ident": np.eye(P, dtype=np.float32), "rope": rope, "wmask": mask, "edge": edge}


def kernel(**inputs):
    import numpy as _np
    import concourse.bacc as _bacc
    from concourse import mybir as _mybir
    from concourse.bass_utils import run_bass_kernel_spmd as _run

    nc = _bacc.Bacc("TRN2", target_bir_lowering=False, num_devices=1)
    arrays, args = {}, {}
    everything = {n: _np.ascontiguousarray(inputs[n]) for n in _INS}
    everything.update(_tables())
    for name, v in everything.items():
        arrays[f"in_{name}"] = v
        args[name] = nc.dram_tensor(f"in_{name}", v.shape, _mybir.dt.from_np(v.dtype), kind="ExternalInput").ap()
    out = nc.dram_tensor("out_0", (1, SEQ, D), F32, kind="ExternalOutput").ap()
    build(nc, args, out)
    r = _run(nc, [arrays], core_ids=[0])
    return r.results[0]["out_0"]
```

```python
from contextlib import ExitStack

import concourse.bass as bass
import numpy as np
from concourse import mybir

F32 = mybir.dt.float32
U32 = mybir.dt.uint32
ALU = mybir.AluOpType
ACT = mybir.ActivationFunctionType
AX = mybir.AxisListType

P = 128
D = 1024
KD = D // P
CTX, SEQ = 256, 1024
TOK = CTX + SEQ
TC, TT = CTX // P, TOK // P
DEPTH = 2
GRID_W = 64
WH, WKV, WD = 8, 2, 64
MH, NOPE, ROPE, MV = 8, 64, 32, 64
QR, KVR = 384, 256
MQ = NOPE + ROPE
E, FF = 16, 1024
CAP_L, CAP_C = 2 * SEQ // E, 2 * CTX // E
THETA = 10000.0
LN_EPS, RMS_EPS, NEG = 1e-5, 1e-6, -1e30
ALPHA = float((2 * DEPTH) ** 0.25)
WSCALE = float(WD ** -0.5)
MSCALE = float(MQ ** -0.5)
C_KA, C_CKV, C_KR, C_QA, C_CQ, C_G = 0, 256, 512, 544, 1056, 1440
NPJ = C_G


def ds(i, n):
    return slice(i, i + n) if isinstance(i, int) else bass.ds(i, n)


class Sems:

    def __init__(self, sems, before=None):
        self.sems, self.before = sems, before or {}

    def __getitem__(self, name):
        return self.sems[name]

    def __call__(self, name, n):
        return self.sems[name], n + self.before.get(name, 0)


def layer_counts(tiles, chunks, tr, ctx):
    pairs, g = tiles // 2, 1 + ctx
    n = dict(wp_in=14 * 16, q_in0=pairs * 32, q_in1=pairs * 32, mk_in0=pairs * 16, mk_in1=pairs * 16, m_in=32, tr=tr, pt=tr, pv=pairs * 32, hT_in0=16, hT_in1=16, hT_in2=16, mw_in0=KD * 32, mw_in1=KD * 32,
             wo_in=16, lnc_in=5 * 16, m5_in=32, z_in0=16 * tiles, z_in1=0, gb2_in=32, out_st=16 * tiles)
    n |= {f"ring{i}": 16 * E * (2 if i < 4 else 1) for i in range(8)}
    n |= {k: 16 * TT for k in "x_in h_st qW_st qM_st".split()}
    n |= {k: TT for k in "h_a h_d p1 p2 p0 rms rstd norm latT latc_a latc_d used_d ropeW kr kn qro tW qW_cp ka_cp".split()}
    n |= {k: 2 * TT for k in "xT ukv uq tK tQ kT_cp qM_cp".split()}
    n |= {k: 16 * pairs for k in "sM sW mxM mxW pM pW".split()}
    n |= {k: KD * chunks for k in "g sg mrg".split()}
    n |= {k: 16 * tiles for k in "xr_in x1_st z_st".split()}
    n |= {k: tiles for k in "es tot y y_mid y_used lnv lnr lnb lnn x1 h2a h2d zs z_set rt rt_cp st2 sq2 rs2 n2 g2".split()}
    n |= {k: 2 * tiles for k in "osb fT fcp x1T mst".split()}
    n |= {k: 1 for k in "sm_m sm_e aff affT topk sel sel_cp".split()}
    n |= {k: E for k in "stage_g stage_s xa xd".split()}
    n |= {k: 16 * E * g for k in "gat sc".split()}
    n |= {k: 8 * E for k in "au sil act yt".split()}
    n |= {k: 4 * E for k in "yc_a yc_d".split()}
    n |= {k: 2 * E for k in "xgT bk ylat".split()}
    n["yctx"] = 2 * E * ctx
    return n


def build(nc, a, out):
    with ExitStack() as ctx:
        def dram(name, shape):
            return nc.dram_tensor(name, shape, F32, kind="Internal").ap()

        mod_d = dram("mod_rows", (DEPTH, 96, P))
        hT_d = dram("h_transposed", (P, KD, TOK))
        qM_d = dram("q_latent_attn", (TT, MQ, MH * P))
        qW_d = dram("q_window", (TT, P, 4 * P))
        x1_d = dram("x_mid", (TOK, D))
        z_d = dram("moe_sum", (TOK, D))
        xs_d = dram("x_next", (TOK, D))

        WORDS = 53200
        arena = ctx.enter_context(nc.sbuf_tensor("arena", [P, WORDS], F32))
        PS = ctx.enter_context(nc.psum_tensor("PS", [P, 8, 512], F32))

        def at(off, *dims):
            n = int(np.prod(dims))
            assert off + n <= WORDS, (off, dims)
            v = arena[:, off:off + n]
            if len(dims) == 1:
                return v
            names = "abcd"[:len(dims)]
            return v.rearrange(f"p ({' '.join(names)}) -> p {' '.join(names)}", **{c: d for c, d in zip(names, dims)})

        ident = at(0, P)
        modT = at(128, DEPTH, 2, 6, KD)
        silc = at(320, 2, KD)
        gcol = at(336, DEPTH, 5)
        epsc = at(346, 2)
        sinks = at(352, DEPTH, 2, WH)
        stat = at(384, 96)
        ones1 = at(480, 2)
        R = 512
        RING, SLOT = 12, KD * 256
        O = R + RING * SLOT
        adaw = [at(O, 2, KD, 512), at(R + 3 * SLOT, 2, KD, 512)]
        adab = [at(O + 8192, 2, 512), at(R + 11 * SLOT, 2, 512)]
        adar = at(O + 9216, 2, 512)
        crow = at(O + 18900, P)
        mrow = at(O + 18600, DEPTH, P)
        w_pj = at(R, KD, NPJ)
        w_uq = at(R + 11520, 3, MH * MQ)
        w_ukv = at(R + 13824, 2, MH * (NOPE + MV))
        hts = at(R + 15872, KD, P)
        xb = at(R + 16896, D)
        rW = at(R + 17920, 10, WD)
        rC = at(R + 18560, 10, WD)
        latn = at(R + 19200, KVR + QR)
        latTt = at(R + 19840, 5, P)
        ksb = at(R + 20480, MH, MQ)
        qsb = at(R + 21248, MH, MQ)
        qWs = at(R + 22016, 4, P)
        qMs = at(R + 22528, MH, P)
        tmpm = at(R + 23552, 4, ROPE)
        junk = at(R + 23680, QR)
        krr = at(R + 24064, ROPE)
        krt = at(R + 24096, ROPE)
        kT = at(O, MH, TOK)
        V = at(O + 10240, TT, MH * MV)
        kaZ = at(O + 15360, WKV, TOK + P)
        va = at(O + 18176, TT + 1, WKV * WD)
        tabs = at(O + 25728, TT, 192)
        oaT = at(R, 4, TOK)
        obT = at(R + 5120, 4, TOK)
        PM = at(R + 10240, 1280)
        PW = at(R + 11520, 640)
        PTM = at(R + 12160, 10, P)
        PTW = at(R + 13440, 5, P)
        qMt = at(R + 15360, 2, MH, P)
        qWt = at(R + 17408, 2, 4, P)
        mask = at(R + 18432, 2, 640)
        osb = at(R + 19712, 2, 512)
        hTr = at(O, KD, TOK)
        mrgT = at(O + 10240, KD, TOK)
        mwt = at(O + 20480, 2, 24, P)
        sg = at(R + 10240, 2, 2, 512)
        w_o = at(R + 14336, KD, D)
        xr = at(O, D)
        zt = at(O + 1024, D)
        xn = at(O + 2048, D)
        x1t = at(O + 3072, D)
        mst = at(O + 4096, KD, P)
        h2t = at(O + 5120, KD, P)
        zs = at(O + 6144, D)
        gb1 = at(O + 7168, 2, D)
        m2b = at(O + 20480, 2, D)
        wrt = at(O + 22528, KD, E)
        logit = at(O + 22656, TT, E)
        afft = at(O + 22816, TT, E)
        affT = at(O + 23040, TOK)
        wk = at(O + 24320, SEQ)
        vals = at(O + 25344, CAP_L)
        idx8 = at(O + 25472, CAP_L).bitcast(U32)
        idxf = at(O + 25600, CAP_L)
        valc = at(O + 25728, CAP_C)
        idc8 = at(O + 25760, CAP_C).bitcast(U32)
        idcf = at(O + 25792, CAP_C)
        idxT = at(O + 25824, 2, E).bitcast(U32)
        affS = at(O + 25856, 2, E)
        icur = at(O + 25888, 4).bitcast(U32)
        xg = at(O + 10240, D)
        xgc = at(O + 11264, D)
        xgT = at(O + 12288, KD, 160)
        actT = at(O + 13568, KD, 160)
        yT = at(O + 14848, KD, 160)
        Y = at(O + 16128, D)
        Yc = at(O + 17152, D)
        silb = at(O + 18176, 2, 160)
        m5b = at(O + 26000, 2, D)
        ring = at(R, RING, KD, 256)
        z2 = at(O + 19584, 2, D)
        o2 = at(O + 21632, 2, D)
        gb2 = at(O + 23680, 2, D)

        TL = [list(range(TT)), list(range(TC, TT))]
        NT = [len(t) for t in TL]
        NPAIR = [n // 2 for n in NT]
        CH = [[(0, 256), (256, 512), (768, 512)], [(256, 512), (768, 512)]]
        NCH = [len(c) for c in CH]
        NN = [CAP_L + CAP_C, CAP_L]

        def sems(names):
            return {n: ctx.enter_context(nc.semaphore(n)) for n in names}
        G = Sems(sems("const_in cond_in cT silc ada_in0 ada_in1 ada rowc mod_st0 mod_st1 modr_in modT modT_cp mod1 bars".split()))
        counts = layer_counts(TT, NCH[0], 32 + 4 * 80, 1)
        own = sems(counts)
        L = [Sems(own), Sems(own, counts)]
        block = ctx.enter_context(nc.Block())

        def x_rows(l, t):
            if l:
                return xs_d[ds(t * P, P), :]
            if isinstance(t, int) and t < TC:
                return a["ctx"][0, t * P:(t + 1) * P, :]
            return a["x"][0, ds((t - TC) * P, P), :]

        def tiles(eng, body, first=0):
            for t in range(first, TC):
                body(t, t, False)
            with eng.Fori(TC, TT - 1) as t:
                body(t, t, False)
            body(TT - 1, TT - 1, True)

        def kind(t):
            return 1 if isinstance(t, int) and t < TC else 0

        def mod_bc(l, v, part):
            r = (v * 6 + part) * KD
            return mod_d[l, r:r + KD, :].rearrange("(o k) p -> o (k p)", o=1).to_broadcast([P, D])

        def pairs(eng, l, body):
            body(0, 0 if l == 0 else TC, None if l == 0 else 0)
            with eng.Fori(l, 4) as i:
                body(i + 1 - l, TC + i * 2, i)

        def led_pairs(eng, l, lead, body):
            lead(0, None if l == 0 else 0)
            if l == 0:
                body(0, 0, None, 0)
            with eng.Fori(0, 3) as i:
                body(i + 1 - l, TC + i * 2, i, i + 1)
            body(4 - l, TC + 6, 3, None)

        HEADS = [(j // 8, j % 8) for j in range(16)] + [(0, 0)]

        def nchunks(k, full):
            return (3, 2)[k] if full else 1

        def chunk_count(j, k, full):
            return j * (nchunks(0, full) + nchunks(1, full)) + k * nchunks(0, full)

        def chunks_before(l, p, lp):
            if lp is None:
                return 0
            return p * 80 if l else (p - 1) * 80 + 32

        def peeled(eng, n, body):
            body(0)
            with eng.Fori(1, n) as i:
                body(i)

        def with_first(eng, body):
            body(0, False)
            body(1, False)
            with eng.Fori(2, E - 1) as e:
                body(e, False)
            body(E - 1, True)

        @block.sync
        def _(sp):
            def ld(dst, src, sem):
                sp.dma_start(dst, src).then_inc(sem, 16)

            ld(ident, a["ident"], G["const_in"])
            ld(crow[0:8, :], a["c"].rearrange("b (k p) -> (b k) p", p=P), G["cond_in"])
            ld(crow[8:16, :], a["c_ctx"].rearrange("(k p) -> k p", p=P), G["cond_in"])
            for l in range(DEPTH):
                with nc.allow_non_contiguous_dma(reason="five short columns"):
                    ld(gcol[:, l, 0:2], a["mla_kv_norm"][l].rearrange("(k p) -> p k", p=P), G["const_in"])
                    ld(gcol[:, l, 2:5], a["mla_q_norm"][l].rearrange("(k p) -> p k", p=P), G["const_in"])
                ld(sinks[:, l, 0, :], a["attn_sink"][l:l + 1, :].to_broadcast([P, WH]), G["const_in"])

            def proj_weights(l):
                w = a["w_in"][l].rearrange("(k p) n -> p k n", p=P)
                parts = []
                for j in range(4):
                    for g in range(2):
                        c0 = C_QA + (g * 4 + j) * WD
                        parts.append((w_pj[:, :, (2 * j + g) * WD:(2 * j + g + 1) * WD], w[:, :, c0:c0 + WD]))
                parts.append((w_pj[:, :, 512:1024], w[:, :, C_KA:C_KR]))
                parts.append((w_pj[:, :, 1024:1408], w[:, :, C_CQ:C_G]))
                parts.append((w_pj[:, :, 1408:1440], w[:, :, C_KR:C_QA]))
                parts.append((w_uq, a["w_uq"][l].rearrange("(k p) n -> p k n", p=P)))
                parts.append((w_ukv, a["w_ukv"][l].rearrange("(k p) n -> p k n", p=P)))
                return parts

            def ada_chunk(l, i):
                for u in range(2):
                    j = l * 12 + i * 2 + u
                    if not isinstance(j, int) or j >= 2:
                        sp.wait_ge(G["ada"], j - 1)
                    cols = ds((i * 2 + u) * 512, 512)
                    ld(adaw[l][:, u], a["w_ada"][l].rearrange("(k p) n -> p k n", p=P)[:, :, cols], G[f"ada_in{u}"])
                    ld(adab[l][0:1, u, :], a["b_ada"][l:l + 1, cols], G[f"ada_in{u}"])

            def ada_rows(l):
                sp.wait_ge(G["mod_st0"], 16 * 6 * (l + 1))
                sp.wait_ge(G["mod_st1"], 16 * 6 * (l + 1))
                ld(mrow[0:96, l, :], mod_d[l], G["modr_in"])

            w = proj_weights(0)
            for i in range(6):
                ada_chunk(0, i)
                for dst, src in w[i * len(w) // 6:(i + 1) * len(w) // 6]:
                    ld(dst, src, L[0]["wp_in"])
            ld(xb, x_rows(0, 0), L[0]["x_in"])

            for l in range(DEPTH):
                s = L[l]
                if l:
                    sp.wait_ge(*L[l - 1]("au", 8 * E))
                    for dst, src in proj_weights(l):
                        ld(dst, src, s["wp_in"])
                    sp.wait_ge(*L[l - 1]("sc", 32 * E))
                ld(tabs, a["rope"].rearrange("(t p) n -> p t n", p=P), s["wp_in"])
                if l == 0:
                    ada_rows(0)
                w = a["w_in"][l].rearrange("(k p) n -> p k n", p=P)

                def keep_x(t):
                    sp.wait_ge(*L[0]("g2", t + 1))
                    ld(xs_d[ds(t * P, P), :], xb, L[0]["out_st"])
                if l:
                    keep_x(0)

                def step(t, n, last):
                    sp.wait_ge(*s("h_a", t + 1))
                    sp.wait_ge(*s("h_d", t + 1))
                    ld(hT_d[:, :, ds(t * P, P)], hts, s["h_st"])
                    if not last and l == 0:
                        sp.wait_ge(*s("xT", 2 * t + 2))
                        ld(xb, x_rows(l, t + 1), s["x_in"])
                    if not last and l:
                        keep_x(t + 1)
                    sp.wait_ge(*s("qW_cp", t + 1))
                    ld(qW_d[ds(t, 1)].rearrange("o p n -> (o p) n"), qWs.rearrange("p a b -> p (a b)"), s["qW_st"])
                    sp.wait_ge(*s("qM_cp", 2 * t + 2))
                    ld(qM_d[ds(t, 1)].rearrange("o p n -> (o p) n"), qMs[0:MQ].rearrange("p a b -> p (a b)"), s["qM_st"])
                tiles(sp, step)

                def q_tile(t0, u):
                    ld(qMt[0:MQ, u].rearrange("p a b -> p (a b)"), qM_d[ds(t0 + u, 1)].rearrange("o p n -> (o p) n"), s[f"q_in{u}"])
                    ld(qWt[:, u].rearrange("p a b -> p (a b)"), qW_d[ds(t0 + u, 1)].rearrange("o p n -> (o p) n"), s[f"q_in{u}"])
                sp.wait_ge(*s("h_st", 16 * TT))
                if l:
                    sp.wait_ge(*L[0]("out_st", 16 * TT))
                for u in range(2):
                    q_tile(TL[l][0], u)
                for u in range(2):
                    ld(mask[:, u, :], a["wmask"], s["m_in"])
                sp.wait_ge(*s("qM_st", 16 * TT))
                sp.wait_ge(*s("qW_st", 16 * TT))
                sp.wait_ge(*s("m_in", 32))

                def pair(p, t0, lp):
                    for u in range(2):
                        if not (isinstance(p, int) and p == 0):
                            sp.wait_ge(*s("sM", p * 16 - 8 + 8 * u))
                            sp.wait_ge(*s("sW", p * 16 - 8 + 8 * u))
                            sp.wait_ge(*s("mxW", p * 16 - 8 + 8 * u))
                            q_tile(t0, u)
                        if lp is None:
                            ld(mask[:, u, 256:384], a["edge"][0, 0], s[f"mk_in{u}"])
                        elif u == 0:
                            ld(mask[:, 0, 256:384], a["edge"][0, ds(lp, 1)].rearrange("o p n -> (o p) n"), s[f"mk_in{u}"])
                        else:
                            ld(mask[:, 1, 512:640], a["edge"][1, ds(lp, 1)].rearrange("o p n -> (o p) n"), s[f"mk_in{u}"])
                pairs(sp, l, pair)

                def weights(i):
                    for u in range(2):
                        f = i * 2 + u
                        if not isinstance(i, int):
                            sp.wait_ge(*s("g", (f - 1) * NCH[l]))
                        wg = w[:, :, C_G:C_G + 2 * D].rearrange("p k (g n) -> p k g n", g=2)
                        ld(mwt[:, u, 0:8, :], wg[:, :, 0, ds(f * P, P)], s[f"mw_in{u}"])
                        ld(mwt[:, u, 8:16, :], wg[:, :, 1, ds(f * P, P)], s[f"mw_in{u}"])
                        ld(mwt[:, u, 16:20, :], a["w_oa"][l].rearrange("(k p) n -> p k n", p=P)[:, :, ds(f * P, P)], s[f"mw_in{u}"])
                        ld(mwt[:, u, 20:24, :], a["w_ob"][l].rearrange("(k p) n -> p k n", p=P)[:, :, ds(f * P, P)], s[f"mw_in{u}"])
                weights(0)
                sp.wait_ge(*s("pv", 32 * NPAIR[l]))
                for ci, (c0, cn) in enumerate(CH[l]):
                    ld(hTr[:, :, c0:c0 + cn], hT_d[:, :, c0:c0 + cn], s[f"hT_in{ci}"])
                with sp.Fori(1, 4) as i:
                    weights(i)
                ld(w_o, a["w_out"][l].rearrange("(k p) n -> p k n", p=P), s["wo_in"])

                def ring_load(e, c):
                    if c < 8:
                        src, blk = a["w_exp_up" if c % 2 else "w_exp_gate"][l], c // 2
                    else:
                        src, blk = a["w_exp_down"][l], c - 8
                    v = src[ds(e, 1)].rearrange("o (k p) n -> p (o k) n", p=P)
                    ld(ring[:, c], v[:, :, blk * 256:(blk + 1) * 256], s[f"ring{c // 2 if c < 8 else c - 4}"])

                sp.wait_ge(*s("mrg", 8 * NCH[l]))
                ld(gb1[:, 0, :], a["ln1_g"][l:l + 1, :].to_broadcast([P, D]), s["lnc_in"])
                ld(gb1[:, 1, :], a["ln1_b"][l:l + 1, :].to_broadcast([P, D]), s["lnc_in"])
                for v in range(2):
                    ld(m2b[:, v, :], mod_bc(l, v, 2), s["lnc_in"])
                ld(wrt, a["w_router"][l].rearrange("(k p) e -> p k e", p=P), s["lnc_in"])
                for v in range(2):
                    ld(m5b[:, v, :], mod_bc(l, v, 5), s["m5_in"])
                ld(xr, x_rows(l, TL[l][0]), s["xr_in"])

                def step1(t, n, last):
                    n = t - TL[l][0]
                    if not last:
                        sp.wait_ge(*s("zs", n + 1))
                        ld(xr, x_rows(l, t + 1), s["xr_in"])
                    sp.wait_ge(*s("x1", n + 1))
                    ld(x1_d[ds(t * P, P), :], x1t, s["x1_st"])
                    sp.wait_ge(*s("z_set", n + 1))
                    ld(z_d[ds(t * P, P), :], zs, s["z_st"])
                ahead = 7 if l else 3
                for c in range(ahead):
                    ring_load(0, c)
                if l == 0:
                    ada_chunk(1, 0)
                tiles(sp, step1, TL[l][0])

                if l == 0:
                    with sp.Fori(1, 6) as i:
                        ada_chunk(1, i)
                    ada_rows(1)
                    sp.wait_ge(G["ada"], 24)
                sp.wait_ge(*s("y", NT[l]))
                for c in range(ahead, RING):
                    ring_load(0, c)

                def experts(e):
                    for c in range(RING):
                        if c < 8:
                            sp.wait_ge(*s("au", (e - 1) * 8 + (c // 2) * 2 + 2))
                        else:
                            sp.wait_ge(*s("yt", (e - 1) * 8 + (c - 8) * 2 + 2))
                        ring_load(e, c)
                with sp.Fori(1, E) as e:
                    experts(e)

        @block.tensor
        def _(pe):
            def mms(o, pairs_, start=True, stop=True):
                n = len(pairs_)
                for i, (lt, rh) in enumerate(pairs_):
                    m = pe.matmul(o, lt, rh, start=start and i == 0, stop=stop and i == n - 1)
                return m

            def tr(o, i):
                return pe.transpose(o, i, ident)

            pe.wait_ge(G["const_in"], 16 * 7)
            pe.wait_ge(G["cond_in"], 32)
            pe.matmul(PS[:, 7, 0:16], crow[0:16, :], ident[0:16, 0:16], start=True, stop=True).then_inc(G["cT"], 1)
            pe.wait_ge(G["silc"], 2)

            def ada_products(l, between=None):
                def chunk(i):
                    for u in range(2):
                        j = l * 12 + i * 2 + u
                        pe.wait_ge(G[f"ada_in{u}"], (l * 6 + i + 1) * 32)
                        if not isinstance(j, int) or j >= 2:
                            pe.wait_ge(G["rowc"], j - 1)
                        mms(PS[0:2, u, :], [(silc[:, :, k], adaw[l][:, u, k, :]) for k in range(KD)], stop=False)
                        pe.matmul(PS[0:2, u, :], ones1[0:1, :], adab[l][0:1, u, :], start=False, stop=True).then_inc(G["ada"], 1)
                chunk(0)
                with pe.Fori(1, 4) as i:
                    chunk(i)
                if between:
                    between()
                with pe.Fori(4, 6) as i:
                    chunk(i)
                pe.wait_ge(G["modr_in"], 16 * (l + 1))
                pe.matmul(PS[:, 3, 0:96], mrow[0:96, l, :], ident[0:96, 0:96], start=True, stop=True).then_inc(G["modT"], 1)
            ada_products(0)

            for l in range(DEPTH):
                s = L[l]

                def x_transposes(t):
                    if l:
                        pe.wait_ge(*L[0]("g2", t + 1))
                    else:
                        pe.wait_ge(*s("x_in", (t + 1) * 16))
                    for c in range(2):
                        for k in range(4):
                            m = tr(PS[:, 4 + c, k * P:(k + 1) * P], xb[:, (c * 4 + k) * P:(c * 4 + k + 1) * P])
                        m.then_inc(s["xT"], 1)

                if l == 0:
                    pe.wait_ge(G["mod1"], 1)
                x_transposes(0)
                pe.wait_ge(*s("wp_in", 16 * 14))

                def step(t, n, last):
                    pe.wait_ge(*s("h_a", t + 1))
                    pe.wait_ge(*s("h_d", t + 1))
                    if not (isinstance(t, int) and t == 0):
                        pe.wait_ge(*s("norm", t))
                        pe.wait_ge(*s("used_d", t))
                        pe.wait_ge(*s("ka_cp", t))
                    mms(PS[:, 1, :], [(hts[:, k, :], w_pj[:, k, 512:1024]) for k in range(KD)]).then_inc(s["p1"], 1)
                    kv_only = l == DEPTH - 1 and isinstance(t, int) and t < TC
                    q0 = 384 if kv_only else 0
                    mms(PS[:, 2, q0:416], [(hts[:, k, :], w_pj[:, k, 1024 + q0:1440]) for k in range(KD)]).then_inc(s["p2"], 1)
                    if kv_only:
                        pe.nop(nofuse=True).then_inc(s["p0"], 1)
                    else:
                        mms(PS[:, 0, :], [(hts[:, k, :], w_pj[:, k, 0:512]) for k in range(KD)]).then_inc(s["p0"], 1)
                    pe.wait_ge(*s("norm", t + 1))
                    if not (isinstance(t, int) and t == 0):
                        pe.wait_ge(*s("qW_cp", t))
                        pe.wait_ge(*s("qM_cp", 2 * t))
                        pe.wait_ge(*s("kT_cp", 2 * t))
                    for k in range(2):
                        tr(PS[:, 7, k * P:(k + 1) * P], latn[:, k * P:(k + 1) * P])
                    for k in range(1 if kv_only else 3):
                        m = tr(PS[:, 3, k * P:(k + 1) * P], latn[:, KVR + k * P:KVR + (k + 1) * P])
                    m.then_inc(s["latT"], 1)
                    if not last:
                        x_transposes(t + 1)
                    pe.wait_ge(*s("latc_a", t + 1))
                    mms(PS[:, 6, :], [(latTt[:, k, :], w_ukv[:, k, 512:1024]) for k in range(2)]).then_inc(s["ukv"], 1)
                    if not last:
                        pe.wait_ge(*s("h_d", t + 2))
                        pe.wait_ge(*s("h_a", t + 2))
                    mms(PS[:, 5, :], [(latTt[:, k, :], w_ukv[:, k, 0:512]) for k in range(2)]).then_inc(s["ukv"], 1)
                    pe.wait_ge(*s("latc_d", t + 1))
                    for h in range(2):
                        n = MQ if kv_only else 384
                        mms(PS[:, 3 + h, 0:n], [(latTt[:, 2 + k, :], w_uq[:, k, h * 384:h * 384 + n]) for k in range(1 if kv_only else 3)]).then_inc(s["uq"], 1)
                    pe.wait_ge(*s("ropeW", t + 1))
                    for k in range(4):
                        tr(PS[:, 7, k * P:(k + 1) * P], rW[:, 2 * k:2 * k + 2, :])
                    tr(PS[:, 1, 0:P], rW[:, 8:10, :]).then_inc(s["tW"], 1)
                    pe.wait_ge(*s("kr", t + 1))
                    pe.wait_ge(*s("kn", t + 1))
                    for g in (1, 0):
                        for h in range(4):
                            m = tr(PS[0:MQ, 5 + g, h * P:(h + 1) * P], ksb[:, g * 4 + h, :])
                        m.then_inc(s["tK"], 1)
                    pe.wait_ge(*s("qro", t + 1))
                    for g in range(2):
                        for h in range(4):
                            m = tr(PS[0:MQ, 3 + g, h * P:(h + 1) * P], qsb[:, g * 4 + h, :])
                        m.then_inc(s["tQ"], 1)
                tiles(pe, step)

                pe.wait_ge(*s("kT_cp", 2 * TT))
                pe.wait_ge(*s("qM_cp", 2 * TT))
                pe.wait_ge(*s("qW_cp", TT))
                pe.wait_ge(*s("ka_cp", TT))
                pe.wait_ge(*s("used_d", TT))

                def scores(p, lp, j, k):
                    u, h = HEADS[j]
                    full = lp is not None
                    cnt = p * 16 + j

                    def first():
                        if h == 0 and k == 0:
                            pe.wait_ge(*s(f"q_in{u}", (p + j // 16) * 32 + 32))
                        if j or not (isinstance(p, int) and p == 0):
                            pe.wait_ge(*s("mxW" if k else "pM", cnt))

                    parts = []
                    if k == 0:
                        nk = TOK if full else CTX
                        for b, c0 in enumerate(range(0, nk, 512)):
                            cn = min(512, nk - c0)
                            parts.append([(PS[:, b, 0:cn], kT[0:MQ, h, c0:c0 + cn])])
                        q = qMt[0:MQ, u, h, :]
                    else:
                        q = qWt[:, u, h % 4, :]
                        kz = kaZ[:, h // 4, :]
                        parts.append([(PS[:, 3, 0:CTX], kz[:, 0:CTX])])
                        if full:
                            parts[0].append((PS[:, 3, CTX:512], kz[:, ds((lp * 2 + u + 1) * P, 2 * P)]))
                            parts.append([(PS[:, 4, 0:P], kz[:, ds((lp * 2 + u + 3) * P, P)])])

                    def part(i):
                        if i == 0:
                            first()
                        for o, keys in parts[i]:
                            m = pe.matmul(o, q, keys, start=True, stop=True)
                        if i == len(parts) - 1:
                            m.then_inc(s["sW" if k else "sM"], 1)
                    return [lambda i=i: part(i) for i in range(len(parts))]

                def lead(p, lp):
                    for k in range(2):
                        for f in scores(p, lp, 0, k):
                            f()

                def pair(p, t0, lp, lp_next):
                    full = lp is not None
                    ch0 = chunks_before(l, p, lp)
                    start = isinstance(p, int) and p == 0

                    def transposes(j, k, c):
                        nkt = ((10, 5)[k]) if full else 2
                        cc = ch0 + chunk_count(j, k, full) + c
                        if j == 9 and k == 0 and c == 0:
                            pe.wait_ge(*s("fcp", p * 4 + 2))
                        if j == 0 and k == 0 and c == 0 and not start:
                            pe.wait_ge(*s("fcp", p * 4))
                        if c == 0:
                            pe.wait_ge(*s("pW" if k else "pM", p * 16 + j + 1))
                        if not (isinstance(cc, int) and cc == 0):
                            pe.wait_ge(*s("pt", cc))
                        for kt in range(c * 4, min(c * 4 + 4, nkt)):
                            m = tr(PS[:, 5, (kt - c * 4) * P:(kt - c * 4 + 1) * P], (PM, PW)[k][:, kt * P:(kt + 1) * P])
                        m.then_inc(s["tr"], 1)

                    def outputs(j, k):
                        u, h = HEADS[j]
                        nkt = ((10, 5)[k]) if full else 2
                        pe.wait_ge(*s("pt", ch0 + chunk_count(j, k, full) + nchunks(k, full)))
                        if h == 0 and not (start and u == 0):
                            pe.wait_ge(*s("osb", (p * 2 + u) * 2))
                        if k == 0:
                            vs = [V[:, kt, h * MV:(h + 1) * MV] for kt in range(nkt)]
                        else:
                            g = h // 4
                            vs = [va[:, kt, g * WD:(g + 1) * WD] for kt in range(2)]
                            if full:
                                vs += [va[:, ds(lp * 2 + u + 1 + i, 1), g * WD:(g + 1) * WD].rearrange("p o d -> p (o d)") for i in range(3)]
                        mms(PS[:, 6 + k, h * 64:(h + 1) * 64], [((PTM, PTW)[k][:, kt, :], vs[kt]) for kt in range(nkt)]).then_inc(s["pv"], 1)

                    def turn(u, j, kk):
                        pe.wait_ge(*s("osb", (p * 2 + u) * 2 + kk + 1))
                        pe.wait_ge(*s("pt", ch0 + chunk_count(j + 1, 0, full)))
                        if kk or u or not start:
                            pe.wait_ge(*s("fcp", (p * 2 + u) * 2 + kk))
                        for i in range(4):
                            m = tr(PS[:, 5, i * P:(i + 1) * P], osb[:, kk, i * P:(i + 1) * P])
                        m.then_inc(s["fT"], 1)

                    for j in range(16):
                        for k in range(2):
                            if j < 15:
                                nxt = scores(p, lp, j + 1, k)
                            else:
                                nxt = scores(p, lp_next, 16, k) if lp_next is not None else []
                            for c in range(max(nchunks(k, full), len(nxt))):
                                if c < nchunks(k, full):
                                    transposes(j, k, c)
                                if c < len(nxt):
                                    nxt[c]()
                        outputs(j, 0)
                        if j == 8:
                            turn(0, j, 0)
                        outputs(j, 1)
                        if j == 8:
                            turn(0, j, 1)
                        if j == 15:
                            turn(1, j, 0)
                            turn(1, j, 1)
                led_pairs(pe, l, lead, pair)

                def merge_block(i, u):
                    f = i * 2 + u
                    for ci, (c0, cn) in enumerate(CH[l]):
                        q = f * NCH[l] + ci
                        set_ = (u * NCH[l] + ci) % 2 * 4
                        if not isinstance(q, int) or q >= 2:
                            pe.wait_ge(*s("mrg", q - 1))
                        if ci == 0:
                            pe.wait_ge(*s(f"mw_in{u}", (i + 1) * 64))
                        if isinstance(q, int) and q == 0:
                            pe.wait_ge(*s("fcp", 4 * NPAIR[l]))
                        if isinstance(q, int) and q < 2:
                            todo = [(0, *CH[l][0]), (4, *CH[l][1])] if q == 0 else []
                        else:
                            todo = [(set_, c0, cn)]
                        for b0, d0, dn in todo:
                            mms(PS[:, b0, 0:dn], [(mwt[:, u, 16 + k, :], oaT[:, k, d0:d0 + dn]) for k in range(4)])
                            mms(PS[:, b0 + 1, 0:dn], [(mwt[:, u, 20 + k, :], obT[:, k, d0:d0 + dn]) for k in range(4)])
                        pe.wait_ge(*s(f"hT_in{ci}", 16))
                        mms(PS[:, set_ + 2, 0:cn], [(mwt[:, u, k, :], hTr[:, k, c0:c0 + cn]) for k in range(KD)])
                        mms(PS[:, set_ + 3, 0:cn], [(mwt[:, u, 8 + k, :], hTr[:, k, c0:c0 + cn]) for k in range(KD)]).then_inc(s["g"], 1)
                for u in range(2):
                    merge_block(0, u)
                with pe.Fori(1, 4) as i:
                    for u in range(2):
                        merge_block(i, u)

                pe.wait_ge(*s("mrg", 8 * NCH[l]))
                pe.wait_ge(*s("wo_in", 16))

                def y_half(t, c):
                    n = t - TL[l][0]
                    pe.wait_ge(*s("mst", 2 * n + c + 1))
                    if c == 0 and not (isinstance(n, int) and n == 0):
                        pe.wait_ge(*s("y_used", n))
                    for k in range(c * 4, c * 4 + 4):
                        for h in range(2):
                            m = pe.matmul(PS[:, h, :], mst[:, k, :], w_o[:, k, h * 512:(h + 1) * 512], start=k == 0, stop=k == KD - 1)
                    m.then_inc(s["y" if c else "y_mid"], 1)

                def x1_transposes(t):
                    n = t - TL[l][0]
                    pe.wait_ge(*s("x1", n + 1))
                    if not (isinstance(n, int) and n == 0):
                        pe.wait_ge(*s("h2a", n))
                        pe.wait_ge(*s("h2d", n))
                    for c in range(2):
                        for k in range(4):
                            m = tr(PS[:, 2 + c, k * P:(k + 1) * P], x1t[:, (c * 4 + k) * P:(c * 4 + k + 1) * P])
                        m.then_inc(s["x1T"], 1)

                def router(t):
                    n = t - TL[l][0]
                    if isinstance(n, int) and n == 0:
                        pe.wait_ge(*s("lnc_in", 16 * 5))
                    pe.wait_ge(*s("h2a", n + 1))
                    pe.wait_ge(*s("h2d", n + 1))
                    if not (isinstance(n, int) and n == 0):
                        pe.wait_ge(*s("rt_cp", n))
                    mms(PS[:, 4, 0:E], [(h2t[:, k, :], wrt[:, k, :]) for k in range(KD)]).then_inc(s["rt"], 1)

                def y_step(t):
                    y_half(t, 0)
                    if not isinstance(t, int) or t - TL[l][0] >= 2:
                        router(t - 2)
                    y_half(t, 1)
                    if not isinstance(t, int) or t - TL[l][0] >= 1:
                        x1_transposes(t - 1)
                for t in range(TL[l][0], TC + 2):
                    y_step(t)
                with pe.Fori(TC + 2, TT) as t:
                    y_step(t)
                router(TT - 2)
                x1_transposes(TT - 1)
                router(TT - 1)

                pe.wait_ge(*s("aff", 1))
                for i, t in enumerate(TL[l]):
                    m = tr(PS[0:E, 5 + t // 4, (t % 4) * P:(t % 4 + 1) * P], afft[:, t, :])
                m.then_inc(s["affT"], 1)

                def select():
                    pe.wait_ge(*s("topk", 1))
                    pe.matmul(PS[:, 2, 0:E], idxf[0:E, :], ident[0:E, 0:E], start=True, stop=True)
                    m = pe.matmul(PS[:, 2, E:2 * E], vals[0:E, :], ident[0:E, 0:E], start=True, stop=True)
                    if l == 0:
                        pe.matmul(PS[0:CAP_C, 2, 2 * E:3 * E], idcf[0:E, :], ident[0:E, 0:E], start=True, stop=True)
                        m = pe.matmul(PS[0:CAP_C, 2, 3 * E:4 * E], valc[0:E, :], ident[0:E, 0:E], start=True, stop=True)
                    m.then_inc(s["sel"], 1)
                if l + 1 < DEPTH:
                    pe.wait_ge(*s("y_used", NT[l]))
                    pe.wait_ge(*s("h2d", NT[l]))
                    ada_products(l + 1, select)
                else:
                    select()

                N = NN[l]

                def xg_transposes(e):
                    pe.wait_ge(*s("gat", (e + 1) * 16 * (2 - l)))
                    if l == 0 and not (isinstance(e, int) and e <= 1):
                        pe.wait_ge(*s("ylat", 2 * (e - 1)))
                        pe.wait_ge(*s("yctx", 2 * (e - 1)))
                    for c in range(2):
                        for k in range(4):
                            m = tr(PS[:, c, k * P:(k + 1) * P], xg[:, (c * 4 + k) * P:(c * 4 + k + 1) * P])
                        if l or c == 0:
                            m.then_inc(s["xgT"], 1)
                    if l == 0:
                        for k in range(KD):
                            m = pe.transpose(PS[:, 2, k * 32:(k + 1) * 32], xgc[0:CAP_C, k * P:(k + 1) * P], ident[0:CAP_C, 0:CAP_C])
                        m.then_inc(s["xgT"], 1)

                def back(e):
                    pe.wait_ge(*s("yc_a", e * 4 + 4))
                    pe.wait_ge(*s("yc_d", e * 4 + 4))
                    for r in range(2):
                        for j in range(4):
                            m = tr(PS[:, (7, 0)[r], j * P:(j + 1) * P], yT[:, r * 4 + j, 0:P])
                        for j in range(4):
                            m = pe.transpose(PS[0:CAP_C, 1 + r, j * P:(j + 1) * P], yT[:, r * 4 + j, P:P + CAP_C], ident)
                        m.then_inc(s["bk"], 1)

                def expert(e, last):
                    first = isinstance(e, int) and e == 0
                    pe.wait_ge(*s("xa", e + 1))
                    pe.wait_ge(*s("xd", e + 1))
                    for f in range(KD):
                        if f % 2 == 0:
                            pe.wait_ge(*s(f"ring{f // 2}", (e + 1) * 32))
                        if not (first and f < 2):
                            pe.wait_ge(*s("act", e * 8 + f - 1))
                        for h in range(2):
                            m = mms(PS[:, 3 + f % 2, h * N:(h + 1) * N],
                                    [(ring[:, (f // 2) * 2 + h, k, (f % 2) * P:(f % 2 + 1) * P], xgT[:, k, 0:N]) for k in range(KD)])
                        m.then_inc(s["au"], 1)
                        if f == 1 and l == 0 and not first:
                            back(e - 1)
                    if not last:
                        xg_transposes(e + 1)
                    pe.wait_ge(*s("act", (e + 1) * 8))
                    if l == 0:
                        for d in range(KD):
                            if d % 2 == 0:
                                pe.wait_ge(*s(f"ring{4 + d // 2}", (e + 1) * 16))
                            if not (first and d < 2):
                                pe.wait_ge(*s("yc_d" if d % 2 else "yc_a", e * 4 + d // 2))
                            mms(PS[:, 5 + d % 2, 0:N], [(ring[:, 8 + d // 2, k, (d % 2) * P:(d % 2 + 1) * P], actT[:, k, 0:N]) for k in range(KD)]).then_inc(s["yt"], 1)
                    else:
                        for c in range(4):
                            pe.wait_ge(*s(f"ring{4 + c}", (e + 1) * 16))
                            if c % 2 == 0 and not first:
                                pe.wait_ge(*s("ylat", 2 * e - 1 + c // 2))
                            mms(PS[:, 5 + c // 2, (c % 2) * 256:(c % 2 + 1) * 256],
                                [(actT[:, k, 0:P], ring[:, 8 + c, k, :]) for k in range(KD)]).then_inc(s["yt"], 2)
                pe.wait_ge(*s("sel_cp", 1))
                xg_transposes(0)
                with_first(pe, expert)
                if l == 0:
                    back(E - 1)

        @block.scalar
        def _(act):
            A = act.activation
            act.wait_ge(G["cT"], 1)
            A(silc.rearrange("p v k -> p (v k)"), PS[:, 7, 0:16], ACT.Silu).then_inc(G["silc"], 1)

            def ada_copies(l):
                def row(i):
                    for u in range(2):
                        j = l * 12 + i * 2 + u
                        act.wait_ge(G["ada"], j + 1)
                        if not isinstance(j, int) or j >= 2:
                            act.wait_ge(G[f"mod_st{u}"], (l * 6 + i) * 16)
                        A(adar[0:2, u, :], PS[0:2, u, :], ACT.Copy).then_inc(G["rowc"], 1)
                peeled(act, 6, row)
                act.wait_ge(G["modT"], l + 1)
                A(arena[:, 128 + 96 * l:224 + 96 * l], PS[:, 3, 0:96], ACT.Copy).then_inc(G["modT_cp"], 1)
            ada_copies(0)

            for l in range(DEPTH):
                s = L[l]

                def h_half(t, sem_val=None):
                    v = kind(t)
                    act.wait_ge(*s("xT", 2 * t + 1))
                    if not (isinstance(t, int) and t == 0):
                        act.wait_ge(*s("h_st", 16 * t))
                        act.wait_ge(*s("p0", t))
                    for k in range(4):
                        m = A(hts[:, k, :], PS[:, 4, k * P:(k + 1) * P], ACT.Identity,
                              scale=modT[:, l, v, 1, k:k + 1], bias=modT[:, l, v, 0, k:k + 1])
                    m.then_inc(s["h_a"], 1)

                def norm_x(t):
                    q = L[0]
                    act.wait_ge(*q("st2", t + 1))
                    A(stat[:, 24:25], stat[:, 27:28], ACT.Sqrt, bias=epsc[:, 0:1]).then_inc(q["sq2"], 1)
                    act.wait_ge(*q("rs2", t + 1))
                    A(o2[:, 0, :], z2[:, 0, :], ACT.Identity, scale=stat[:, 12:13], bias=stat[:, 13:14]).then_inc(q["n2"], 1)
                act.wait_ge(G["mod1"], 1 + l)
                act.wait_ge(G["bars"], 3)
                if l:
                    norm_x(0)
                h_half(0)

                def step(t, n, last):
                    if l and not last:
                        norm_x(t + 1)
                    act.wait_ge(*s("p1", t + 1))
                    A(junk[:, 0:KVR], PS[:, 1, 256:512], ACT.Square, accum_out=stat[:, 0:1])
                    act.drain()
                    act.wait_ge(*s("p2", t + 1))
                    A(junk[:, 0:QR], PS[:, 2, 0:QR], ACT.Square, accum_out=stat[:, 1:2])
                    act.drain()
                    A(stat[:, 2:3], stat[:, 0:1], ACT.Sqrt, scale=1.0 / KVR, bias=epsc[:, 1:2])
                    A(stat[:, 3:4], stat[:, 1:2], ACT.Sqrt, scale=1.0 / QR, bias=epsc[:, 1:2]).then_inc(s["rms"], 1)
                    act.wait_ge(*s("rstd", t + 1))
                    if not (isinstance(t, int) and t == 0):
                        act.wait_ge(*s("latT", t))
                    A(latn[:, 0:KVR], PS[:, 1, 256:512], ACT.Copy, scale=stat[:, 4:5])
                    A(latn[:, KVR:], PS[:, 2, 0:QR], ACT.Copy, scale=stat[:, 5:6]).then_inc(s["norm"], 1)
                    act.wait_ge(*s("latT", t + 1))
                    for k in range(2):
                        m = A(latTt[:, k, :], PS[:, 7, k * P:(k + 1) * P], ACT.Copy, scale=gcol[:, l, k:k + 1])
                    m.then_inc(s["latc_a"], 1)
                    if not last:
                        h_half(t + 1)
                    for i, g in enumerate((1, 0)):
                        act.wait_ge(*s("ukv", 2 * t + i + 1))
                        if i == 0 and not (isinstance(t, int) and t == 0):
                            act.wait_ge(*s("tK", 2 * t))
                        src = PS[:, 5 + g, :].rearrange("p (h c) -> p h c", h=4)
                        A(V[:, ds(t, 1), g * 256:(g + 1) * 256].rearrange("p o (h c) -> p (o h) c", h=4), src[:, :, NOPE:], ACT.Copy)
                        m = A(ksb[:, g * 4:(g + 1) * 4, 0:NOPE], src[:, :, 0:NOPE], ACT.Copy)
                    m.then_inc(s["kn"], 1)
                    act.wait_ge(*s("tW", t + 1))
                    if not (isinstance(t, int) and t == 0):
                        act.wait_ge(*s("qW_st", 16 * t))
                    A(qWs.rearrange("p a b -> p (a b)"), PS[:, 7, :], ACT.Copy).then_inc(s["qW_cp"], 1)
                    for i, g in enumerate((1, 0)):
                        act.wait_ge(*s("tK", 2 * t + i + 1))
                        A(kT[0:MQ, g * 4:(g + 1) * 4, ds(t * P, P)], PS[0:MQ, 5 + g, :].rearrange("p (h c) -> p h c", h=4), ACT.Copy).then_inc(s["kT_cp"], 1)
                tiles(act, step)

                def pair(p, t0, lp, lp_next, leading=False):
                    full = lp is not None
                    ch0 = chunks_before(l, p, lp)
                    start = isinstance(p, int) and p == 0

                    def expo(j, k):
                        u, h = HEADS[j]
                        wide = full or j == 16
                        act.wait_ge(*s("mxW" if k else "mxM", p * 16 + j + 1))
                        if k == 0:
                            nk = TOK if wide else CTX
                            if j or not start:
                                act.wait_ge(*s("tr", ch0 + (chunk_count(j - 1, 1, full) if j else 0)))
                            A(PM[:, 0:nk], PS[:, 0:3, :].rearrange("p b n -> p (b n)")[:, 0:nk], ACT.Exp, scale=MSCALE,
                              bias=stat[:, 32 + u * 8 + h:33 + u * 8 + h], accum_out=stat[:, 64 + u * 8 + h:65 + u * 8 + h]).then_inc(s["pM"], 1)
                        else:
                            nk = 640 if wide else CTX
                            A(PW[:, 0:nk], PW[:, 0:nk], ACT.Exp, bias=stat[:, 48 + u * 8 + h:49 + u * 8 + h],
                              accum_out=stat[:, 80 + u * 8 + h:81 + u * 8 + h]).then_inc(s["pW"], 1)

                    def copy_chunk(j, k, c):
                        nkt = ((10, 5)[k]) if full else 2
                        a0, a1 = c * 4, min(c * 4 + 4, nkt)
                        act.wait_ge(*s("tr", ch0 + chunk_count(j, k, full) + c + 1))
                        A((PTM, PTW)[k][:, a0:a1, :].rearrange("p a b -> p (a b)"), PS[:, 5, 0:(a1 - a0) * P], ACT.Copy).then_inc(s["pt"], 1)

                    def turn(u):
                        for kk in range(2):
                            act.wait_ge(*s("fT", (p * 2 + u) * 2 + kk + 1))
                            A((obT, oaT)[kk][:, :, ds((t0 + u) * P, P)], PS[:, 5, :].rearrange("p (a b) -> p a b", a=4), ACT.Copy).then_inc(s["fcp"], 1)

                    if leading:
                        expo(0, 0)
                        expo(0, 1)
                        return
                    for j in range(16):
                        copy_chunk(j, 0, 0)
                        if full:
                            copy_chunk(j, 0, 2)
                        copy_chunk(j, 1, 0)
                        if full:
                            copy_chunk(j, 1, 1)
                        if j < 15 or lp_next is not None:
                            expo(j + 1, 0)
                            expo(j + 1, 1)
                        if j in (7, 15):
                            act.wait_ge(*s("es", p * 2 + j // 8 + 1))
                            A(stat[:, 16:24], stat[:, 8:16], ACT.Exp).then_inc(s["tot"], 1)
                        if j in (8, 15):
                            turn(j // 15)
                led_pairs(act, l, lambda p, lp: pair(p, 0, lp, None, True), pair)

                def merge_block(f, u):
                    for ci, (c0, cn) in enumerate(CH[l]):
                        q = f * NCH[l] + ci
                        set_ = (u * NCH[l] + ci) % 2
                        act.wait_ge(*s("g", q + 1))
                        if not isinstance(f, int) or q >= 2:
                            act.wait_ge(*s("mrg", q - 1))
                        A(sg[:, set_, 0, 0:cn], PS[:, set_ * 4 + 2, 0:cn], ACT.Sigmoid)
                        A(sg[:, set_, 1, 0:cn], PS[:, set_ * 4 + 3, 0:cn], ACT.Sigmoid).then_inc(s["sg"], 1)
                for u in range(2):
                    merge_block(u, u)
                with act.Fori(1, 4) as i:
                    for u in range(2):
                        merge_block(i * 2 + u, u)

                def ln_a(t):
                    n = t - TL[l][0]
                    act.wait_ge(*s("lnv", n + 1))
                    A(stat[:, 7:8], stat[:, 9:10], ACT.Sqrt, bias=epsc[:, 0:1]).then_inc(s["lnr"], 1)
                    act.wait_ge(*s("lnb", n + 1))
                    A(xn, zt, ACT.Identity, scale=stat[:, 10:11], bias=stat[:, 11:12]).then_inc(s["lnn"], 1)
                    act.wait_ge(*s("x1", n + 1))
                    if not (isinstance(n, int) and n == 0):
                        act.wait_ge(*s("z_st", 16 * n))
                    A(zs, x1t, ACT.Copy, scale=ALPHA).then_inc(s["z_set"], 1)

                def tr_a(t):
                    n = t - TL[l][0]
                    v = kind(t)
                    act.wait_ge(*s("x1T", 2 * n + 1))
                    if not (isinstance(n, int) and n == 0):
                        act.wait_ge(*s("rt", n))
                    for k in range(4):
                        m = A(h2t[:, k, :], PS[:, 2, k * P:(k + 1) * P], ACT.Identity,
                              scale=modT[:, l, v, 4, k:k + 1], bias=modT[:, l, v, 3, k:k + 1])
                    m.then_inc(s["h2a"], 1)

                def logits_a(t):
                    act.wait_ge(*s("rt", t - TL[l][0] + 1))
                    A(logit[:, ds(t, 1), :].rearrange("p o e -> p (o e)"), PS[:, 4, 0:E], ACT.Copy).then_inc(s["rt_cp"], 1)

                def step_a(t):
                    if not isinstance(t, int) or t - TL[l][0] >= 2:
                        logits_a(t - 2)
                    if not isinstance(t, int) or t - TL[l][0] >= 1:
                        tr_a(t - 1)
                    ln_a(t)
                for t in range(TL[l][0], TC + 2):
                    step_a(t)
                with act.Fori(TC + 2, TT) as t:
                    step_a(t)
                logits_a(TT - 2)
                tr_a(TT - 1)
                logits_a(TT - 1)
                tl = TL[l][0]
                act.wait_ge(*s("sm_m", 1))
                A(afft[:, tl:TT, :], afft[:, tl:TT, :], ACT.Exp).then_inc(s["sm_e"], 1)
                if l + 1 < DEPTH:
                    ada_copies(l + 1)
                act.wait_ge(*s("sel", 1))

                N = NN[l]

                def rows_a(e):
                    act.wait_ge(*s("xgT", 2 * e + 1))
                    if not (isinstance(e, int) and e == 0):
                        act.wait_ge(*s("au", e * 8))
                    for k in range(4):
                        m = A(xgT[:, k, 0:P], PS[:, 0, k * P:(k + 1) * P], ACT.Identity,
                              scale=modT[:, l, 0, 4, k:k + 1], bias=modT[:, l, 0, 3, k:k + 1])
                    if l == 0:
                        act.wait_ge(*s("xgT", 2 * e + 2))
                        for k in range(KD):
                            m = A(xgT[:, k, P:N], PS[:, 2, k * 32:(k + 1) * 32], ACT.Identity,
                                  scale=modT[:, l, 1, 4, k:k + 1], bias=modT[:, l, 1, 3, k:k + 1])
                    m.then_inc(s["xa"], 1)

                def expert(e, last):
                    for f in range(KD):
                        act.wait_ge(*s("au", e * 8 + f + 1))
                        if not (isinstance(e, int) and e == 0 and f < 2):
                            act.wait_ge(*s("act", e * 8 + f - 1))
                        A(silb[:, f % 2, 0:N], PS[:, 3 + f % 2, 0:N], ACT.Silu).then_inc(s["sil"], 1)
                    if not last:
                        rows_a(e + 1)
                    for d in range(0, KD if l == 0 else 0, 2):
                        act.wait_ge(*s("yt", e * 8 + d + 1))
                        if d == 0 and not (isinstance(e, int) and e == 0):
                            act.wait_ge(*s("bk", 2 * e))
                        A(yT[:, d, 0:N], PS[:, 5, 0:N], ACT.Copy).then_inc(s["yc_a"], 1)
                rows_a(0)
                with_first(act, expert)

                if l < DEPTH - 1:
                    continue

                def norm_pair(i):
                    for u in range(2):
                        n = i * 2 + u
                        act.wait_ge(*s("st2", n + 1))
                        A(stat[:, 24 + u:25 + u], stat[:, 27 + 2 * u:28 + 2 * u], ACT.Sqrt, bias=epsc[:, 0:1]).then_inc(s["sq2"], 1)
                        act.wait_ge(*s("rs2", n + 1))
                        if u == 0 and not isinstance(i, int):
                            act.wait_ge(*s("out_st", i * 32))
                        A(o2[:, u, :], z2[:, u, :], ACT.Identity, scale=stat[:, 12 + 2 * u:13 + 2 * u], bias=stat[:, 13 + 2 * u:14 + 2 * u]).then_inc(s["n2"], 1)

                    for u in range(2):
                        n = i * 2 + u
                        act.wait_ge(*s("g2", n + 1))
                        act.dma_start(out[0, ds(n * P, P), :], o2[:, u, :]).then_inc(s["out_st"], 16)
                peeled(act, NPAIR[l], norm_pair)
            act.wait_ge(*L[DEPTH - 1]("out_st", 16 * NT[DEPTH - 1]))

        @block.vector
        def _(dve):
            def TTR(o, x, y, op):
                return dve.tensor_tensor(o, x, y, op)

            dve.memset(ones1, 1.0).then_inc(G["silc"], 1)
            dve.memset(epsc[:, 0:1], LN_EPS)
            dve.memset(epsc[:, 1:2], RMS_EPS).then_inc(G["bars"], 1)
            dve.wait_ge(G["const_in"], 16 * 7)
            for l in range(DEPTH):
                dve.tensor_scalar(sinks[:, l, 1, :], sinks[:, l, 0, :], -1.0, None, ALU.mult).then_inc(G["bars"], 1)

            def ada_scales(l):
                dve.wait_ge(G["modT_cp"], l + 1)
                for v in range(2):
                    for part in (1, 4):
                        m = dve.tensor_scalar(modT[:, l, v, part, :], modT[:, l, v, part, :], 1.0, None, ALU.add)
                m.then_inc(G["mod1"], 1)
            ada_scales(0)

            def rope(dst, src, table, h, half, tmp):
                w = 4 * half
                C = table[:, 0:w]
                S = table[:, w:2 * w]
                x = src.rearrange("p h (a s n) -> p h a s n", a=2, s=2)
                t = tmp.rearrange("p h (a s n) -> p h a s n", a=2, s=2)
                Sv = S.rearrange("p (a s n) -> p a s n", a=2, s=2)
                TTR(dst, src, C.unsqueeze(1).to_broadcast([P, h, w]), ALU.mult)
                for i in range(2):
                    if h == 1:
                        TTR(t[:, 0, :, i, :], x[:, 0, :, 1 - i, :], Sv[:, :, i, :], ALU.mult)
                    else:
                        TTR(t[:, :, :, i, :], x[:, :, :, 1 - i, :], Sv[:, :, i, :].unsqueeze(1).to_broadcast([P, h, 2, half]), ALU.mult)
                dve.drain()
                return TTR(dst, dst, tmp, ALU.add)

            for l in range(DEPTH):
                s = L[l]
                if l:
                    dve.wait_ge(*L[l - 1]("sc", 16 * E * 2))

                def zeros():
                    dve.memset(kaZ.rearrange("p a b -> p (a b)"), 0.0)
                    dve.memset(va[:, TT, :], 0.0)
                    dve.drain()

                def h_half(t):
                    v = kind(t)
                    dve.wait_ge(*s("xT", 2 * t + 2))
                    if not (isinstance(t, int) and t == 0):
                        dve.wait_ge(*s("h_st", 16 * t))
                        dve.wait_ge(*s("p0", t))
                    for k in range(4):
                        m = dve.tensor_scalar(hts[:, 4 + k, :], PS[:, 5, k * P:(k + 1) * P], modT[:, l, v, 1, 4 + k:5 + k],
                                              modT[:, l, v, 0, 4 + k:5 + k], ALU.mult, ALU.add)
                    m.then_inc(s["h_d"], 1)

                def norm_x(t):
                    q = L[0]
                    dve.wait_ge(*q("z_in0", (t + 1) * 16))
                    for h in range(2):
                        dve.bn_stats(stat[:, 32 + 6 * h:38 + 6 * h], z2[:, 0, h * 512:(h + 1) * 512])
                    dve.drain()
                    dve.bn_aggr(stat[:, 26:28], stat[:, 32:44]).then_inc(q["st2"], 1)
                    dve.wait_ge(*q("sq2", t + 1))
                    dve.reciprocal(stat[:, 12:13], stat[:, 24:25])
                    dve.drain()
                    dve.tensor_scalar(stat[:, 13:14], stat[:, 26:27], stat[:, 12:13], -1.0, ALU.mult, ALU.mult).then_inc(q["rs2"], 1)
                    dve.wait_ge(*q("n2", t + 1))
                    TTR(o2[:, 0, :], o2[:, 0, :], gb2[:, 0, :], ALU.mult)
                    dve.drain()
                    if not (isinstance(t, int) and t == 0):
                        dve.wait_ge(*s("xT", 2 * t))
                        dve.wait_ge(*q("out_st", 16 * t))
                    TTR(xb, o2[:, 0, :], gb2[:, 1, :], ALU.add).then_inc(q["g2"], 1)
                if l:
                    zeros()
                    dve.wait_ge(*L[0]("gb2_in", 32))
                    norm_x(0)
                if l == 0:
                    zeros()
                h_half(0)
                dve.wait_ge(*s("wp_in", 16 * 14))

                def step(t, n, last):
                    tab = tabs[:, ds(t, 1), :].rearrange("p o n -> p (o n)")
                    if l and not last:
                        norm_x(t + 1)
                    dve.wait_ge(*s("rms", t + 1))
                    dve.reciprocal(stat[:, 4:6], stat[:, 2:4]).then_inc(s["rstd"], 1)
                    dve.wait_ge(*s("latT", t + 1))
                    for k in range(3):
                        m = dve.tensor_scalar(latTt[:, 2 + k, :], PS[:, 3, k * P:(k + 1) * P], gcol[:, l, 2 + k:3 + k], None, ALU.mult)
                    m.then_inc(s["latc_d"], 1)
                    if not last:
                        h_half(t + 1)
                    dve.wait_ge(*s("p0", t + 1))
                    if not (isinstance(t, int) and t == 0):
                        dve.wait_ge(*s("tW", t))
                    dve.tensor_copy(va[:, ds(t, 1), :].rearrange("p o n -> p (o n)"), PS[:, 1, P:2 * P])
                    src = PS[:, 0:2, :].rearrange("p b n -> p (b n)")[:, 0:640].rearrange("p (h c) -> p h c", c=WD)
                    rope(rW, src, tab[:, 0:128], 10, 16, rC).then_inc(s["ropeW"], 1)
                    rope(krr.unsqueeze(1), PS[:, 2, QR:QR + ROPE].unsqueeze(1), tab[:, 128:192], 1, 8, krt.unsqueeze(1)).then_inc(s["used_d"], 1)
                    dve.drain()
                    if not (isinstance(t, int) and t == 0):
                        dve.wait_ge(*s("tK", 2 * t))
                    dve.tensor_copy(ksb[:, :, NOPE:], krr.unsqueeze(1).to_broadcast([P, MH, ROPE])).then_inc(s["kr"], 1)
                    if not (isinstance(t, int) and t == 0):
                        dve.wait_ge(*s("tQ", 2 * t))
                    for g in range(2):
                        dve.wait_ge(*s("uq", 2 * t + g + 1))
                        src = PS[:, 3 + g, 0:384].rearrange("p (h c) -> p h c", h=4)
                        dve.tensor_copy(qsb[:, g * 4:(g + 1) * 4, 0:NOPE], src[:, :, 0:NOPE])
                        m = rope(qsb[:, g * 4:(g + 1) * 4, NOPE:], src[:, :, NOPE:], tab[:, 128:192], 4, 8, tmpm)
                        dve.drain() if g == 0 else None
                    m.then_inc(s["qro"], 1)
                    dve.wait_ge(*s("tW", t + 1))
                    for g in range(2):
                        m = dve.tensor_copy(kaZ[g * 64:(g + 1) * 64, g, ds(t * P, P)], PS[g * 64:(g + 1) * 64, 1, 0:P])
                    m.then_inc(s["ka_cp"], 1)
                    if not (isinstance(t, int) and t == 0):
                        dve.wait_ge(*s("qM_st", 16 * t))
                    for g in range(2):
                        dve.wait_ge(*s("tQ", 2 * t + g + 1))
                        dve.tensor_copy(qMs[0:MQ, g * 4:(g + 1) * 4, :].rearrange("p a b -> p (a b)"), PS[0:MQ, 3 + g, :]).then_inc(s["qM_cp"], 1)
                tiles(dve, step)

                dve.wait_ge(*s("m_in", 32))

                def pair(p, t0, lp, lp_next, leading=False):
                    full = lp is not None
                    ch0 = chunks_before(l, p, lp)
                    start = isinstance(p, int) and p == 0

                    def stats(j, k):
                        u, h = HEADS[j]
                        wide = full or j == 16
                        if k == 0:
                            nk = TOK if wide else CTX
                            dve.wait_ge(*s("sM", p * 16 + j + 1))
                            dve.tensor_reduce(stat[:, 31:32], PS[:, 0:3, :].rearrange("p b n -> p (b n)")[:, 0:nk], AX.X, ALU.max, negate=True)
                            dve.drain()
                            dve.tensor_scalar(stat[:, 32 + u * 8 + h:33 + u * 8 + h], stat[:, 31:32], MSCALE, None, ALU.mult).then_inc(s["mxM"], 1)
                        else:
                            nk = 640 if wide else CTX
                            dve.wait_ge(*s("sW", p * 16 + j + 1))
                            if h == 0:
                                dve.wait_ge(*s(f"mk_in{u}", (p + j // 16) * 16 + 16))
                            if j or not start:
                                dve.wait_ge(*s("tr", ch0 + chunk_count(j, 0, full)))
                            dve.nop(nofuse=True)
                            dve.tensor_tensor_reduce(out=PW[:, 0:nk], in0=PS[:, 3:5, :].rearrange("p b n -> p (b n)")[:, 0:nk],
                                                     in1=mask[:, u, 0:nk], scale=WSCALE, scalar=-3.0e38,
                                                     op0=ALU.add, op1=ALU.max, accum_out=stat[:, 30:31])
                            dve.drain()
                            dve.tensor_scalar(stat[:, 48 + u * 8 + h:49 + u * 8 + h], stat[:, 30:31], -1.0, sinks[:, l, 1, h:h + 1],
                                              ALU.mult, ALU.min).then_inc(s["mxW"], 1)

                    def copy_chunk(j):
                        dve.wait_ge(*s("tr", ch0 + chunk_count(j, 0, full) + 2))
                        dve.tensor_copy(PTM[:, 4:8, :].rearrange("p a b -> p (a b)"), PS[:, 5, :]).then_inc(s["pt"], 1)

                    def finish(u):
                        dve.wait_ge(*s("pW", p * 16 + 8 * u + 8))
                        TTR(stat[:, 8:16], stat[:, 48 + u * 8:56 + u * 8], sinks[:, l, 0, :], ALU.add).then_inc(s["es"], 1)
                        dve.wait_ge(*s("tot", p * 2 + u + 1))
                        TTR(stat[:, 80 + u * 8:88 + u * 8], stat[:, 80 + u * 8:88 + u * 8], stat[:, 16:24], ALU.add)
                        dve.drain()
                        dve.reciprocal(stat[:, 80 + u * 8:88 + u * 8], stat[:, 80 + u * 8:88 + u * 8])
                        dve.reciprocal(stat[:, 64 + u * 8:72 + u * 8], stat[:, 64 + u * 8:72 + u * 8])
                        dve.drain()
                        dve.wait_ge(*s("pv", p * 32 + 16 * u + 16))
                        if u or not start:
                            dve.wait_ge(*s("fT", (p * 2 + u) * 2))
                        for kk, c in ((0, 64), (1, 80)):
                            r = stat[:, c + u * 8:c + 8 + u * 8].unsqueeze(2).to_broadcast([P, 8, 64])
                            TTR(osb[:, kk, :].rearrange("p (h d) -> p h d", h=8), PS[:, 6 + kk, :].rearrange("p (h d) -> p h d", h=8), r, ALU.mult).then_inc(s["osb"], 1)

                    if leading:
                        stats(0, 0)
                        stats(0, 1)
                        return
                    for j in range(16):
                        if full:
                            copy_chunk(j)
                        if j < 15 or lp_next is not None:
                            stats(j + 1, 0)
                            stats(j + 1, 1)
                        if j in (7, 15):
                            finish(j // 8)
                led_pairs(dve, l, lambda p, lp: pair(p, 0, lp, None, True), pair)

                def merge_block(f, u):
                    for ci, (c0, cn) in enumerate(CH[l]):
                        q = f * NCH[l] + ci
                        set_ = (u * NCH[l] + ci) % 2
                        dve.wait_ge(*s("sg", q + 1))
                        for j in range(2):
                            TTR(sg[:, set_, j, 0:cn], sg[:, set_, j, 0:cn], PS[:, set_ * 4 + j, 0:cn], ALU.mult)
                        dve.drain()
                        TTR(mrgT[:, ds(f, 1), c0:c0 + cn].rearrange("p o n -> p (o n)"), sg[:, set_, 0, 0:cn], sg[:, set_, 1, 0:cn], ALU.add).then_inc(s["mrg"], 1)
                for u in range(2):
                    merge_block(u, u)
                with dve.Fori(1, 4) as i:
                    for u in range(2):
                        merge_block(i * 2 + u, u)

                dve.wait_ge(*s("lnc_in", 16 * 5))

                def ln_d(t):
                    n = t - TL[l][0]
                    v = kind(t)
                    dve.wait_ge(*s("y", n + 1))
                    TTR(zt, PS[:, 0:2, :].rearrange("p b n -> p (b n)"), m2b[:, v, :], ALU.mult).then_inc(s["y_used"], 1)
                    if not (isinstance(n, int) and n == 0):
                        tr_d(t - 1)
                    dve.drain()
                    dve.wait_ge(*s("xr_in", (n + 1) * 16))
                    dve.scalar_tensor_tensor(out=zt, in0=xr, scalar=ALPHA, in1=zt, op0=ALU.mult, op1=ALU.add).then_inc(s["zs"], 1)
                    dve.drain()
                    for h in range(2):
                        dve.bn_stats(stat[:, 12 + 6 * h:18 + 6 * h], zt[:, h * 512:(h + 1) * 512])
                    dve.drain()
                    dve.bn_aggr(stat[:, 8:10], stat[:, 12:24]).then_inc(s["lnv"], 1)
                    dve.wait_ge(*s("lnr", n + 1))
                    dve.reciprocal(stat[:, 10:11], stat[:, 7:8])
                    dve.drain()
                    dve.tensor_scalar(stat[:, 11:12], stat[:, 8:9], stat[:, 10:11], -1.0, ALU.mult, ALU.mult).then_inc(s["lnb"], 1)
                    dve.wait_ge(*s("lnn", n + 1))
                    TTR(xn, xn, gb1[:, 0, :], ALU.mult)
                    dve.drain()
                    if not (isinstance(n, int) and n == 0):
                        dve.wait_ge(*s("x1T", 2 * n))
                        dve.wait_ge(*s("x1_st", 16 * n))
                        dve.wait_ge(*s("z_set", n))
                    TTR(x1t, xn, gb1[:, 1, :], ALU.add).then_inc(s["x1"], 1)

                def tr_d(t):
                    n = t - TL[l][0]
                    v = kind(t)
                    dve.wait_ge(*s("x1T", 2 * n + 2))
                    if not (isinstance(n, int) and n == 0):
                        dve.wait_ge(*s("rt", n))
                    for k in range(4):
                        m = dve.tensor_scalar(h2t[:, 4 + k, :], PS[:, 3, k * P:(k + 1) * P], modT[:, l, v, 4, 4 + k:5 + k],
                                              modT[:, l, v, 3, 4 + k:5 + k], ALU.mult, ALU.add)
                    m.then_inc(s["h2d"], 1)
                for t in range(TL[l][0], TC + 2):
                    ln_d(t)
                with dve.Fori(TC + 2, TT) as t:
                    ln_d(t)
                tr_d(TT - 1)

                tl = TL[l][0]
                nt = NT[l]
                dve.wait_ge(*s("rt_cp", nt))
                lg = logit[:, tl:TT, :]
                av = afft[:, tl:TT, :]
                dve.tensor_reduce(stat[:, 32:32 + nt], lg, AX.X, ALU.max)
                dve.drain()
                TTR(av, lg, stat[:, 32:32 + nt].unsqueeze(2).to_broadcast([P, nt, E]), ALU.subtract).then_inc(s["sm_m"], 1)
                dve.wait_ge(*s("sm_e", 1))
                dve.tensor_reduce(stat[:, 32:32 + nt], av, AX.X, ALU.add)
                dve.drain()
                dve.reciprocal(stat[:, 32:32 + nt], stat[:, 32:32 + nt])
                dve.drain()
                TTR(av, av, stat[:, 32:32 + nt].unsqueeze(2).to_broadcast([P, nt, E]), ALU.mult).then_inc(s["aff"], 1)
                dve.wait_ge(*s("affT", 1))
                dve.tensor_copy(affT[0:E, tl * P:TOK], PS[0:E, 5:8, :].rearrange("p b n -> p (b n)")[:, tl * P:TOK])
                dve.drain()
                for src0, vv, ii, ff, cap, base in (
                        [(CTX, vals, idx8, idxf, CAP_L, CTX)] + ([(0, valc, idc8, idcf, CAP_C, 0)] if l == 0 else [])):
                    n = SEQ if src0 else CTX
                    cur = affT[0:E, src0:src0 + n]
                    for r in range(cap // 8):
                        o8 = vv[0:E, r * 8:(r + 1) * 8]
                        dve.max(o8, cur)
                        dve.drain()
                        dve.max_index(ii[0:E, r * 8:(r + 1) * 8], o8, cur)
                        if r < cap // 8 - 1:
                            nx = affT[0:E, src0:src0 + n] if r % 2 else wk[0:E, 0:n]
                            dve.match_replace(nx, o8, cur, -1.0)
                            dve.drain()
                            cur = nx
                    dve.drain()
                    dve.tensor_scalar(ff[0:E, :], ii[0:E, :], float(base), None, ALU.add)
                    dve.drain()
                dve.drain().then_inc(s["topk"], 1)
                dve.wait_ge(*s("sel", 1))
                dve.tensor_copy(idxT[:, 0, :], PS[:, 2, 0:E])
                m = dve.tensor_copy(affS[:, 0, :], PS[:, 2, E:2 * E])
                if l == 0:
                    dve.tensor_copy(idxT[0:CAP_C, 1, :], PS[0:CAP_C, 2, 2 * E:3 * E])
                    m = dve.tensor_copy(affS[0:CAP_C, 1, :], PS[0:CAP_C, 2, 3 * E:4 * E])
                m.then_inc(s["sel_cp"], 1)
                dve.wait_ge(*s("m5_in", 32))
                dve.drain()

                N = NN[l]

                def stage(e, j, sem):
                    m = dve.tensor_copy(icur[:, j:j + 1], idxT[:, 0, ds(e, 1)])
                    if l == 0:
                        m = dve.tensor_copy(icur[0:CAP_C, j + 1:j + 2], idxT[0:CAP_C, 1, ds(e, 1)])
                    m.then_inc(s[sem], 1)

                def rows_d(e):
                    dve.wait_ge(*s("xgT", 2 * e + 2))
                    if not (isinstance(e, int) and e == 0):
                        dve.wait_ge(*s("au", e * 8))
                    for k in range(4, 8):
                        m = dve.tensor_scalar(xgT[:, k, 0:P], PS[:, 1, (k - 4) * P:(k - 3) * P], modT[:, l, 0, 4, k:k + 1],
                                              modT[:, l, 0, 3, k:k + 1], ALU.mult, ALU.add)
                    m.then_inc(s["xd"], 1)

                def rows_out(e):
                    if not (isinstance(e, int) and e == 0):
                        dve.wait_ge(*s("sc", e * 16 * (2 - l)))
                    stage(e, 2, "stage_s")
                    for r in range(2):
                        if l == 0:
                            dve.wait_ge(*s("bk", 2 * e + r + 1))
                        else:
                            dve.wait_ge(*s("yt", 8 * e + 4 * r + 4))
                        dve.scalar_tensor_tensor(out=Y[:, r * 512:(r + 1) * 512], in0=PS[:, ((7, 0), (5, 6))[l][r], :], scalar=affS[:, 0, ds(e, 1)],
                                                 in1=m5b[:, 0, r * 512:(r + 1) * 512], op0=ALU.mult, op1=ALU.mult).then_inc(s["ylat"], 1)
                        if l == 0:
                            dve.scalar_tensor_tensor(out=Yc[0:CAP_C, r * 512:(r + 1) * 512], in0=PS[0:CAP_C, 1 + r, :],
                                                     scalar=affS[0:CAP_C, 1, ds(e, 1)], in1=m5b[0:CAP_C, 1, r * 512:(r + 1) * 512],
                                                     op0=ALU.mult, op1=ALU.mult).then_inc(s["yctx"], 1)

                def expert(e, last):
                    first = isinstance(e, int) and e == 0
                    if not last:
                        dve.wait_ge(*s("gat", (e + 1) * 16 * (2 - l)))
                        stage(e + 1, 0, "stage_g")
                    for f in range(KD):
                        dve.wait_ge(*s("sil", e * 8 + f + 1))
                        TTR(actT[:, f, 0:N], silb[:, f % 2, 0:N], PS[:, 3 + f % 2, N:2 * N], ALU.mult).then_inc(s["act"], 1)
                        if f == 1 and l == 0 and not first:
                            rows_out(e - 1)
                    if not last:
                        rows_d(e + 1)
                    for d in range(1, KD if l == 0 else 0, 2):
                        dve.wait_ge(*s("yt", e * 8 + d + 1))
                        if d == 1 and not first:
                            dve.wait_ge(*s("bk", 2 * e))
                        dve.tensor_copy(yT[:, d, 0:N], PS[:, 6, 0:N]).then_inc(s["yc_d"], 1)
                    if l:
                        rows_out(e)
                stage(0, 0, "stage_g")
                if l + 1 < DEPTH:
                    ada_scales(l + 1)
                rows_d(0)
                with_first(dve, expert)
                if l == 0:
                    rows_out(E - 1)

                if l < DEPTH - 1:
                    continue
                dve.wait_ge(*s("gb2_in", 32))
                with dve.Fori(0, NPAIR[l]) as i:
                    for u in range(2):
                        n = i * 2 + u
                        dve.wait_ge(*s(f"z_in{u}", (i + 1) * 16))
                        for h in range(2):
                            dve.bn_stats(stat[:, 32 + 6 * h:38 + 6 * h], z2[:, u, h * 512:(h + 1) * 512])
                        dve.drain()
                        dve.bn_aggr(stat[:, 26 + 2 * u:28 + 2 * u], stat[:, 32:44]).then_inc(s["st2"], 1)
                        dve.wait_ge(*s("sq2", n + 1))
                        dve.reciprocal(stat[:, 12 + 2 * u:13 + 2 * u], stat[:, 24 + u:25 + u])
                        dve.drain()
                        dve.tensor_scalar(stat[:, 13 + 2 * u:14 + 2 * u], stat[:, 26 + 2 * u:27 + 2 * u], stat[:, 12 + 2 * u:13 + 2 * u], -1.0,
                                          ALU.mult, ALU.mult).then_inc(s["rs2"], 1)
                    for u in range(2):
                        n = i * 2 + u
                        dve.wait_ge(*s("n2", n + 1))
                        TTR(o2[:, u, :], o2[:, u, :], gb2[:, 0, :], ALU.mult)
                        dve.drain()
                        TTR(o2[:, u, :], o2[:, u, :], gb2[:, 1, :], ALU.add).then_inc(s["g2"], 1)

        @block.gpsimd
        def _(pool):
            def ada_stores(l, i0, i1):
                with pool.Fori(i0, i1) as i:
                    for u in range(2):
                        pool.wait_ge(G["rowc"], l * 12 + i * 2 + u + 1)
                        dst = mod_d[l].rearrange("(v k) p -> v (k p)", v=2)[:, ds((i * 2 + u) * 512, 512)]
                        pool.dma_start(dst, adar[0:2, u, :]).then_inc(G[f"mod_st{u}"], 16)
            ada_stores(0, 0, 6)
            for l in range(DEPTH):
                s = L[l]
                pool.wait_ge(*s("mrg", 8 * NCH[l]))
                tl = TL[l][0]

                def take(t):
                    n = t - tl
                    for c in range(2):
                        if not (isinstance(n, int) and n == 0):
                            pool.wait_ge(*s("y" if c else "y_mid", n))
                        pool.tensor_copy(mst[:, c * 4:c * 4 + 4, :], mrgT[:, c * 4:c * 4 + 4, ds(t * P, P)]).then_inc(s["mst"], 1)
                take(tl)
                with pool.Fori(tl + 1, TT) as t:
                    take(t)
                if l + 1 < DEPTH:
                    ada_stores(l + 1, 0, 4)

                pool.wait_ge(*s("x1_st", 16 * NT[l]))
                pool.wait_ge(*s("z_st", 16 * NT[l]))
                pool.wait_ge(*s("y", NT[l]))

                def gather(e):
                    pool.wait_ge(*s("stage_g", e + 1))
                    if not (isinstance(e, int) and e == 0):
                        pool.wait_ge(*s("xgT", 2 * e))
                    pool.nop(nofuse=True)
                    pool.indirect_dma_start(out=xg, out_offset=None, in_=x1_d,
                                            in_offset=bass.IndirectOffsetOnAxis(ap=icur[:, 0:1], axis=0)).then_inc(s["gat"], 16)
                    if l == 0:
                        pool.nop(nofuse=True)
                        pool.indirect_dma_start(out=xgc[0:CAP_C, :], out_offset=None, in_=x1_d,
                                                in_offset=bass.IndirectOffsetOnAxis(ap=icur[0:CAP_C, 1:2], axis=0)).then_inc(s["gat"], 16)

                def scatter(e):
                    pool.wait_ge(*s("stage_s", e + 1))
                    pool.wait_ge(*s("ylat", 2 * e + 2))
                    if not (isinstance(e, int) and e == 0):
                        pool.wait_ge(*s("sc", e * 16 * (2 - l)))
                    pool.nop(nofuse=True)
                    pool.indirect_dma_start(out=z_d, out_offset=bass.IndirectOffsetOnAxis(ap=icur[:, 2:3], axis=0), in_=Y,
                                            in_offset=None, compute_op=ALU.add).then_inc(s["sc"], 16)
                    if l == 0:
                        pool.wait_ge(*s("yctx", 2 * e + 2))
                        pool.nop(nofuse=True)
                        pool.indirect_dma_start(out=z_d, out_offset=bass.IndirectOffsetOnAxis(ap=icur[0:CAP_C, 3:4], axis=0),
                                                in_=Yc[0:CAP_C, :], in_offset=None, compute_op=ALU.add).then_inc(s["sc"], 16)

                def expert(e, last):
                    if not last:
                        gather(e + 1)
                    if not (isinstance(e, int) and e == 0):
                        scatter(e - 1)
                gather(0)
                if l + 1 < DEPTH:
                    ada_stores(l + 1, 4, 6)
                pool.dma_start(gb2[:, 0, :], a["ln2_g"][l:l + 1, :].to_broadcast([P, D])).then_inc(s["gb2_in"], 16)
                pool.dma_start(gb2[:, 1, :], a["ln2_b"][l:l + 1, :].to_broadcast([P, D])).then_inc(s["gb2_in"], 16)
                with_first(pool, expert)
                scatter(E - 1)

                pool.wait_ge(*s("sc", 16 * E * (2 - l)))
                if l == 0:
                    pool.dma_start(z2[:, 0, :], z_d[0:P, :]).then_inc(s["z_in0"], 16)
                    with pool.Fori(1, TT) as t:
                        pool.wait_ge(*s("n2", t))
                        pool.dma_start(z2[:, 0, :], z_d[ds(t * P, P), :]).then_inc(s["z_in0"], 16)
                else:
                    for u in range(2):
                        pool.dma_start(z2[:, u, :], z_d[(tl + u) * P:(tl + u + 1) * P, :]).then_inc(s[f"z_in{u}"], 16)
                    with pool.Fori(0, NPAIR[l] - 1) as i:
                        for u in range(2):
                            pool.wait_ge(*s("n2", i * 2 + u + 1))
                            pool.dma_start(z2[:, u, :], z_d[ds((i * 2 + u + 2 + tl) * P, P), :]).then_inc(s[f"z_in{u}"], 16)


_INS = ["x", "c", "ctx", "c_ctx", "w_ada", "b_ada", "w_in", "attn_sink", "mla_q_norm", "mla_kv_norm", "w_uq", "w_ukv",
        "w_oa", "w_ob", "w_out", "ln1_g", "ln1_b", "w_router", "w_exp_gate", "w_exp_up", "w_exp_down", "ln2_g", "ln2_b"]


def _tables():
    n = np.arange(SEQ)
    pos = np.stack([n // GRID_W, n % GRID_W], 1).astype(np.float32)
    cols = []
    for dim in (WD, ROPE):
        nf = dim // 4
        inv = np.power(np.float32(THETA), -np.arange(nf, dtype=np.float32) / np.float32(nf)).astype(np.float32)
        ang = pos[:, :, None] * inv
        c, s = np.cos(ang), np.sin(ang)
        cols.append(np.stack([c, c], 2).reshape(SEQ, dim))
        cols.append(np.stack([-s, s], 2).reshape(SEQ, dim))
    lat = np.concatenate(cols, 1)
    still = np.concatenate([np.ones((CTX, WD)), np.zeros((CTX, WD)), np.ones((CTX, ROPE)), np.zeros((CTX, ROPE))], 1)
    rope = np.concatenate([still, lat], 0).astype(np.float32)
    i, j = np.arange(P)[:, None], np.arange(P)[None, :]
    off = NEG / WSCALE
    prev = np.where(j >= i, 0.0, off)
    nxt = np.where(j <= i, 0.0, off)
    z = np.zeros((P, P))
    mask = np.concatenate([z, z, prev, z, nxt], 1).astype(np.float32)
    full = np.full((P, P), off)
    edge = np.stack([np.stack([full, prev, prev, prev]), np.stack([nxt, nxt, nxt, full])]).astype(np.float32)
    return {"ident": np.eye(P, dtype=np.float32), "rope": rope, "wmask": mask, "edge": edge}


def kernel(**inputs):
    import numpy as _np
    import concourse.bacc as _bacc
    from concourse import mybir as _mybir
    from concourse.bass_utils import run_bass_kernel_spmd as _run

    nc = _bacc.Bacc("TRN2", target_bir_lowering=False, num_devices=1)
    arrays, args = {}, {}
    everything = {n: _np.ascontiguousarray(inputs[n]) for n in _INS}
    everything.update(_tables())
    for name, v in everything.items():
        arrays[f"in_{name}"] = v
        args[name] = nc.dram_tensor(f"in_{name}", v.shape, _mybir.dt.from_np(v.dtype), kind="ExternalInput").ap()
    out = nc.dram_tensor("out_0", (1, SEQ, D), F32, kind="ExternalOutput").ap()
    build(nc, args, out)
    r = _run(nc, [arrays], core_ids=[0])
    return r.results[0]["out_0"]
```
